# Optimizing a Trainium2 kernel written in Bass

```python
import jax, jax.numpy as jnp
from jax import lax
import numpy as np

D_MODEL = 1024
BATCH = 1
SEQ = 512
DEPTH = 1

HEAD_DIM = 64
A_HEADS = 8
A_KV_HEADS = 2
IDX_HEADS = 8
IDX_DIM = 64
TOPK_MAX = 256
B_HEADS = 8
B_KV_HEADS = 2
WINDOW = 128
Q_BLOCK = 128
D_FF = 4 * D_MODEL
ROPE_THETA = 10000.0
RMS_EPS = 1e-6
LN_EPS = 1e-6

A_Q = A_HEADS * HEAD_DIM
A_KV = A_KV_HEADS * HEAD_DIM
IDX_Q = IDX_HEADS * IDX_DIM
B_Q = B_HEADS * HEAD_DIM
B_KV = B_KV_HEADS * HEAD_DIM
SPLIT_SIZES = (A_Q, A_KV, A_KV, IDX_Q, IDX_DIM, IDX_HEADS, B_Q, B_KV, B_KV, D_MODEL, D_MODEL)
D_IN = sum(SPLIT_SIZES)


def rmsnorm(x, g):
    xf = x.astype(jnp.float32)
    y = xf * lax.rsqrt(jnp.mean(xf * xf, axis=-1, keepdims=True) + RMS_EPS)
    return (y * g.astype(jnp.float32)).astype(x.dtype)

def layernorm(x, w, b):
    xf = x.astype(jnp.float32)
    mu = jnp.mean(xf, axis=-1, keepdims=True)
    var = jnp.mean(jnp.square(xf - mu), axis=-1, keepdims=True)
    y = (xf - mu) * lax.rsqrt(var + LN_EPS)
    return (y * w.astype(jnp.float32) + b.astype(jnp.float32)).astype(x.dtype)

def rope_tables(L, dim):
    inv = 1.0 / (ROPE_THETA ** (jnp.arange(0, dim, 2, dtype=jnp.float32) / dim))
    ang = jnp.arange(L, dtype=jnp.float32)[:, None] * inv[None, :]
    return jnp.cos(ang), jnp.sin(ang)

def apply_rope(x, cos, sin):
    xf = x.astype(jnp.float32)
    x1, x2 = jnp.split(xf, 2, axis=-1)
    c = cos[None, :, None, :]
    s = sin[None, :, None, :]
    return jnp.concatenate([x1 * c - x2 * s, x2 * c + x1 * s], axis=-1).astype(x.dtype)

def dsa_branch(q, k, v, q_idx, k_idx, w_idx, topk):
    Bn, L, H, dh = q.shape
    G = k.shape[2]
    R = H // G
    nb = L // Q_BLOCK
    kpos = jnp.arange(L)
    k_idx32 = k_idx.astype(jnp.float32)
    scale = HEAD_DIM ** -0.5

    def one_block(i):
        start = i * Q_BLOCK
        qb = lax.dynamic_slice_in_dim(q, start, Q_BLOCK, axis=1)
        qib = lax.dynamic_slice_in_dim(q_idx, start, Q_BLOCK, axis=1)
        wb = lax.dynamic_slice_in_dim(w_idx, start, Q_BLOCK, axis=1)
        qpos = start + jnp.arange(Q_BLOCK)
        s = jnp.einsum('bqhd,bkd->bqhk', qib.astype(jnp.float32), k_idx32)
        score = jnp.einsum('bqhk,bqh->bqk', jax.nn.relu(s), wb.astype(jnp.float32))
        causal = kpos[None, :] <= qpos[:, None]
        score = jnp.where(causal[None], score, -jnp.inf)
        _, sel = lax.top_k(score, topk)
        ks = jax.vmap(lambda kk, ii: kk[ii])(k, sel)
        vs = jax.vmap(lambda vv, ii: vv[ii])(v, sel)
        valid = sel <= qpos[None, :, None]
        qg = qb.reshape(Bn, Q_BLOCK, G, R, dh).astype(jnp.float32)
        logits = jnp.einsum('bqgrd,bqkgd->bqgrk', qg, ks.astype(jnp.float32)) * scale
        logits = jnp.where(valid[:, :, None, None, :], logits, -jnp.inf)
        p = jax.nn.softmax(logits, axis=-1)
        o = jnp.einsum('bqgrk,bqkgd->bqgrd', p, vs.astype(jnp.float32))
        return o.reshape(Bn, Q_BLOCK, H * dh).astype(q.dtype)

    out = lax.map(one_block, jnp.arange(nb))
    return jnp.transpose(out, (1, 0, 2, 3)).reshape(Bn, L, H * dh)

def swa_branch(q, k, v, sinks):
    Bn, L, H, dh = q.shape
    G = k.shape[2]
    R = H // G
    W = WINDOW
    nb = L // W
    qb = q.reshape(Bn, nb, W, G, R, dh).astype(jnp.float32)
    pad = ((0, 0), (W, 0), (0, 0), (0, 0))
    kp = jnp.pad(k, pad).reshape(Bn, nb + 1, W, G, dh)
    vp = jnp.pad(v, pad).reshape(Bn, nb + 1, W, G, dh)
    kb = jnp.concatenate([kp[:, :-1], kp[:, 1:]], axis=2).astype(jnp.float32)
    vb = jnp.concatenate([vp[:, :-1], vp[:, 1:]], axis=2).astype(jnp.float32)
    logits = jnp.einsum('bnqgrd,bnkgd->bngrqk', qb, kb) * (HEAD_DIM ** -0.5)
    rel = jnp.arange(W)[:, None] + W - jnp.arange(2 * W)[None, :]
    kabs = jnp.arange(nb)[:, None] * W - W + jnp.arange(2 * W)[None, :]
    mask = ((rel >= 0) & (rel < W))[None, :, :] & (kabs >= 0)[:, None, :]
    logits = jnp.where(mask[None, :, None, None, :, :], logits, -jnp.inf)
    sink = jnp.broadcast_to(sinks.astype(jnp.float32).reshape(1, 1, G, R, 1, 1), logits.shape[:-1] + (1,))
    p = jax.nn.softmax(jnp.concatenate([logits, sink], axis=-1), axis=-1)[..., :-1]
    o = jnp.einsum('bngrqk,bnkgd->bnqgrd', p, vb)
    return o.reshape(Bn, L, H * dh).astype(q.dtype)

def first_inputs(seed: int = 0) -> dict:
    key = jax.random.key(seed)
    ks = jax.random.split(key, 14)
    f32 = jnp.float32
    nrm = lambda k, shape: jax.random.normal(k, shape, dtype=f32)
    return {
        "x": nrm(ks[0], (BATCH, SEQ, D_MODEL)),
        "attn_norm_w": 1.0 + 0.02 * nrm(ks[1], (DEPTH, D_MODEL)),
        "w_in": nrm(ks[2], (DEPTH, D_MODEL, D_IN)) * D_MODEL ** -0.5,
        "idx_k_norm_w": 1.0 + 0.02 * nrm(ks[3], (DEPTH, IDX_DIM)),
        "idx_k_norm_b": 0.02 * nrm(ks[4], (DEPTH, IDX_DIM)),
        "sinks": 0.5 * nrm(ks[5], (DEPTH, B_HEADS)),
        "w_branch_a": nrm(ks[6], (DEPTH, A_Q, D_MODEL)) * A_Q ** -0.5,
        "w_branch_b": nrm(ks[7], (DEPTH, B_Q, D_MODEL)) * B_Q ** -0.5,
        "w_out": nrm(ks[8], (DEPTH, D_MODEL, D_MODEL)) * D_MODEL ** -0.5,
        "mlp_norm_w": 1.0 + 0.02 * nrm(ks[9], (DEPTH, D_MODEL)),
        "w_up": nrm(ks[10], (DEPTH, D_MODEL, D_FF)) * D_MODEL ** -0.5,
        "w_down": nrm(ks[11], (DEPTH, D_FF, D_MODEL)) * D_FF ** -0.5,
        "final_norm_w": 1.0 + 0.02 * nrm(ks[12], (D_MODEL,)),
    }

def first_block(x, attn_norm_w, w_in, idx_k_norm_w, idx_k_norm_b, sinks, w_branch_a, w_branch_b,
              w_out, mlp_norm_w, w_up, w_down, final_norm_w):
    Bn, L, _ = x.shape
    topk = min(TOPK_MAX, L // 4)
    cos, sin = rope_tables(L, HEAD_DIM)
    cos_i, sin_i = rope_tables(L, IDX_DIM)
    offsets = [sum(SPLIT_SIZES[:i + 1]) for i in range(len(SPLIT_SIZES) - 1)]
    w_scale = (IDX_HEADS ** -0.5) * (IDX_DIM ** -0.5)

    for l in range(DEPTH):
        h = rmsnorm(x, attn_norm_w[l])
        proj = jnp.einsum('bld,de->ble', h, w_in[l])
        a_q, a_k, a_v, i_q, i_k, i_w, b_q, b_k, b_v, g_a, g_b = jnp.split(proj, offsets, axis=-1)

        a_q = apply_rope(a_q.reshape(Bn, L, A_HEADS, HEAD_DIM), cos, sin)
        a_k = apply_rope(a_k.reshape(Bn, L, A_KV_HEADS, HEAD_DIM), cos, sin)
        a_v = a_v.reshape(Bn, L, A_KV_HEADS, HEAD_DIM)
        i_q = apply_rope(i_q.reshape(Bn, L, IDX_HEADS, IDX_DIM), cos_i, sin_i)
        i_k = layernorm(i_k, idx_k_norm_w[l], idx_k_norm_b[l])
        i_k = apply_rope(i_k[:, :, None, :], cos_i, sin_i)[:, :, 0, :]
        i_w = i_w * w_scale
        o_a = dsa_branch(a_q, a_k, a_v, i_q, i_k, i_w, topk)

        b_q = apply_rope(b_q.reshape(Bn, L, B_HEADS, HEAD_DIM), cos, sin)
        b_k = apply_rope(b_k.reshape(Bn, L, B_KV_HEADS, HEAD_DIM), cos, sin)
        b_v = b_v.reshape(Bn, L, B_KV_HEADS, HEAD_DIM)
        o_b = swa_branch(b_q, b_k, b_v, sinks[l])

        y_a = jnp.einsum('ble,ed->bld', o_a, w_branch_a[l])
        y_b = jnp.einsum('ble,ed->bld', o_b, w_branch_b[l])
        mix = jax.nn.sigmoid(g_a) * y_a + jax.nn.sigmoid(g_b) * y_b
        x = x + jnp.einsum('bld,de->ble', mix, w_out[l])

        h2 = rmsnorm(x, mlp_norm_w[l])
        u = jax.nn.relu(jnp.einsum('bld,df->blf', h2, w_up[l]))
        x = x + jnp.einsum('blf,fd->bld', u * u, w_down[l])

    return rmsnorm(x, final_norm_w)


GLA_HEADS = 4
GLA_DK = 64
GLA_DV = 128
GLA_KEY_W = GLA_HEADS * GLA_DK
GLA_VAL_W = GLA_HEADS * GLA_DV
GLA_GATE_RANK = 16
GLA_GATE_NORMALIZER = 16.0
GLA_CHUNK = 64
POOL_GROUPS = 4
POOL_WINDOWS = (2, 4, 8, 16)
POOL_W = D_MODEL // 2
POOL_GW = POOL_W // POOL_GROUPS
IN_WIDTHS = (GLA_KEY_W, GLA_KEY_W, GLA_VAL_W, GLA_VAL_W, GLA_GATE_RANK, POOL_W, D_MODEL, D_MODEL)
D_IN_2 = sum(IN_WIDTHS)
N_GROUPS = 4
EXPERTS_PER_GROUP = 8
N_EXPERTS = N_GROUPS * EXPERTS_PER_GROUP
TOP_K_IN_GROUP = 2
D_EXPERT = 256
MOE_BLOCK = 128
NORM_EPS = 1e-6


def rmsnorm_2(x, g):
    xf = x.astype(jnp.float32)
    y = xf * lax.rsqrt(jnp.mean(xf * xf, axis=-1, keepdims=True) + NORM_EPS)
    return (y * g.astype(jnp.float32)).astype(x.dtype)

def gla_mix(q, k, v, log_a):
    B, S, _ = q.shape
    C = GLA_CHUNK
    N = S // C

    def split(t, d):
        return t.astype(jnp.float32).reshape(B, N, C, GLA_HEADS, d).transpose(0, 3, 1, 2, 4)

    qc, kc, gc = split(q, GLA_DK), split(k, GLA_DK), split(log_a, GLA_DK)
    vc = split(v, GLA_DV)
    b = jnp.cumsum(gc, axis=3)
    b_last = b[:, :, :, -1:, :]
    q_dec = qc * jnp.exp(b) * (GLA_DK ** -0.5)
    k_dec = kc * jnp.exp(-b)
    causal = jnp.tril(jnp.ones((C, C), dtype=bool))
    scores = jnp.where(causal, jnp.einsum('bhntd,bhnsd->bhnts', q_dec, k_dec), 0.0)
    o_intra = jnp.einsum('bhnts,bhnsv->bhntv', scores, vc)
    k_end = kc * jnp.exp(b_last - b)
    inc = jnp.einsum('bhnsd,bhnsv->bhndv', k_end, vc)
    decay = jnp.exp(b_last[:, :, :, 0, :])

    def step(state, inp):
        dec, u = inp
        return dec[..., None] * state + u, state

    state0 = jnp.zeros((B, GLA_HEADS, GLA_DK, GLA_DV), jnp.float32)
    _, s_prev = lax.scan(step, state0, (jnp.moveaxis(decay, 2, 0), jnp.moveaxis(inc, 2, 0)))
    s_prev = jnp.moveaxis(s_prev, 0, 2)
    o = o_intra + jnp.einsum('bhntd,bhndv->bhntv', q_dec, s_prev)
    return o.transpose(0, 2, 3, 1, 4).reshape(B, S, GLA_VAL_W)

def head_rmsnorm(o, g):
    B, S, _ = o.shape
    oh = o.reshape(B, S, GLA_HEADS, GLA_DV)
    oh = oh * lax.rsqrt(jnp.mean(oh * oh, axis=-1, keepdims=True) + NORM_EPS)
    return oh.reshape(B, S, GLA_VAL_W) * g.astype(jnp.float32)

def pool_mix(u, pool_w, pool_scale):
    B, S, _ = u.shape
    uf = u.astype(jnp.float32)
    ug = uf.reshape(B, S, POOL_GROUPS, POOL_GW)
    cs = jnp.cumsum(uf, axis=1).reshape(B, S, POOL_GROUPS, POOL_GW)
    pos = jnp.arange(S, dtype=jnp.float32)
    pooled = []
    for gi, w in enumerate(POOL_WINDOWS):
        c = cs[:, :, gi]
        shifted = jnp.pad(c[:, :S - w], ((0, 0), (w, 0), (0, 0)))
        cnt = jnp.minimum(pos + 1.0, float(w))[None, :, None]
        pooled.append((c - shifted) / cnt)
    pooled = jnp.stack(pooled, axis=2)
    mixed = jnp.einsum('bsgc,gcd->bsgd', pooled - ug, pool_w.astype(jnp.float32))
    return (mixed.reshape(B, S, POOL_W) * pool_scale.astype(jnp.float32)).astype(u.dtype)

def hier_moe(h, w_rg, b_rg, w_re, b_re, w_gate, w_up, w_down):
    B, S, D = h.shape
    T = B * S
    ht = h.reshape(T, D)
    g_logits = (ht @ w_rg).astype(jnp.float32) + b_rg.astype(jnp.float32)
    g_p, g_idx = lax.top_k(jax.nn.softmax(g_logits, axis=-1), 1)
    e_all = jnp.einsum('td,gde->tge', ht, w_re).astype(jnp.float32) + b_re.astype(jnp.float32)
    e_logits = e_all[jnp.arange(T), g_idx[:, 0]]
    e_top, e_idx = lax.top_k(e_logits, TOP_K_IN_GROUP)
    gate = g_p * jax.nn.softmax(e_top, axis=-1)
    A = T * TOP_K_IN_GROUP
    weights = gate.reshape(A)
    expert_ids = (g_idx * EXPERTS_PER_GROUP + e_idx).reshape(A).astype(jnp.int32)
    token_ids = jnp.repeat(jnp.arange(T, dtype=jnp.int32), TOP_K_IN_GROUP)

    n_blocks = -(-(A + N_EXPERTS * (MOE_BLOCK - 1)) // MOE_BLOCK)
    R = n_blocks * MOE_BLOCK
    order = jnp.argsort(expert_ids)
    sorted_e = expert_ids[order]
    counts = jnp.zeros((N_EXPERTS,), jnp.int32).at[expert_ids].add(1)
    padded = ((counts + MOE_BLOCK - 1) // MOE_BLOCK) * MOE_BLOCK
    starts = jnp.cumsum(counts) - counts
    pends = jnp.cumsum(padded)
    pstarts = pends - padded
    dest = pstarts[sorted_e] + (jnp.arange(A, dtype=jnp.int32) - starts[sorted_e])
    row_token = jnp.full((R,), T, jnp.int32).at[dest].set(token_ids[order])
    row_w = jnp.zeros((R,), jnp.float32).at[dest].set(weights[order])
    block_e = jnp.minimum(jnp.searchsorted(pends, jnp.arange(n_blocks, dtype=jnp.int32) * MOE_BLOCK,
                                           side='right'), N_EXPERTS - 1).astype(jnp.int32)
    h_pad = jnp.concatenate([ht, jnp.zeros((1, D), ht.dtype)], axis=0)
    x_blocks = h_pad[row_token].reshape(n_blocks, MOE_BLOCK, D)

    def expert_block(args):
        xb, e = args
        return (jax.nn.silu(xb @ w_gate[e]) * (xb @ w_up[e])) @ w_down[e]

    y_rows = lax.map(expert_block, (x_blocks, block_e)).reshape(R, D)
    y_rows = y_rows * row_w[:, None].astype(y_rows.dtype)
    out = jnp.zeros((T + 1, D), y_rows.dtype).at[row_token].add(y_rows)[:T]
    return out.reshape(B, S, D).astype(h.dtype)

def second_inputs(seed: int = 0) -> dict:
    key = jax.random.key(seed)
    ks = jax.random.split(key, 24)
    L, D = DEPTH, D_MODEL
    nrm = lambda k, shape, s: jax.random.normal(k, shape, jnp.float32) * s
    return {
        "x": nrm(ks[0], (BATCH, SEQ, D), 1.0),
        "norm1_g": 1.0 + nrm(ks[1], (L, D), 0.05),
        "w_in": nrm(ks[2], (L, D, D_IN_2), D ** -0.5),
        "w_alpha_up": nrm(ks[3], (L, GLA_GATE_RANK, GLA_KEY_W), GLA_GATE_RANK ** -0.5),
        "b_alpha": nrm(ks[4], (L, GLA_KEY_W), 0.1),
        "gla_norm_g": 1.0 + nrm(ks[5], (L, GLA_VAL_W), 0.05),
        "w_gla_branch": nrm(ks[6], (L, GLA_VAL_W, D), GLA_VAL_W ** -0.5),
        "pool_w": nrm(ks[7], (L, POOL_GROUPS, POOL_GW, POOL_GW), POOL_GW ** -0.5),
        "pool_scale": 1.0 + nrm(ks[8], (L, POOL_W), 0.05),
        "w_pool_branch": nrm(ks[9], (L, POOL_W, D), POOL_W ** -0.5),
        "w_out": nrm(ks[10], (L, D, D), D ** -0.5),
        "norm2_g": 1.0 + nrm(ks[11], (L, D), 0.05),
        "w_router_group": nrm(ks[12], (L, D, N_GROUPS), D ** -0.5),
        "b_router_group": nrm(ks[13], (L, N_GROUPS), 0.01),
        "w_router_expert": nrm(ks[14], (L, N_GROUPS, D, EXPERTS_PER_GROUP), D ** -0.5),
        "b_router_expert": nrm(ks[15], (L, N_GROUPS, EXPERTS_PER_GROUP), 0.01),
        "w_exp_gate": nrm(ks[16], (L, N_EXPERTS, D, D_EXPERT), D ** -0.5),
        "w_exp_up": nrm(ks[17], (L, N_EXPERTS, D, D_EXPERT), D ** -0.5),
        "w_exp_down": nrm(ks[18], (L, N_EXPERTS, D_EXPERT, D), D_EXPERT ** -0.5),
        "norm_f_g": 1.0 + nrm(ks[19], (D,), 0.05),
    }

def second_block(x, norm1_g, w_in, w_alpha_up, b_alpha, gla_norm_g, w_gla_branch, pool_w, pool_scale,
              w_pool_branch, w_out, norm2_g, w_router_group, b_router_group, w_router_expert,
              b_router_expert, w_exp_gate, w_exp_up, w_exp_down, norm_f_g):
    split_idx = [int(i) for i in np.cumsum(IN_WIDTHS)[:-1]]
    for l in range(DEPTH):
        h = rmsnorm_2(x, norm1_g[l])
        proj = h @ w_in[l]
        q, k, v, r, a_low, u_pool, gate_gla, gate_pool = jnp.split(proj, split_idx, axis=-1)
        log_a = jax.nn.log_sigmoid((a_low @ w_alpha_up[l] + b_alpha[l]).astype(jnp.float32)) / GLA_GATE_NORMALIZER
        o = gla_mix(q, k, v, log_a)
        o = (head_rmsnorm(o, gla_norm_g[l]) * jax.nn.silu(r.astype(jnp.float32))).astype(x.dtype)
        y_gla = o @ w_gla_branch[l]
        y_pool = pool_mix(u_pool, pool_w[l], pool_scale[l]) @ w_pool_branch[l]
        merged = jax.nn.sigmoid(gate_gla) * y_gla + jax.nn.sigmoid(gate_pool) * y_pool
        x = x + merged @ w_out[l]
        h2 = rmsnorm_2(x, norm2_g[l])
        x = x + hier_moe(h2, w_router_group[l], b_router_group[l], w_router_expert[l], b_router_expert[l],
                         w_exp_gate[l], w_exp_up[l], w_exp_down[l])
    return rmsnorm_2(x, norm_f_g)


def setup_inputs(seed=0):
    out = dict(first_inputs(seed))
    for name, value in second_inputs(seed + 1).items():
        if name != "x":
            out[name + "_2"] = value
    return out


def reference(
    x, attn_norm_w, w_in, idx_k_norm_w, idx_k_norm_b, sinks, w_branch_a, w_branch_b, w_out,
    mlp_norm_w, w_up, w_down, final_norm_w, norm1_g_2, w_in_2, w_alpha_up_2, b_alpha_2,
    gla_norm_g_2, w_gla_branch_2, pool_w_2, pool_scale_2, w_pool_branch_2, w_out_2, norm2_g_2,
    w_router_group_2, b_router_group_2, w_router_expert_2, b_router_expert_2, w_exp_gate_2,
    w_exp_up_2, w_exp_down_2, norm_f_g_2,
):
    x = first_block(
        x, attn_norm_w, w_in, idx_k_norm_w, idx_k_norm_b, sinks, w_branch_a, w_branch_b, w_out,
        mlp_norm_w, w_up, w_down, final_norm_w,
    )
    return second_block(
        x, norm1_g_2, w_in_2, w_alpha_up_2, b_alpha_2, gla_norm_g_2, w_gla_branch_2, pool_w_2,
        pool_scale_2, w_pool_branch_2, w_out_2, norm2_g_2, w_router_group_2, b_router_group_2,
        w_router_expert_2, b_router_expert_2, w_exp_gate_2, w_exp_up_2, w_exp_down_2,
        norm_f_g_2,
    )


_drawn_inputs = setup_inputs


def setup_inputs(seed=0):
    import zlib

    import numpy as np

    out = dict(_drawn_inputs(seed))
    spreads = {}
    factors = {'idx_k_norm_b': 3.016,
     'sinks': 6.735,
     'b_router_group_2': 2.918,
     'b_router_expert_2': 4.677}
    for name, (base, spread) in spreads.items():
        noise = np.random.default_rng([zlib.crc32(name.encode()), seed]).standard_normal(out[name].shape)
        drawn = base * np.exp(spread * noise) if base else spread * noise
        out[name] = __import__('jax').numpy.asarray(drawn.astype(out[name].dtype))
    for name, factor in factors.items():
        out[name] = (out[name] * factor).astype(out[name].dtype)
    return out
```

```python
from contextlib import ExitStack

import concourse.bass as bass
from concourse import mybir

F32 = mybir.dt.float32
F32R = mybir.dt.float32r
I32 = mybir.dt.int32
ALU = mybir.AluOpType
ACT = mybir.ActivationFunctionType
AX = mybir.AxisListType.X

P = 128
L = 512
D = 1024
NT, NK = L // P, D // P
HD, HEADS, REP = 64, 8, 4
TOPK = 128
FF = 4 * D
QUARTERS = FF // D
DV, GH, CHUNK = 128, 4, 64
NCH = L // CHUNK
WINDOWS = (2, 4, 8, 16)
NG, EPG, NE, DE = 4, 8, 32, 256
OVER = 8
NB = NE + OVER
SKIP = 1 << 20
EPS = 1e-6
NEG = -1e30
MASKED, TAKEN = -3.0e38, -3.3e38
ATT_SCALE = HD ** -0.5
W_SCALE = HEADS ** -0.5 * HD ** -0.5

CONST_COLS = {}
_at = 0
for _name, _n in (("ident", P), ("before", P), ("causal", P), ("earlier", P), ("pair_causal", P),
                  ("cos", L), ("sin", L), ("cos_tok", NT * 32), ("sin_tok", NT * 32),
                  ("inv_count", 4 * 16), ("iota_e", NE), ("down4", NG), ("down8", EPG), ("token", NT)):
    CONST_COLS[_name] = (_at, _at + _n)
    _at += _n
CONST_WIDTH = _at

RING = 4
AHEAD = 3
C_IN, C_BR, C_OUT, C_MLP = 0, 33, 41, 49
C_IN2 = C_MLP + QUARTERS * 2 * NK
C_BR2, C_OUT2 = C_IN2 + 33, C_IN2 + 41
N_CHUNKS = C_OUT2 + NK
IN1_GROUPS = ((1, 4, 768), (5, 4, 0), (9, 2, 512), (11, 2, 1864), (13, 4, 1352), (17, 16, 2120))
IN2_GROUPS = ((1, 4, 0), (5, 4, 512), (9, 4, 1024), (13, 4, 1552), (17, 16, 2064))


def unit(u):
    g = u // HEADS
    b, qt = ("b", g) if g < NT else ("a", g - NT)
    k0 = max(0, qt - 1) if b == "b" else 0
    return b, qt, k0, qt + 1 - k0, u % HEADS


UNITS = 2 * NT * HEADS
STEPS = UNITS + 8


def pe_attention():
    for s in range(STEPS):
        if s < UNITS:
            yield "logits", s
        if 2 <= s < UNITS + 2:
            yield "probs_t", s - 2
        if 3 <= s < UNITS + 3:
            yield "values", s - 3
        if s >= 14 and s % 8 == 6:
            yield "out_t", s // 8 - 1


class Jobs:

    def __init__(self):
        self.at, self.freer, self.freed, self.count = {}, [], [], {"dve": 0, "act": 0}

    def add(self, name, freer):
        self.at[name] = len(self.freer)
        self.count[freer] += 1
        self.freer.append(freer)
        self.freed.append(self.count[freer])


def job_table():
    jobs = Jobs()
    for k in range(NK):
        jobs.add(("x_t", k), "dve")
    jobs.add("sum0", "dve")
    jobs.add("ik_tok", "dve")
    jobs.add(("v_tok", "a"), "act")
    jobs.add(("v_tok", "b"), "act")
    jobs.add("ik_t", "act")
    for qt in range(1, NT):
        for h in range(HEADS):
            jobs.add(("index", qt, h), "act")
    for what, n in pe_attention():
        if what != "values":
            jobs.add((what, n), "act" if what == "probs_t" else "dve")
    for n in (1, 2, 3):
        jobs.add(f"sum{n}", "dve")
    for j in range(2):
        jobs.add(("z", j), "dve")
    for h in range(GH):
        jobs.add(("gv_tok", h), "act")
    for j in range(2):
        jobs.add(("kend_tok", j), "act")
    for n in range(NCH - 1):
        jobs.add(("inc", n), "dve")
    for h in range(GH):
        jobs.add(("scores", h), "dve")
    for h in range(GH):
        jobs.add(("o", h), "dve")
        jobs.add(("o_sum", h), "dve")
    for g in range(4):
        jobs.add(("pool", g), "dve")
    jobs.add("sum4", "dve")
    jobs.add("route", "dve")
    for i in range(NT):
        for n in range(2):
            jobs.add(("rows", i, n), "act")
    jobs.add("places", "dve")
    return jobs


def gated_blocks(nc, A, out):
    sems, stack = {}, ExitStack()

    def S(name):
        if name not in sems:
            sems[name] = stack.enter_context(nc.semaphore(name))
        return sems[name]

    with stack:
        base = nc.sbuf_base() if callable(nc.sbuf_base) else nc.sbuf_base
        base = -(-base // 64) * 64

        def place(name, shape, offset, dt=F32):
            return nc.alloc_sbuf_tensor_at(name, shape, dt, offset=offset)

        def words(shape):
            n = 4
            for s in shape[1:]:
                n *= s
            return -(-n // 32) * 32

        def lay(at, *tensors):
            made = []
            for name, shape, *dt in tensors:
                made.append(place(name, shape, at, *dt))
                at += words(shape)
            return (*made, at)

        (con, small, ones, eps_t, rs, ssum, sq, nt0, ikstat, ikmv, ikr, iw, sinkb, lnwb, top8,
         mx, nm, den, es, xT, top) = lay(
            base, ("con", [P, CONST_WIDTH]), ("small", [P, 64]), ("ones", [P, P]), ("eps_t", [P, 1]),
            ("rs", [P, L]), ("ssum", [P, L]), ("sq", [P, 2, L]), ("nt0", [P, L]),
            ("ikstat", [P, NT, 6]), ("ikmv", [P, NT, 2]), ("ikr", [P, 4, NT]), ("iw", [P, NT, HEADS]),
            ("sinkb", [P, HEADS]), ("lnwb", [P, 2, HD]), ("top8", [P, NT - 1, 8]),
            ("mx", [P, 2 * NT, HEADS]), ("nm", [P, 2 * NT, HEADS]), ("den", [P, 2 * NT, HEADS]),
            ("es", [P, 2 * NT, HEADS]), ("xT", [P, NK, L]))
        KEEP_AT = {1: 0, 2: 2 * P, 3: 5 * P}
        keep = place("keep", [P, 9 * P], base + sum(words(x) for x in (
            [P, CONST_WIDTH], [P, 64], [P, P], [P, 1], [P, L], [P, L])))
        v_tok_a_at = base + sum(words(x) for x in ([P, CONST_WIDTH], [P, 64], [P, P], [P, 1], [P, L]))

        def const(name, rows=P):
            a, b = CONST_COLS[name]
            return con[0:rows, a:b]

        ident = const("ident")
        g_attn, g_mlp, g_fin, g_n1, g_n2 = (small[:, 8 * i:8 * i + 8] for i in range(5))
        b_alpha, g_gla, p_scale = small[:, 40:42], small[:, 42:46], small[:, 46:50]
        g_fin1 = small[:, 50:58]

        raw, whi, wlo, a_at = lay(top, ("raw", [P, RING, D]), ("whi", [P, RING, D], F32R),
                                  ("wlo", [P, RING, D], F32R))
        actA_hi, actA_lo, b_at = lay(a_at, ("actA_hi", [P, NK, L], F32R), ("actA_lo", [P, NK, L], F32R))
        actB_hi, actB_lo, s_at = lay(b_at, ("actB_hi", [P, NK, L], F32R), ("actB_lo", [P, NK, L], F32R))
        pbuf, pT, o_n, _ = lay(a_at, ("pbuf", [P, 3, L]), ("pT", [P, 2, L]), ("o_n", [P, 2, L]))
        x_tok, _ = lay(b_at, ("x_tok", [P, NT, D]))
        iqT, score, rel, ik_s, ikn, ikrope, ikt, ikT, _ = lay(
            b_at, ("iqT", [P, 4, L]), ("score", [P, NT - 1, L]), ("rel", [P, 4, L]), ("ik_s", [P, L]),
            ("ikn", [P, NT, HD]), ("ikrope", [P, NT, 2 * HD]), ("ikt", [P, 4, NT * 32]), ("ikT", [P, L]))
        sg, aqT, bqT, akT, bkT, bv_tok, end1 = lay(
            s_at, ("sg", [P, 2, NK, L]), ("aqT", [P, 4, L]), ("bqT", [P, 4, L]), ("akT", [P, 2, L]),
            ("bkT", [P, 2, L]), ("bv_tok", [P, NT, P]))
        av_tok = place("av_tok", [P, NT, P], v_tok_a_at)
        rot, rt1, vT, _ = lay(s_at, ("rot", [P, 2, L]), ("rt1", [P, L]), ("vT", [P, 2, L]))
        mixb, mixt, _ = lay(s_at + words([P, 2, NK, L]), ("mixb", [P, 2, L]), ("mixt", [P, 2, L]))
        relu_u, u_sq, ytmp, _ = lay(s_at, ("relu_u", [P, 2, L]), ("u_sq", [P, 2, L]), ("ytmp", [P, L]))
        kT = {"a": akT, "b": bkT}
        qT = {"a": aqT, "b": bqT}
        v_tok = {"a": av_tok, "b": bv_tok}
        sg2, qdec, gv_tok, rsil, rsf, ssum2, go, end2 = lay(
            s_at, ("sg2", [P, 2, NK, L]), ("qdec", [P, 2, L]), ("gv_tok", [P, NT, GH * DV]),
            ("rsil", [P, GH, L]), ("rsf", [P, L]), ("ssum2", [P, L]), ("go", [P, L]))
        qs, ks, kend, pool_t, _ = lay(s_at, ("qs", [P, 2, L]), ("ks", [P, 2, L]), ("kend", [P, 2, L]),
                                      ("pool_t", [P, 2, L]))
        diff, alow, wal, pw, rs_o, dec, _ = lay(
            s_at + words([P, NK, L]), ("diff", [P, 4, L]), ("alow", [16, L]), ("wal", [16, 2 * P]),
            ("pw", [P, 4, P]), ("rs_o", [P, L]), ("dec", [P, 2, NCH]))
        gvT = place("gvT", [P, GH, L], s_at + words([P, 18, L]) + words([P, NT, GH * DV]))
        o_s = ssum2
        pool_t2 = place("pool_t2", [P, 2, L], base + sum(words(x) for x in (
            [P, CONST_WIDTH], [P, 64], [P, P], [P, 1], [P, L], [P, L])))
        half = words([P, 4, L])
        zs = place("zs", [P, 2, L], a_at)
        az = place("az", [P, 2, L], a_at + half // 2)
        kend_tok = place("kend_tok", [P, NT, 2 * P], a_at)
        gst = place("gst", [P, 2, NCH, DV], a_at + half)
        cs = place("cs", [P, 2, L], a_at + 2 * half)
        kdec = place("kdec", [P, 2, L], a_at + 2 * half + half // 2)
        scT = place("scT", [P, GH, L], a_at + 3 * half)
        (wring, xe, xeT, hid, hidT, ye, wr, brt, lg, rt, gw, slot_of, tabi, gix, six, gfin, h2T, end3) = lay(
            top, ("wring", [P, RING, 6 * D]), ("xe", [P, 2, D]), ("xeT", [P, 2, D]), ("hid", [P, 2, DE]),
            ("hidT", [P, 2, DE]), ("ye", [P, 2, D]), ("wr", [P, NK, NG + NE]), ("brt", [P, NG + NE]),
            ("lg", [P, NT, NG + NE]), ("rt", [P, 10, NT * NE]), ("gw", [P, 16, NT]),
            ("slot_of", [P, 2, NT], I32), ("tabi", [P, 3, NB + 2], I32), ("gix", [P, 2], I32), ("six", [P, 2], I32),
            ("gfin", [P, D]), ("h2T", [P, NK, L]))
        y2, _ = lay(end3 - words([P, NK, L]), ("y2", [P, 2, 2 * D]))
        over_n = place("over_n", [1, 16], end3, I32)
        assert max(end1, end2, end3 + 64) <= nc.sbuf_usable_end

        bank = [stack.enter_context(nc.psum_tensor(f"bank{i}", [P, L], F32)) for i in range(RING)]
        side = [stack.enter_context(nc.psum_tensor(f"side{i}", [P, L], F32)) for i in range(4)]
        jobs = job_table()

        h2_rows = nc.dram_tensor("h2_rows", [L, D], F32).ap()
        y2_rows = nc.dram_tensor("y2_rows", [2 * L, D], F32).ap()
        slot_rows = nc.dram_tensor("slot_rows", [P * NB, 1], I32).ap()

        w_in_v = A["w_in"][0].rearrange("(k p) n -> p k n", p=P)
        w_in2_v = A["w_in_2"][0].rearrange("(k p) n -> p k n", p=P)
        br_v = [A[n][0].rearrange("(k p) n -> p k n", p=P) for n in ("w_branch_a", "w_branch_b")]
        br2_v = [A[n][0].rearrange("(k p) n -> p k n", p=P) for n in ("w_gla_branch_2", "w_pool_branch_2")]
        w_out_v = A["w_out"][0].rearrange("(k p) n -> p k n", p=P)
        w_out2_v = A["w_out_2"][0].rearrange("(k p) n -> p k n", p=P)
        w_up_v = A["w_up"][0].rearrange("(k p) n -> p k n", p=P)
        w_down_v = A["w_down"][0].rearrange("(k p) n -> p k n", p=P)

        def loads(c):
            return 2 if C_BR <= c < C_OUT or C_BR2 <= c < C_OUT2 else 1

        def raw_value(c):
            return 16 * sum(loads(j) for j in range(c % RING, c + 1, RING))

        raw_loaded = [S(f"raw_loaded{r}") for r in range(RING)]
        hi_made, lo_made, chunk_done, chunk_freed = S("hi_made"), S("lo_made"), S("chunk_done"), S("chunk_freed")
        side_full = S("side_full")
        side_freed = {"dve": S("side_freed_by_dve"), "act": S("side_freed_by_act")}
        STAGES = ("in", "branch", "out", "mlp", "in2", "branch2", "out2")

        def at(i, u, k):
            return u + k if i is None else RING * i + (u + k)

        def wait_from(e, sem, i, u, k):
            if i is not None or u + k > 0:
                e.wait_ge(sem, at(i, u, k))

        def for_experts(e, expert):
            for u in range(RING):
                expert(None, u)
            with e.Fori(1, NE // RING) as i:
                for u in range(RING):
                    expert(i, u)
            e.wait_ge(S("over_ready"), 1)
            over = e.value_load(over_n[0:1, 0:1], min_val=0, max_val=OVER)
            with e.If(over > 0):
                with e.Fori(NE // RING, NB // RING) as i:
                    for u in range(RING):
                        expert(i, u)

        block = stack.enter_context(nc.Block())

        @block.sync
        def _(sp):
            for i in range(NT):
                sp.dma_start(x_tok[:, i, :], A["x"][0, i * P:(i + 1) * P, :]).then_inc(S("x_in"), 16)
            sp.dma_start(con[:, :], A["consts"]).then_inc(S("x_in"), 16)

            def load_chunk(c, wait, *views):
                if wait is not None:
                    sp.wait_ge(lo_made, wait)
                for k0, k1, v in views:
                    sp.dma_start(raw[:, c % RING, k0 * P:k1 * P].rearrange("p (k n) -> p k n", n=P), v)\
                      .then_inc(raw_loaded[c % RING], 16)

            def load_group(first, n, view, col, step=P):
                if n % RING or first < RING:
                    for j in range(n):
                        c = first + j
                        load_chunk(c, c - RING + 1 if c >= RING else None,
                                   (0, NK, view[:, :, col + P * j:col + P * (j + 1)]))
                    return
                with sp.Fori(0, n // RING) as i:
                    for u in range(RING):
                        load_chunk(first + u, first + u - RING + 1 + RING * i,
                                   (0, NK, view[:, :, bass.ds(i * (RING * P) + (col + u * P), P)]))

            def load_branches(first, views):
                with sp.Fori(0, NK // RING) as i:
                    for u in range(RING):
                        at = bass.ds(i * (RING * P) + u * P, P)
                        load_chunk(first + u, first + u - RING + 1 + RING * i,
                                   (0, 4, views[0][:, :, at]), (4, 8, views[1][:, :, at]))

            load_group(0, 1, w_in_v, 1280)
            for name, t in (("attn_norm_w", g_attn), ("mlp_norm_w", g_mlp), ("norm1_g_2", g_n1), ("norm2_g_2", g_n2)):
                sp.dma_start(t, A[name][0].rearrange("(k p) -> p k", p=P), allow_slow_non_contiguous=True)\
                  .then_inc(S("small_in"), 16)
            sp.dma_start(g_fin, A["final_norm_w"].rearrange("(k p) -> p k", p=P), allow_slow_non_contiguous=True)\
              .then_inc(S("small_in"), 16)
            for name, t in (("b_alpha_2", b_alpha), ("gla_norm_g_2", g_gla), ("pool_scale_2", p_scale)):
                sp.dma_start(t, A[name][0].rearrange("(k p) -> p k", p=P), allow_slow_non_contiguous=True)\
                  .then_inc(S("small_in"), 16)
            sp.dma_start(sinkb[:, :], A["sinks"][0].partition_broadcast(P)).then_inc(S("small_in"), 16)
            sp.dma_start(lnwb[:, 0, :], A["idx_k_norm_w"][0].partition_broadcast(P)).then_inc(S("small_in"), 16)
            sp.dma_start(lnwb[:, 1, :], A["idx_k_norm_b"][0].partition_broadcast(P)).then_inc(S("small_in"), 16)
            for j, n, col in IN1_GROUPS:
                load_group(C_IN + j, n, w_in_v, col)
            load_branches(C_BR, br_v)
            load_group(C_OUT, NK, w_out_v, 0)
            for q in range(QUARTERS):
                load_group(C_MLP + 2 * NK * q, NK, w_up_v, D * q)
                load_group(C_MLP + 2 * NK * q + NK, NK, w_down_v[:, NK * q:NK * (q + 1), :], 0)
            load_group(C_IN2, 1, w_in2_v, 1536)
            sp.wait_ge(chunk_freed, C_OUT)
            sp.dma_start(wal[:, :], A["w_alpha_up_2"][0]).then_inc(S("small2_in"), 16)
            sp.dma_start(pw[:, :, :], A["pool_w_2"][0].rearrange("g c d -> c g d")).then_inc(S("small2_in"), 16)
            for j, n, col in IN2_GROUPS:
                load_group(C_IN2 + j, n, w_in2_v, col)
            load_branches(C_BR2, br2_v)
            load_group(C_OUT2, NK, w_out2_v, 0)

            sp.wait_ge(S("dense_over"), 1)
            sp.wait_ge(S("table_ready"), 2)
            sp.dma_start(slot_rows.rearrange("(p b) o -> p (b o)", b=NB), tabi[:, 0, 0:NB]).then_inc(S("table_in"), 16)
            sp.dma_start(wr[:, :, 0:NG], A["w_router_group_2"][0].rearrange("(k p) g -> p k g", p=P),
                         allow_slow_non_contiguous=True).then_inc(S("route_in"), 16)
            for g in range(NG):
                sp.dma_start(wr[:, :, NG + EPG * g:NG + EPG * (g + 1)],
                             A["w_router_expert_2"][0, g].rearrange("(k p) e -> p k e", p=P),
                             allow_slow_non_contiguous=True).then_inc(S("route_in"), 16)
            sp.dma_start(brt[:, 0:NG], A["b_router_group_2"][0].partition_broadcast(P)).then_inc(S("route_in"), 16)
            sp.dma_start(brt[:, NG:], A["b_router_expert_2"][0].rearrange("g e -> (g e)").partition_broadcast(P))\
              .then_inc(S("route_in"), 16)
            sp.dma_start(gfin[:, :], A["norm_f_g_2"].partition_broadcast(P)).then_inc(S("route_in"), 16)

            wg_v = A["w_exp_gate_2"][0].rearrange("e (k p) n -> p e k n", p=P)
            wu_v = A["w_exp_up_2"][0].rearrange("e (k p) n -> p e k n", p=P)
            wd_v = A["w_exp_down_2"][0].rearrange("e (k p) n -> p e k n", p=P)

            def load_expert(slot, e):
                gu = wring[:, slot, 0:4 * D].rearrange("p (k h n) -> p k h n", h=2, n=DE)
                down = wring[:, slot, 4 * D:6 * D].rearrange("p (o k n) -> p o k n", o=1, n=D)
                at = slice(e, e + 1) if isinstance(e, int) else bass.ds(e, 1)
                for h, v in enumerate((wg_v, wu_v)):
                    sp.dma_start(gu[:, :, h, :], v[:, at, :, :].rearrange("p e k n -> p (e k) n"))\
                      .then_inc(S(f"expert_in{slot}"), 16)
                sp.dma_start(down, wd_v[:, at, :, :]).then_inc(S(f"expert_in{slot}"), 16)

            for e in range(RING):
                load_expert(e, e)
            for i in range(NT):
                sp.wait_ge(S("rows_out"), 2 * (i + 1))
                sp.dma_start(h2_rows[i * P:(i + 1) * P, :], xe[:, i % 2, :]).then_inc(S(f"h2_stored{i % 2}"), 16)
            sp.wait_ge(S("table_scattered"), 16 * 2 * NT)
            sp.dma_start(tabi[:, 0, 0:NB], slot_rows.rearrange("(p b) o -> p (b o)", b=NB)).then_inc(S("table_back"), 16)
            with sp.Fori(1, NE // RING) as i:
                for u in range(RING):
                    sp.wait_ge(S("down_done"), RING * i + (u - RING + 1))
                    load_expert(u, RING * i + u)
            sp.wait_ge(S("over_ready"), 1)
            over = sp.value_load(over_n[0:1, 0:1], min_val=0, max_val=OVER)
            with sp.If(over > 0):
                with sp.Fori(0, OVER // RING) as i:
                    for u in range(RING):
                        sp.wait_ge(S("down_done"), RING * i + (NE + u - RING + 1))
                        e = sp.value_load(over_n[0:1, bass.ds(RING * i + (1 + u), 1)], min_val=0, max_val=NE - 1)
                        load_expert(u, e)

            sp.wait_ge(S("experts_over"), 1)
            for i in range(NT):
                if i >= 2:
                    sp.wait_ge(S("final_sum"), i - 1)
                sp.dma_start(y2[:, i % 2, :].rearrange("p (k n) -> p k n", k=2),
                             y2_rows.rearrange("(k t p) n -> t p k n", k=2, p=P)[i]).then_inc(S(f"y2_in{i % 2}"), 16)
            for i in range(NT):
                sp.wait_ge(S("final_out"), i + 1)
                sp.dma_start(out[i * P:(i + 1) * P, :], ye[:, i % 2, :]).then_inc(S(f"stored{i % 2}"), 16)
            for j in range(2):
                sp.wait_ge(S(f"stored{j}"), 16 * NT // 2)

        @block.gpsimd
        def _(pool):
            def second_part(slot, wait):
                pool.wait_ge(hi_made, wait)
                nc.gpsimd.tensor_tensor(wlo[:, slot, :], raw[:, slot, :], whi[:, slot, :].bitcast(F32),
                                        ALU.subtract).then_inc(lo_made, 1)

            with pool.Fori(0, N_CHUNKS // RING) as i:
                for u in range(RING):
                    second_part(u, RING * i + (u + 1))
            for c in range(N_CHUNKS // RING * RING, N_CHUNKS):
                second_part(c % RING, c + 1)

            pool.wait_ge(S("dense_over"), 1)
            pool.wait_ge(S("table_in"), 16)
            pool.wait_ge(S("slots_made"), 2)
            for k in range(2):
                for i in range(NT):
                    pool.indirect_dma_start(
                        slot_rows, bass.IndirectOffsetOnAxis(ap=slot_of[:, k, i:i + 1], axis=0),
                        tabi[:, 2, NT * k + i:NT * k + i + 1], None).then_inc(S("table_scattered"), 16)
            for j in range(2):
                pool.wait_ge(S(f"h2_stored{j}"), 16 * NT // 2)
            for j in range(2):
                nc.gpsimd.memset(xe[:, j, :], 0.0).then_inc(S("xe_clear"), 1)
            pool.wait_ge(S("xe_clear"), 2)
            pool.wait_ge(S("rows_ready"), 1)

            row_bound, slot_bound = pool.to_reg(L - 1), pool.to_reg(2 * L - 1)

            def gather(j, b, used, column_set, copies):
                if used is not None:
                    pool.wait_ge(S("xe_used"), used)
                nc.gpsimd.tensor_copy(gix[:, j:j + 1], tabi[:, 1, bass.ds(b, 1)]).then_inc(S(column_set), 1)
                pool.wait_ge(S("rows_ready"), 1)
                pool.wait_ge(S(column_set), copies)
                pool.indirect_dma_start(xe[:, j, :], None, h2_rows,
                                        bass.IndirectOffsetOnAxis(ap=gix[:, j:j + 1], axis=0),
                                        bounds_check=row_bound, oob_is_err=False).then_inc(S(f"gathered{j}"), 16)

            def scatter(j, b, copies):
                pool.wait_ge(S("y_by_act"), copies)
                pool.wait_ge(S("y_by_dve"), copies)
                nc.gpsimd.tensor_copy(six[:, j:j + 1], tabi[:, 0, bass.ds(b, 1)]).then_inc(S("six_set"), 1)
                pool.wait_ge(S("table_back"), 16)
                pool.wait_ge(S("six_set"), copies)
                pool.indirect_dma_start(y2_rows, bass.IndirectOffsetOnAxis(ap=six[:, j:j + 1], axis=0),
                                        ye[:, j, :], None, bounds_check=slot_bound, oob_is_err=False)\
                    .then_inc(S(f"scattered{j}"), 16)

            gather(0, 0, None, "first_gix_set", 1)
            gather(1, 1, None, "first_gix_set", 2)
            with pool.Fori(0, NE // 2) as i:
                for j in range(2):
                    scatter(j, 2 * i + j, 2 * i + (j + 1))
                    pool.wait_ge(S(f"scattered{j}"), 16 * i + 16)
                    gather(j, 2 * i + (j + 2), 2 * i + (j + 1), "gix_set", 2 * i + (j + 1))
            pool.wait_ge(S("over_ready"), 1)
            over = pool.value_load(over_n[0:1, 0:1], min_val=0, max_val=OVER)
            with pool.If(over > 0):
                with pool.Fori(0, OVER // 2) as i:
                    for j in range(2):
                        scatter(j, 2 * i + (NE + j), 2 * i + (NE + j + 1))
                        pool.wait_ge(S(f"scattered{j}"), 16 * i + (16 * NE // 2 + 16))
                        gather(j, 2 * i + (NE + j + 2), 2 * i + (NE + j + 1), "gix_set", 2 * i + (NE + j + 1))
                for j in range(2):
                    pool.wait_ge(S(f"gathered{j}"), 16 * (NB // 2 + 1))
            for j in range(2):
                pool.wait_ge(S(f"gathered{j}"), 16 * (NE // 2 + 1))
            nc.gpsimd.memset(gix[:, :], 0).then_inc(S("experts_over"), 1)

        def wait_job(e, name):
            e.wait_ge(side_full, jobs.at[name] + 1)

        def wait_freed(e, name):
            i = jobs.at[name]
            e.wait_ge(side_freed[jobs.freer[i]], jobs.freed[i])

        def side_of(name):
            return side[jobs.at[name] % 4]

        def out_bank(c):
            return bank[c % RING]

        class Chain:

            def __init__(self, e, sem):
                self.e, self.sem, self.n = e, sem, {}

            def __call__(self, ins, sem=None):
                sem = sem or self.sem
                self.n[id(sem)] = self.n.get(id(sem), 0) + 1
                ins.then_inc(sem, 1)
                self.e.wait_ge(sem, self.n[id(sem)])

        def rope_index(c):
            return [1, 2, 3, 4, 5, 6, 7, 8, 9, 11, 13, 14, 15, 16].index(c)

        ROPED = (1, 2, 3, 4, 5, 6, 7, 8, 9, 11, 13, 14, 15, 16)
        N_SMALL = 11

        @block.scalar
        def _(act):
            chain = Chain(act, S("act_step"))
            a = nc.scalar.activation

            def first_part(c):
                if c >= N_CHUNKS:
                    return
                act.wait_ge(raw_loaded[c % RING], raw_value(c))
                if c >= RING:
                    act.wait_ge(chunk_done, c - RING + 1)
                a(whi[:, c % RING, :], raw[:, c % RING, :], ACT.Copy).then_inc(hi_made, 1)

            def split_first(stage, hi, k, src, gain):
                ins = a(hi[:, k, :], src, ACT.Copy) if gain is None else \
                    a(hi[:, k, :], src, ACT.Copy, scale=gain[:, k:k + 1])
                ins.then_inc(S(f"hi_{stage}"), 1)

            def squares(n, src, gain=None, of="sq_made", added="sum_added"):
                if n >= 2:
                    act.wait_ge(S(added), n - 1)
                ins = a(sq[:, n % 2, :], src, ACT.Square) if gain is None else \
                    a(sq[:, n % 2, :], src, ACT.Square, scale=gain)
                ins.then_inc(S(of), 1)

            def guess(src, n, dst=None, width=D, tmp=None):
                dst = rs[:, :] if dst is None else dst
                tmp = nt0[:, :] if tmp is None else tmp
                nc.scalar.preload_act_table_set("natural_log_exp_and_others")
                chain(a(tmp, src, ACT.Ln, scale=1.0 / width, bias=eps_t[:, :]))
                chain(a(dst, tmp, ACT.Exp, scale=-0.5), S("guess_made"))

            act.wait_ge(S("x_in"), 16 * (NT + 1))
            act.wait_ge(S("eps_set"), 1)
            act.wait_ge(S("small_in"), 16 * N_SMALL)
            first_part(0)
            for k in range(NK):
                wait_freed(act, ("x_t", k))
                split_first("in", actA_hi, k, xT[:, k, :], g_attn)
                squares(k, xT[:, k, :])
            first_part(1)
            first_part(2)
            wait_job(act, "sum0")
            guess(side_of("sum0")[:, :], 0)
            for c in range(C_IN, C_IN + 17):
                first_part(c + AHEAD)
                if c in ROPED:
                    r = ROPED.index(c)
                    act.wait_ge(chunk_done, c + 1)
                    if r >= 2:
                        act.wait_ge(S("roped"), r - 1)
                    for q in range(4):
                        other = 32 * (q ^ 1)
                        ins = a(rot[32 * q:32 * q + 32, r % 2, :], out_bank(c)[other:other + 32, :], ACT.Copy,
                                scale=-1.0 if q % 2 == 0 else 1.0)
                    ins.then_inc(S("rot_made"), 1)
                if c == 6:
                    act.wait_ge(S("ik_var"), 1)
                    guess(ikmv[:, :, 1], 1, ikr[:, 1, :], 1, ikr[:, 0, :])
                if c == 12:
                    for n, b in enumerate("ab"):
                        wait_job(act, ("v_tok", b))
                        a(v_tok[b][:, :, :].rearrange("p t f -> p (t f)"), side_of(("v_tok", b))[:, :], ACT.Copy)\
                            .then_inc(side_freed["act"], 1)
                    wait_job(act, "ik_t")
                    a(ikT[:, :], side_of("ik_t")[:, :], ACT.Copy).then_inc(side_freed["act"], 1)
            n = 0
            for qt in range(1, NT):
                for h in range(HEADS):
                    wait_job(act, ("index", qt, h))
                    if n >= 4:
                        act.wait_ge(S("index_added"), n - 3)
                    w = (qt + 1) * P
                    a(rel[:, n % 4, 0:w], side_of(("index", qt, h))[:, 0:w], ACT.Relu).then_inc(side_freed["act"], 1)
                    n += 1
            for c in range(C_IN + 17, C_IN + 33):
                if c + AHEAD < C_BR + AHEAD:
                    first_part(c + AHEAD)
                j = c - C_IN - 17
                act.wait_ge(chunk_freed, c + 1)
                t = sg[:, j // NK, j % NK, :]
                a(t, t, ACT.Sigmoid).then_inc(S("gate_made"), 1)

            nc.scalar.preload_act_table_set("natural_log_exp_and_others")
            for s in range(STEPS):
                if s % 8 == 7 and s >= 15:
                    g = s // 8 - 1
                    b, qt = unit(g * HEADS)[:2]
                    k = 4 if b == "b" else 0
                    wait_job(act, ("out_t", g))
                    a(actB_hi[:, k:k + 4, qt * P:(qt + 1) * P],
                      side_of(("out_t", g))[:, :].rearrange("p (f q) -> p f q", q=P), ACT.Copy)\
                        .then_inc(S("hi_branch"), 1)
                if s < UNITS:
                    b, qt, k0, nk, h = unit(s)
                    t = pbuf[:, s % 3, 0:nk * P]
                    act.wait_ge(S("logits_made"), s + 1)
                    a(t, t, ACT.Exp, bias=nm[:, s // HEADS, h:h + 1],
                      accum_out=den[:, s // HEADS, h:h + 1]).then_inc(S("probs_made"), 1)
                if 1 <= s < UNITS + 1:
                    u = s - 1
                    nk = unit(u)[3]
                    wait_job(act, ("probs_t", u))
                    if u >= 2:
                        act.wait_ge(S("values_done"), u - 1)
                    a(pT[:, u % 2, 0:nk * P], side_of(("probs_t", u))[:, 0:nk * P], ACT.Copy)\
                        .then_inc(side_freed["act"], 1)
                if s % 8 == 1 and 9 <= s <= 8 * NT + 1:
                    g = s // 8 - 1
                    act.wait_ge(S("sinks_shifted"), g + 1)
                    a(es[:, g, :], es[:, g, :], ACT.Exp).then_inc(S("sinks_exp"), 1)

            def mix_parts(first, stage, hi):
                for m in range(NK):
                    first_part(first + m + AHEAD)
                    act.wait_ge(S(f"mixed_{stage}"), m + 1)
                    split_first(stage, hi, m, mixb[:, m % 2, :], None)

            mix_parts(C_BR, "out", actA_hi)
            for m in range(NK):
                first_part(C_OUT + m + AHEAD)
                act.wait_ge(chunk_freed, C_OUT + m + 1)
                split_first("mlp", actB_hi, m, xT[:, m, :], g_mlp)
                squares(NK + m, xT[:, m, :])
            for q in range(QUARTERS):
                up = C_MLP + 2 * NK * q
                for m in range(NK):
                    first_part(up + m + AHEAD)
                    act.wait_ge(chunk_freed, up + m + 1)
                    chain(a(u_sq[:, m % 2, :], relu_u[:, m % 2, :], ACT.Square), S("u_made"))
                    split_first(f"u{q}", actA_hi, m, u_sq[:, m % 2, :], None)
                if q == 0:
                    wait_job(act, "sum1")
                    guess(side_of("sum1")[:, :], 2)
                for m in range(NK):
                    first_part(up + NK + m + AHEAD)
                    if q == QUARTERS - 1:
                        act.wait_ge(S("x1_made"), m + 1)
                        split_first("in2", actB_hi, m, xT[:, m, :], g_fin1)
                        squares(2 * NK + 2 * m, xT[:, m, :])
                        squares(2 * NK + 2 * m + 1, xT[:, m, :], g_fin[:, m:m + 1])
            wait_job(act, "sum2")
            guess(side_of("sum2")[:, :], 3, rsf[:, :])
            act.wait_ge(S("second_sum"), 1)
            guess(ssum2[:, :], 4)

            for c in range(C_IN2, C_IN2 + 5):
                first_part(c + AHEAD)
            for j in range(2):
                wait_freed(act, ("z", j))
                chain(a(az[:, j, :], zs[:, j, :], ACT.Abs))
                chain(a(az[:, j, :], az[:, j, :], ACT.Exp, scale=-1.0))
                a(az[:, j, :], az[:, j, :], ACT.Ln, bias=1.0).then_inc(S("log_made"), 1)
            for c in range(C_IN2 + 5, C_IN2 + 9):
                first_part(c + AHEAD)
            for j in range(2):
                act.wait_ge(S("decay_summed"), j + 1)
                a(az[:, j, :], cs[:, j, :], ACT.Exp, scale=1.0 / 16.0).then_inc(S("decays"), 1)
                a(zs[:, j, :], cs[:, j, :], ACT.Exp, scale=-1.0 / 16.0).then_inc(S("decays"), 1)
            for j in range(2):
                act.wait_ge(S("decay_left"), j + 1)
                a(cs[:, j, :], cs[:, j, :], ACT.Exp, scale=1.0 / 16.0).then_inc(S("decays"), 1)
            for h in range(GH):
                wait_job(act, ("gv_tok", h))
                a(gv_tok[:, :, h * DV:(h + 1) * DV], side_of(("gv_tok", h))[:, :].rearrange("p (t f) -> p t f", f=DV),
                  ACT.Copy).then_inc(side_freed["act"], 1)
            for c in range(C_IN2 + 9, C_IN2 + 13):
                first_part(c + AHEAD)
                h = c - C_IN2 - 9
                act.wait_ge(chunk_freed, c + 1)
                a(pool_t[:, h % 2, :], rsil[:, h, :], ACT.Sigmoid).then_inc(S("r_sigmoid"), 1)
                act.wait_ge(S("r_silu"), h + 1)
            for c in range(C_IN2 + 13, C_IN2 + 17):
                first_part(c + AHEAD)
            for j in range(2):
                wait_job(act, ("kend_tok", j))
                a(kend_tok[:, :, j * P:(j + 1) * P], side_of(("kend_tok", j))[:, :].rearrange("p (t f) -> p t f", f=P),
                  ACT.Copy).then_inc(side_freed["act"], 1)

            def gate(c):
                first_part(c + AHEAD)
                j = c - C_IN2 - 17
                act.wait_ge(chunk_freed, c + 1)
                t = sg2[:, j // NK, j % NK, :]
                a(t, t, ACT.Sigmoid).then_inc(S("gate_made"), 1)

            for c in range(C_IN2 + 17, C_IN2 + 21):
                gate(c)
            for h in range(GH):
                wait_job(act, ("o", h))
                n = 4 * NK + h
                act.wait_ge(S("o_sum_taken"), h) if h else None
                a(sq[:, 0, :], side_of(("o", h))[:, :], ACT.Square).then_inc(S("o_squares"), 1)
                wait_job(act, ("o_sum", h))
                guess(side_of(("o_sum", h))[:, :], 5 + h, rs_o[:, :], DV)
                act.wait_ge(S("o_normed"), h + 1)
                split_first("branch2", actA_hi, h, o_s[:, :], None)
            for c in range(C_IN2 + 21, C_IN2 + 25):
                gate(c)
            for g in range(4):
                wait_freed(act, ("pool", g))
                split_first("branch2", actA_hi, 4 + g, pool_t2[:, g % 2, :], None)
            for c in range(C_IN2 + 25, C_IN2 + 33):
                gate(c)
            mix_parts(C_BR2, "out2", actB_hi)
            for m in range(NK):
                first_part(C_OUT2 + m + AHEAD)
                act.wait_ge(chunk_freed, C_OUT2 + m + 1)
                squares(m, xT[:, m, :], None, "sq4_made", "sum4_added")
            wait_job(act, "sum4")
            guess(side_of("sum4")[:, :], 9)

            act.wait_ge(S("group_shifted"), 1)
            a(rt[:, 0, 0:NT * NG], rt[:, 0, 0:NT * NG], ACT.Exp).then_inc(S("group_exp"), 1)
            act.wait_ge(S("expert_shifted"), 1)
            a(gw[:, 6, :], gw[:, 6, :], ACT.Exp).then_inc(S("expert_exp"), 1)
            for i in range(NT):
                for n in range(2):
                    wait_job(act, ("rows", i, n))
                    if i >= 2 and n == 0:
                        act.wait_ge(S(f"h2_stored{i % 2}"), 16)
                    chain(a(xe[:, i % 2, n * L:(n + 1) * L], side_of(("rows", i, n))[:, :], ACT.Copy), S("rows_out"))
                    act.sem_inc(side_freed["act"], 1)

            def x_turned(i, u):
                act.wait_ge(S("xe_used"), at(i, u, 2))
                wait_from(act, S("gate_up_done"), i, u, 0)
                a(xeT[:, (u + 1) % 2, 0:L], side[0][:, :], ACT.Copy).then_inc(S("xe_t_by_act"), 1)

            def expert(i, u):
                act.wait_ge(S("gate_up_done"), at(i, u, 1))
                wait_from(act, S("hid_turned"), i, u, -1)
                a(hid[:, u % 2, :], bank[u % 2][:, 0:DE], ACT.Silu).then_inc(S("silu_made"), 1)
                x_turned(i, u)
                act.wait_ge(S("down_done"), at(i, u, 1))
                if i is not None or u >= 2:
                    act.wait_ge(S(f"scattered{u % 2}"), 16 * (u // 2) if i is None else 32 * i + 16 * (u // 2))
                a(ye[:, u % 2, 0:L], bank[2][:, :], ACT.Copy).then_inc(S("y_by_act"), 1)

            act.wait_ge(S("xe_used"), 1)
            a(xeT[:, 0, 0:L], side[0][:, :], ACT.Copy).then_inc(S("xe_t_by_act"), 1)
            for_experts(act, expert)

            act.wait_ge(S("experts_over"), 1)
            for i in range(NT):
                act.wait_ge(S("final_sum"), i + 1)
                chain(a(xe[:, 0, :], ye[:, i % 2, :], ACT.Square, accum_out=gw[:, 12, i:i + 1]))
                guess(gw[:, 12, i:i + 1], 10 + i, gw[:, 13, i:i + 1], D, gw[:, 14, i:i + 1])

        @block.vector
        def _(dve):
            chain = Chain(dve, S("dve_step"))
            v = nc.vector
            guesses = [0]

            def refine(src, dst=None, width=D, tmp=None, tmp2=None, freed=None):
                dst = rs[:, :] if dst is None else dst
                tmp = nt0[:, :] if tmp is None else tmp
                tmp2 = ssum[:, :] if tmp2 is None else tmp2
                guesses[0] += 1
                dve.wait_ge(S("guess_made"), guesses[0])
                chain(v.tensor_scalar(tmp, src, -0.5 / width, -0.5 * EPS, ALU.mult, ALU.add), freed)
                chain(v.tensor_tensor(tmp2, dst, dst, ALU.mult))
                chain(v.tensor_tensor(tmp2, tmp2, tmp, ALU.mult))
                chain(v.scalar_tensor_tensor(dst, tmp2, 1.5, dst, ALU.add, ALU.mult))

            def second(stage, hi, lo, k, src, gain):
                dve.wait_ge(S(f"hi_{stage}"), k + 1)
                first = hi[:, k, :].bitcast(F32)
                if gain is None:
                    ins = v.tensor_tensor(lo[:, k, :], src, first, ALU.subtract)
                else:
                    ins = v.scalar_tensor_tensor(lo[:, k, :], src, gain[:, k:k + 1], first, ALU.mult, ALU.subtract)
                chain(ins, S(f"ready_{stage}"))

            def add_squares(n, m, total=None, made="sq_made", added="sum_added"):
                total = ssum if total is None else total
                dve.wait_ge(S(made), n + 1)
                if m == 0:
                    chain(v.tensor_copy(total[:, :], sq[:, n % 2, :]), S(added))
                else:
                    chain(v.tensor_tensor(total[:, :], total[:, :], sq[:, n % 2, :], ALU.add), S(added))

            freed = side_freed["dve"]
            chain(v.memset(eps_t[:, :], EPS), S("eps_set"))
            chain(v.memset(ones[:, :], 1.0), S("ones_set"))
            dve.wait_ge(S("x_in"), 16 * (NT + 1))
            dve.wait_ge(S("small_in"), 16 * N_SMALL)
            chain(v.tensor_tensor(g_fin1, g_fin, g_n1, ALU.mult), S("gain_set"))
            for k in range(NK + 1):
                if k < NK:
                    wait_job(dve, ("x_t", k))
                    chain(v.tensor_copy(xT[:, k, :], side_of(("x_t", k))[:, :]), freed)
                if k >= 1:
                    second("in", actA_hi, actA_lo, k - 1, xT[:, k - 1, :], g_attn)
                    add_squares(k - 1, k - 1)
            refine(side_of("sum0")[:, :], freed=freed)
            chain(v.tensor_tensor(const("cos"), const("cos"), rs[:, :], ALU.mult))
            chain(v.tensor_tensor(const("sin"), const("sin"), rs[:, :], ALU.mult))

            def take(c, dst, by=None):
                dve.wait_ge(chunk_done, c + 1)
                chain(v.tensor_tensor(dst, out_bank(c)[0:dst.shape[0], :], (rs[:, :] if by is None else by)[0:dst.shape[0], :],
                                      ALU.mult), chunk_freed)

            def rope(c, *dst):
                r = ROPED.index(c)
                dve.wait_ge(S("rot_made"), r + 1)
                chain(v.tensor_tensor(rt1[:, :], out_bank(c)[:, :], const("cos"), ALU.mult), chunk_freed)
                chain(v.tensor_tensor(rot[:, r % 2, :], rot[:, r % 2, :], const("sin"), ALU.mult))
                for n, (rows, out_rows, to) in enumerate(dst):
                    chain(v.tensor_tensor(to[out_rows, :], rt1[rows, :], rot[rows, r % 2, :], ALU.add),
                          S("roped") if n == len(dst) - 1 else None)

            ALL, LOW, HIGH = slice(0, P), slice(0, HD), slice(HD, P)

            def rope_keys(c, to):
                rope(c, (LOW, LOW, to[:, 0, :]), (LOW, HIGH, to[:, 0, :]),
                     (HIGH, HIGH, to[:, 1, :]), (HIGH, LOW, to[:, 1, :]))

            take(C_IN, ik_s[:, :])
            for c in range(1, 5):
                rope(c, (ALL, ALL, iqT[:, c - 1, :]))
            wait_job(dve, "ik_tok")
            by_tok = side_of("ik_tok")[:, :].rearrange("p (t f) -> p t f", f=P)
            chain(v.tensor_scalar(iw[:, :, :], by_tok[:, :, HD:HD + HEADS], W_SCALE, None, ALU.mult))
            for t in range(NT):
                chain(v.bn_stats(ikstat[:, t, :], by_tok[:, t, 0:HD]))
                chain(v.bn_aggr(ikmv[:, t, :], ikstat[:, t, :]), S("ik_var") if t == NT - 1 else None)
            for t in range(NT):
                chain(v.tensor_scalar(ikn[:, t, :], by_tok[:, t, 0:HD], ikmv[:, t, 0:1], None, ALU.subtract),
                      freed if t == NT - 1 else None)
            for c in range(5, 7):
                rope(c, (ALL, ALL, aqT[:, c - 5, :]))
            refine(ikmv[:, :, 1], ikr[:, 1, :], 1, ikr[:, 2, :], ikr[:, 3, :])
            for t in range(NT):
                chain(v.tensor_scalar(ikn[:, t, :], ikn[:, t, :], ikr[:, 1, t:t + 1], None, ALU.mult))
            for n, op in ((0, ALU.mult), (1, ALU.add)):
                chain(v.tensor_tensor(ikn[:, :, :], ikn[:, :, :],
                                      lnwb[:, n, :].unsqueeze(1).broadcast_to([P, NT, HD]), op))
            cos_t, sin_t = (const(n).rearrange("p (t f) -> p t f", f=32) for n in ("cos_tok", "sin_tok"))
            tmp = [ikt[:, n, :].rearrange("p (t f) -> p t f", f=32) for n in range(4)]
            x1, x2 = ikn[:, :, 0:32], ikn[:, :, 32:64]
            for n, (x, cs_) in enumerate(((x1, cos_t), (x2, sin_t), (x2, cos_t), (x1, sin_t))):
                chain(v.tensor_tensor(tmp[n], x, cs_, ALU.mult))
            for half in range(2):
                o = ikrope[:, :, half * HD:(half + 1) * HD]
                chain(v.tensor_tensor(o[:, :, 0:32], tmp[0], tmp[1], ALU.subtract))
                chain(v.tensor_tensor(o[:, :, 32:64], tmp[2], tmp[3], ALU.add), S("ik_roped"))
            for c in range(7, 9):
                rope(c, (ALL, ALL, aqT[:, c - 5, :]))
            rope_keys(9, akT)
            take(10, vT[:, 0, :])
            rope_keys(11, bkT)
            take(12, vT[:, 1, :])
            for c in range(13, 17):
                rope(c, (ALL, ALL, bqT[:, c - 13, :]))
            n = 0
            for qt in range(1, NT):
                w = (qt + 1) * P
                s = score[:, qt - 1, 0:w]
                for h in range(HEADS):
                    wait_freed(dve, ("index", qt, h))
                    r = rel[:, n % 4, 0:w]
                    if h == 0:
                        ins = v.tensor_scalar(s, r, iw[:, qt, h:h + 1], None, ALU.mult)
                    else:
                        ins = v.scalar_tensor_tensor(s, r, iw[:, qt, h:h + 1], s, ALU.mult, ALU.add)
                    chain(ins, S("index_added"))
                    n += 1
                own = score[:, qt - 1, qt * P:w]
                chain(v.tensor_tensor(own, own, const("causal"), ALU.add))
            for c in range(17, 33):
                take(c, sg[:, (c - 17) // NK, (c - 17) % NK, :])
                for qt in range(1, NT):
                    s = score[:, qt - 1, 0:(qt + 1) * P]
                    chain(v.max(top8[:, qt - 1, :], s))
                    chain(v.match_replace(s, top8[:, qt - 1, :], s, TAKEN))
            for qt in range(1, NT):
                w = (qt + 1) * P
                chain(v.tensor_scalar(keep[:, KEEP_AT[qt]:KEEP_AT[qt] + w], score[:, qt - 1, 0:w],
                                      TAKEN * 0.98, NEG, ALU.is_gt, ALU.mult))

            b0 = CONST_COLS["before"][0]
            for s in range(STEPS):
                if s % 8 == 0 and 8 <= s <= 8 * NT:
                    g = s // 8 - 1
                    chain(v.tensor_tensor(es[:, g, :], sinkb[:, :], nm[:, g, :], ALU.add), S("sinks_shifted"))
                if s % 8 == 7 and s >= 15:
                    g = s // 8 - 1
                    b, qt = unit(g * HEADS)[:2]
                    k = 4 if b == "b" else 0
                    cols = slice(qt * P, (qt + 1) * P)
                    dve.wait_ge(S("hi_branch"), g + 1)
                    chain(v.tensor_tensor(actB_lo[:, k:k + 4, cols],
                                          side_of(("out_t", g))[:, :].rearrange("p (f q) -> p f q", q=P),
                                          actB_hi[:, k:k + 4, cols].bitcast(F32), ALU.subtract), freed)
                if s < UNITS:
                    b, qt, k0, nk, h = unit(s)
                    g = s // HEADS
                    wait_job(dve, ("logits", s))
                    if s >= 3:
                        wait_job(dve, ("probs_t", s - 3))
                    if qt == 0:
                        bias = const("causal")
                    elif b == "b":
                        bias = con[:, b0:b0 + 2 * P]
                    else:
                        bias = keep[:, KEEP_AT[qt]:KEEP_AT[qt] + nk * P]
                    chain(v.tensor_tensor_reduce(
                        out=pbuf[:, s % 3, 0:nk * P], in0=side_of(("logits", s))[:, 0:nk * P], in1=bias,
                        scale=ATT_SCALE, scalar=-3.0e38, op0=ALU.add, op1=ALU.max,
                        accum_out=mx[:, g, h:h + 1]), freed)
                    if b == "b":
                        ins = v.tensor_scalar(nm[:, g, h:h + 1], mx[:, g, h:h + 1], sinkb[:, h:h + 1], -1.0,
                                              ALU.max, ALU.mult)
                    else:
                        ins = v.tensor_scalar(nm[:, g, h:h + 1], mx[:, g, h:h + 1], -1.0, None, ALU.mult)
                    chain(ins, S("logits_made"))
                if s % 8 == 3 and s >= 11:
                    g = s // 8 - 1
                    dve.wait_ge(S("probs_made"), (g + 1) * HEADS)
                    if g < NT:
                        dve.wait_ge(S("sinks_exp"), g + 1)
                        chain(v.tensor_tensor(den[:, g, :], den[:, g, :], es[:, g, :], ALU.add))
                    chain(v.reciprocal(mx[:, g, :], den[:, g, :]))
                    dve.wait_ge(S("values_done"), (g + 1) * HEADS)
                    if g >= 2:
                        wait_job(dve, ("out_t", g - 2))
                    chain(v.tensor_tensor(o_n[:, g % 2, :].rearrange("p (h d) -> p h d", d=HD),
                                          bank[g % RING][:, :].rearrange("p (h d) -> p h d", d=HD),
                                          mx[:, g, :].unsqueeze(2).broadcast_to([P, HEADS, HD]), ALU.mult),
                          S("outs_made"))

            def mix(first, stage, gates, hi, lo, gates_before):
                for m in range(NK + 1):
                    if m < NK:
                        c = first + m
                        dve.wait_ge(chunk_done, c + 1)
                        dve.wait_ge(S("gate_made"), gates_before + 2 * NK)
                        if m >= 2:
                            dve.wait_ge(S(f"hi_{stage}"), m - 1)
                        chain(v.tensor_tensor(mixb[:, m % 2, :], out_bank(c)[:, :], gates[:, 0, m, :], ALU.mult))
                        chain(v.tensor_tensor(mixt[:, m % 2, :], side[c % 4][:, :], gates[:, 1, m, :], ALU.mult), chunk_freed)
                        chain(v.tensor_tensor(mixb[:, m % 2, :], mixb[:, m % 2, :], mixt[:, m % 2, :], ALU.add),
                              S(f"mixed_{stage}"))
                    if m >= 1:
                        second(stage, hi, lo, m - 1, mixb[:, (m - 1) % 2, :], None)

            mix(C_BR, "out", sg, actA_hi, actA_lo, 0)
            for m in range(NK + 1):
                if m < NK:
                    dve.wait_ge(chunk_done, C_OUT + m + 1)
                    chain(v.tensor_tensor(xT[:, m, :], xT[:, m, :], out_bank(C_OUT + m)[:, :], ALU.add), chunk_freed)
                if m >= 1:
                    second("mlp", actB_hi, actB_lo, m - 1, xT[:, m - 1, :], g_mlp)
                    add_squares(NK + m - 1, m - 1)
            for q in range(QUARTERS):
                up = C_MLP + 2 * NK * q
                for m in range(NK + 1):
                    if m < NK:
                        dve.wait_ge(chunk_done, up + m + 1)
                        if NK * q + m >= 2:
                            dve.wait_ge(S("u_made"), NK * q + m - 1)
                        chain(v.tensor_scalar(relu_u[:, m % 2, :], out_bank(up + m)[:, :], 0.0, None, ALU.max), chunk_freed)
                    if m >= 1:
                        second(f"u{q}", actA_hi, actA_lo, m - 1, u_sq[:, (m - 1) % 2, :], None)
                if q == 0:
                    refine(side_of("sum1")[:, :], freed=freed)
                    chain(v.tensor_tensor(rs[:, :], rs[:, :], rs[:, :], ALU.mult))
                for m in range(NK + 1):
                    c = up + NK + m
                    if m < NK:
                        dve.wait_ge(chunk_done, c + 1)
                        chain(v.tensor_tensor(ytmp[:, :], out_bank(c)[:, :], rs[:, :], ALU.mult), chunk_freed)
                        chain(v.tensor_tensor(xT[:, m, :], xT[:, m, :], ytmp[:, :], ALU.add),
                              S("x1_made") if q == QUARTERS - 1 else None)
                    if m >= 1 and q == QUARTERS - 1:
                        second("in2", actB_hi, actB_lo, m - 1, xT[:, m - 1, :], g_fin1)
                        add_squares(2 * NK + 2 * (m - 1), m - 1)
                        add_squares(2 * NK + 2 * (m - 1) + 1, m - 1, ssum2)
            refine(side_of("sum2")[:, :], rsf[:, :], freed=freed)
            wait_job(dve, "sum3")
            chain(v.tensor_tensor(ssum2[:, :], side_of("sum3")[:, :], rsf[:, :], ALU.mult), freed)
            chain(v.tensor_tensor(ssum2[:, :], ssum2[:, :], rsf[:, :], ALU.mult), S("second_sum"))
            refine(ssum2[:, :])
            chain(v.tensor_tensor(rs[:, :], rs[:, :], rsf[:, :], ALU.mult))

            take(C_IN2, alow[:, :])
            chain(v.memset(go[:, :], 1.0))
            chain(v.memset(go[:, :].rearrange("p (c t) -> p c t", t=CHUNK)[:, :, 0:1], 0.0), S("alow_made"))
            for j in range(2):
                take(C_IN2 + 1 + j, qs[:, j, :])
            for j in range(2):
                take(C_IN2 + 3 + j, ks[:, j, :])
            for j in range(2):
                wait_job(dve, ("z", j))
                chain(v.tensor_scalar(zs[:, j, :], side_of(("z", j))[:, :], b_alpha[:, j:j + 1], None, ALU.add), freed)
            for m in range(NK):
                chain(v.scalar_tensor_tensor(xT[:, m, :], xT[:, m, :], g_fin[:, m:m + 1], rsf[:, :], ALU.mult, ALU.mult))
            for h in range(GH):
                take(C_IN2 + 5 + h, gvT[:, h, :])
            by_chunk = lambda t: t.rearrange("p (c t) -> p c t", t=CHUNK)
            for j in range(2):
                dve.wait_ge(S("log_made"), j + 1)
                chain(v.scalar_tensor_tensor(zs[:, j, :], zs[:, j, :], 0.0, az[:, j, :], ALU.min, ALU.subtract))
                chain(v.tensor_tensor_scan(cs[:, j, :], go[:, :], zs[:, j, :], 0.0, ALU.mult, ALU.add), S("decay_summed"))
            for j in range(2):
                dve.wait_ge(S("decays"), 2 * (j + 1))
                chain(v.tensor_copy(dec[:, j, :], by_chunk(az[:, j, :])[:, :, CHUNK - 1]))
                chain(v.scalar_tensor_tensor(qdec[:, j, :], qs[:, j, :], CHUNK ** -0.5, az[:, j, :], ALU.mult, ALU.mult))
                chain(v.tensor_tensor(kdec[:, j, :], ks[:, j, :], zs[:, j, :], ALU.mult))
                last = by_chunk(cs[:, j, :])[:, :, CHUNK - 1:CHUNK]
                chain(v.tensor_copy(top8[:, 0, :], last.rearrange("p c t -> p (c t)")))
                chain(v.tensor_tensor(by_chunk(cs[:, j, :]), top8[:, 0, :].unsqueeze(2).broadcast_to([P, NCH, CHUNK]),
                                      by_chunk(cs[:, j, :]), ALU.subtract), S("decay_left"))
            for j in range(2):
                dve.wait_ge(S("decays"), 5 + j)
                chain(v.tensor_tensor(kend[:, j, :], ks[:, j, :], cs[:, j, :], ALU.mult), S("kend_made"))
            for h in range(GH):
                take(C_IN2 + 9 + h, rsil[:, h, :])
                dve.wait_ge(S("r_sigmoid"), h + 1)
                chain(v.tensor_tensor(rsil[:, h, :], rsil[:, h, :], pool_t[:, h % 2, :], ALU.mult), S("r_silu"))
            inv = const("inv_count")
            for g, win in enumerate(WINDOWS):
                take(C_IN2 + 13 + g, diff[:, g, :])
                src, step, n = diff[:, g, :], 1, 0
                while step < win:
                    dst = pool_t[:, n % 2, :]
                    chain(v.tensor_copy(dst[:, 0:step], src[:, 0:step]))
                    chain(v.tensor_tensor(dst[:, step:], src[:, step:], src[:, 0:L - step], ALU.add))
                    src, step, n = dst, 2 * step, n + 1
                chain(v.tensor_tensor(src[:, 0:16], src[:, 0:16], inv[:, 16 * g:16 * g + 16], ALU.mult))
                chain(v.tensor_scalar(src[:, 16:], src[:, 16:], 1.0 / win, None, ALU.mult))
                chain(v.tensor_tensor(diff[:, g, :], src, diff[:, g, :], ALU.subtract), S("diff_made"))
            for n in range(NCH - 1):
                wait_job(dve, ("inc", n))
                for j in range(2):
                    for e in range(2):
                        rows = slice(HD * e, HD * (e + 1))
                        inc = side_of(("inc", n))[rows, 256 * j + DV * e:256 * j + DV * (e + 1)]
                        done = freed if (j, e) == (1, 1) else None
                        if n == 0:
                            chain(v.tensor_copy(gst[rows, j, 1, :], inc), done)
                        else:
                            chain(v.scalar_tensor_tensor(gst[rows, j, n + 1, :], gst[rows, j, n, :],
                                                         dec[rows, j, n:n + 1], inc, ALU.mult, ALU.add), done)
            for h in range(GH):
                wait_job(dve, ("scores", h))
                chain(v.tensor_tensor(scT[:, h, :].rearrange("p (j t) -> p j t", t=P),
                                      side_of(("scores", h))[:, :].rearrange("p (j t) -> p j t", t=P),
                                      const("pair_causal").unsqueeze(1).broadcast_to([P, NT, P]), ALU.mult), freed)

            def gate(c):
                j = c - C_IN2 - 17
                take(c, sg2[:, j // NK, j % NK, :])

            for c in range(C_IN2 + 17, C_IN2 + 21):
                gate(c)
            for h in range(GH):
                wait_job(dve, ("o", h))
                dve.wait_ge(S("o_squares"), h + 1)
                if h:
                    dve.wait_ge(S("ready_branch2"), h)
                chain(v.tensor_copy(o_s[:, :], side_of(("o", h))[:, :]), freed)
                refine(side_of(("o_sum", h))[:, :], rs_o[:, :], DV, freed=freed)
                chain(v.scalar_tensor_tensor(o_s[:, :], o_s[:, :], g_gla[:, h:h + 1], rs_o[:, :], ALU.mult, ALU.mult),
                      S("o_sum_taken"))
                chain(v.tensor_tensor(o_s[:, :], o_s[:, :], rsil[:, h, :], ALU.mult), S("o_normed"))
                second("branch2", actA_hi, actA_lo, h, o_s[:, :], None)
            for c in range(C_IN2 + 21, C_IN2 + 25):
                gate(c)
            for g in range(4):
                wait_job(dve, ("pool", g))
                if g >= 2:
                    dve.wait_ge(S("ready_branch2"), 4 + g - 1)
                chain(v.tensor_scalar(pool_t2[:, g % 2, :], side_of(("pool", g))[:, :], p_scale[:, g:g + 1], None, ALU.mult), freed)
                second("branch2", actA_hi, actA_lo, 4 + g, pool_t2[:, g % 2, :], None)
            for c in range(C_IN2 + 25, C_IN2 + 33):
                gate(c)
            mix(C_BR2, "out2", sg2, actB_hi, actB_lo, 2 * NK)
            for m in range(NK + 1):
                if m < NK:
                    dve.wait_ge(chunk_done, C_OUT2 + m + 1)
                    chain(v.tensor_tensor(xT[:, m, :], xT[:, m, :], out_bank(C_OUT2 + m)[:, :], ALU.add), chunk_freed)
                if m >= 1:
                    add_squares(m - 1, m - 1, None, "sq4_made", "sum4_added")

            chain(v.memset(tabi[:, :, :], SKIP), S("dense_over"))
            for k in range(2):
                chain(v.tensor_scalar(gw[:, k, :], const("token"), float(L * k), None, ALU.add))
                chain(v.tensor_copy(tabi[:, 2, NT * k:NT * (k + 1)], gw[:, k, :]), S("table_ready"))
            refine(side_of("sum4")[:, :], freed=freed)
            for m in range(NK):
                chain(v.scalar_tensor_tensor(h2T[:, m, :], xT[:, m, :], g_n2[:, m:m + 1], rs[:, :], ALU.mult, ALU.mult),
                      S("h2_made"))
            dve.wait_ge(S("route_in"), 16 * (NG + 4))
            wait_job(dve, "route")
            chain(v.tensor_tensor(lg[:, :, :], side_of("route")[:, 0:NT * (NG + NE)].rearrange("p (t e) -> p t e", t=NT),
                                  brt[:, :].unsqueeze(1).broadcast_to([P, NT, NG + NE]), ALU.add), freed)

            def tile3(n, w):
                return rt[:, n, 0:NT * w].rearrange("p (t w) -> p t w", w=w)

            def spread(t, w):
                return t.unsqueeze(2).broadcast_to([P, NT, w])

            def first_largest(x, w, peak, down, to):
                chain(v.tensor_reduce(gw[:, peak, :], x, AX, ALU.max))
                chain(v.tensor_tensor(to, x, spread(gw[:, peak, :], w), ALU.is_equal))
                chain(v.tensor_tensor(to, to, down.unsqueeze(1).broadcast_to([P, NT, w]), ALU.mult))
                chain(v.tensor_reduce(gw[:, 15, :], to, AX, ALU.max))
                chain(v.tensor_tensor(to, to, spread(gw[:, 15, :], w), ALU.is_equal))

            group = tile3(2, NG)
            first_largest(lg[:, :, 0:NG], NG, 0, const("down4"), group)
            chain(v.tensor_tensor(tile3(0, NG), lg[:, :, 0:NG], spread(gw[:, 0, :], NG), ALU.subtract), S("group_shifted"))
            own = rt[:, 3, :].rearrange("p (t e g) -> p t e g", t=NT, g=NG)
            chain(v.tensor_tensor(own, lg[:, :, NG:].rearrange("p t (g e) -> p t e g", e=EPG),
                                  group.unsqueeze(2).broadcast_to([P, NT, EPG, NG]), ALU.mult))
            logit = tile3(4, EPG)
            chain(v.tensor_reduce(logit, own, AX, ALU.add))
            one, two = tile3(5, EPG), tile3(7, EPG)
            first_largest(logit, EPG, 4, const("down8"), one)
            chain(v.scalar_tensor_tensor(tile3(6, EPG), one, -1.0e38, logit, ALU.mult, ALU.add))
            first_largest(tile3(6, EPG), EPG, 5, const("down8"), two)
            chain(v.tensor_tensor(gw[:, 6, :], gw[:, 5, :], gw[:, 4, :], ALU.subtract), S("expert_shifted"))
            M = [rt[:, 8 + k, :].rearrange("p (t g e) -> p t g e", t=NT, g=NG) for k in range(2)]
            for k, pick in enumerate((one, two)):
                chain(v.tensor_tensor(M[k], group.unsqueeze(3).broadcast_to([P, NT, NG, EPG]),
                                      pick.unsqueeze(2).broadcast_to([P, NT, NG, EPG]), ALU.mult))
            dve.wait_ge(S("group_exp"), 1)
            chain(v.tensor_reduce(gw[:, 1, :], tile3(0, NG), AX, ALU.add))
            chain(v.tensor_tensor(rt[:, 1, :], rt[:, 8, :], rt[:, 9, :], ALU.add), S("picks_made"))
            chain(v.reciprocal(gw[:, 2, :], gw[:, 1, :]))
            dve.wait_ge(S("expert_exp"), 1)
            chain(v.tensor_scalar(gw[:, 7, :], gw[:, 6, :], 1.0, None, ALU.add))
            chain(v.reciprocal(gw[:, 8, :], gw[:, 7, :]))
            chain(v.tensor_tensor(gw[:, 10, :], gw[:, 2, :], gw[:, 8, :], ALU.mult))
            chain(v.tensor_tensor(gw[:, 11, :], gw[:, 10, :], gw[:, 6, :], ALU.mult))
            wait_job(dve, "places")
            pos, q_, t1, sl = (rt[:, n, :] for n in (0, 2, 3, 4))
            cnt, o_e, o_in, o_at = (rt[:, 5, NE * n:NE * (n + 1)] for n in range(4))
            chain(v.tensor_copy(cnt, side_of("places")[:, NT * NE:NT * NE + NE]))
            chain(v.tensor_copy(pos, side_of("places")[:, 0:NT * NE]), freed)

            def blocks_past(to, x, least):
                chain(v.tensor_scalar(to, x, float(P + least), None, ALU.is_ge))
                for n in (2, 3):
                    chain(v.scalar_tensor_tensor(to, x, float(n * P + least), to, ALU.is_ge, ALU.add))

            blocks_past(q_, pos, 0)
            blocks_past(o_e, cnt, 1)
            chain(v.tensor_tensor_scan(o_in, ones[:, 0:NE], o_e, 0.0, ALU.mult, ALU.add))
            chain(v.tensor_tensor(o_at, o_in, o_e, ALU.subtract))
            chain(v.tensor_tensor(o_at, o_at, const("iota_e"), ALU.subtract))
            chain(v.tensor_scalar(o_at, o_at, float(NE - 1), None, ALU.add))
            by_e = lambda t: t.rearrange("p (t e) -> p t e", e=NE)
            over_e = lambda t: t.unsqueeze(1).broadcast_to([P, NT, NE])
            chain(v.tensor_tensor(by_e(t1), by_e(q_), over_e(o_at), ALU.add))
            chain(v.scalar_tensor_tensor(t1, q_, 1.0, t1, ALU.min, ALU.mult))
            chain(v.tensor_tensor(by_e(t1), by_e(t1), over_e(const("iota_e")), ALU.add))
            chain(v.scalar_tensor_tensor(sl, q_, -float(P), pos, ALU.mult, ALU.add))
            chain(v.scalar_tensor_tensor(sl, sl, float(NB), t1, ALU.mult, ALU.add))
            for k in range(2):
                chain(v.tensor_tensor(t1, sl, rt[:, 8 + k, :], ALU.mult))
                chain(v.tensor_reduce(gw[:, 3, :], by_e(t1), AX, ALU.add))
                chain(v.tensor_copy(slot_of[:, k, :], gw[:, 3, :]), S("slots_made"))
            below = rt[0:1, 6, :].rearrange("p (j e) -> p j e", e=NE)
            for part in range(2):
                w = OVER // 2
                chain(v.tensor_tensor(below[:, 0:w, :], o_in[0:1, :].unsqueeze(1).broadcast_to([1, w, NE]),
                                      const("iota_e", 1)[:, part * w:(part + 1) * w].unsqueeze(2).broadcast_to([1, w, NE]),
                                      ALU.is_le))
                chain(v.tensor_reduce(rt[0:1, 7, part * w:(part + 1) * w], below[:, 0:w, :], AX, ALU.add))
            chain(v.tensor_scalar(rt[0:1, 7, 0:OVER], rt[0:1, 7, 0:OVER], float(NE - 1), None, ALU.min))
            chain(v.tensor_copy(over_n[0:1, 1:1 + OVER], rt[0:1, 7, 0:OVER]))
            chain(v.tensor_copy(over_n[0:1, 0:1], o_in[0:1, NE - 1:NE]), S("over_ready"))
            dve.wait_ge(S("table_back"), 16)
            chain(v.tensor_copy(rt[:, 2, 0:NB], tabi[:, 0, 0:NB]))
            chain(v.tensor_scalar(rt[:, 3, 0:NB], rt[:, 2, 0:NB], float(L), -float(L), ALU.is_ge, ALU.mult))
            chain(v.tensor_tensor(rt[:, 3, 0:NB], rt[:, 3, 0:NB], rt[:, 2, 0:NB], ALU.add))
            chain(v.tensor_copy(tabi[:, 1, 0:NB], rt[:, 3, 0:NB]), S("rows_ready"))

            def x_turned(i, u):
                dve.wait_ge(S("xe_used"), at(i, u, 2))
                wait_from(dve, S("gate_up_done"), i, u, 0)
                v.tensor_copy(xeT[:, (u + 1) % 2, L:], side[1][:, :]).then_inc(S("xe_t_by_dve"), 1)

            def expert(i, u):
                dve.wait_ge(S("silu_made"), at(i, u, 1))
                v.tensor_tensor(hid[:, u % 2, :], hid[:, u % 2, :], bank[u % 2][:, DE:], ALU.mult)\
                    .then_inc(S("hid_made"), 1)
                x_turned(i, u)
                dve.wait_ge(S("hid_turned"), at(i, u, 1))
                wait_from(dve, S("down_done"), i, u, -1)
                v.tensor_copy(hidT[:, u % 2, :], side[2][:, 0:DE]).then_inc(S("hid_t_made"), 1)
                dve.wait_ge(S("down_done"), at(i, u, 1))
                if i is not None or u >= 2:
                    dve.wait_ge(S(f"scattered{u % 2}"), 16 * (u // 2) if i is None else 32 * i + 16 * (u // 2))
                v.tensor_copy(ye[:, u % 2, L:], bank[3][:, :]).then_inc(S("y_by_dve"), 1)

            dve.wait_ge(S("xe_used"), 1)
            v.tensor_copy(xeT[:, 0, L:], side[1][:, :]).then_inc(S("xe_t_by_dve"), 1)
            for_experts(dve, expert)

            dve.wait_ge(S("experts_over"), 1)
            for i in range(NT):
                dve.wait_ge(S(f"y2_in{i % 2}"), 16 * (i // 2 + 1))
                dve.wait_ge(S("x_back"), i + 1)
                t = ye[:, i % 2, :]
                if i >= 2:
                    dve.wait_ge(S(f"stored{i % 2}"), 16 * (i // 2))
                for n in range(2):
                    chain(v.scalar_tensor_tensor(t[:, n * L:(n + 1) * L], y2[:, i % 2, n * L:(n + 1) * L],
                                                 gw[:, 10, i:i + 1], bank[2 * (i % 2) + n][:, :], ALU.mult, ALU.add),
                          S("x_taken") if n else None)
                chain(v.scalar_tensor_tensor(t, y2[:, i % 2, D:], gw[:, 11, i:i + 1], t, ALU.mult, ALU.add), S("final_sum"))
                refine(gw[:, 12, i:i + 1], gw[:, 13, i:i + 1], D, gw[:, 14, i:i + 1], gw[:, 15, i:i + 1])
                chain(v.scalar_tensor_tensor(t, t, gw[:, 13, i:i + 1], gfin[:, :], ALU.mult, ALU.mult), S("final_out"))

        @block.tensor
        def _(pe):
            mm = nc.tensor.matmul

            def open_job(name):
                i = jobs.at[name]
                if i >= 4:
                    pe.wait_ge(side_freed[jobs.freer[i - 4]], jobs.freed[i - 4])
                return side[i % 4]

            def close_job(ins):
                ins.then_inc(side_full, 1)

            def chunk(slot, done, hi, lo, ready, counts, two, free):
                pe.wait_ge(lo_made, done)
                if free is not None:
                    pe.wait_ge(chunk_freed, free)
                for k in range(NK):
                    pe.wait_ge(ready, counts[k])
                    b = side[slot] if two and k >= 4 else bank[slot]
                    w_hi, w_lo = (w[:, slot, k * P:(k + 1) * P] for w in (whi, wlo))
                    first, last = k in ((0, 4) if two else (0,)), k in ((3, 7) if two else (7,))
                    mm(b[:, :], w_hi, hi[:, k, :], start=first, stop=False)
                    mm(b[:, :], w_hi, lo[:, k, :], start=False, stop=False)
                    ins = mm(b[:, :], w_lo, hi[:, k, :], start=False, stop=last)
                ins.then_inc(chunk_done, 1)

            def chunks(first, n, hi, lo, ready, counts=tuple(range(1, NK + 1)), two=False):
                if n % RING or first < RING:
                    for c in range(first, first + n):
                        chunk(c % RING, c + 1, hi, lo, ready, counts, two, c - RING + 1 if c >= RING else None)
                    return
                with pe.Fori(0, n // RING) as i:
                    for u in range(RING):
                        chunk((first + u) % RING, RING * i + (first + u + 1), hi, lo, ready, counts, two,
                              RING * i + (first + u - RING + 1))

            def turn(dst, src, last=False):
                return nc.tensor.transpose(dst, src, ident[0:src.shape[0], 0:src.shape[0]])

            def total(name, src, sem, count):
                pe.wait_ge(sem, count)
                close_job(mm(open_job(name)[:, :], ones[:, :], src, start=True, stop=True))

            pe.wait_ge(S("x_in"), 16 * (NT + 1))
            pe.wait_ge(S("ones_set"), 1)
            for k in range(NK):
                b = open_job(("x_t", k))
                for i in range(NT):
                    ins = turn(b[:, i * P:(i + 1) * P], x_tok[:, i, k * P:(k + 1) * P])
                close_job(ins)
            total("sum0", ssum[:, :], S("sum_added"), NK)

            inA = (actA_hi, actA_lo, S("ready_in"))
            chunks(C_IN, 1, *inA)
            chunks(1, 4, *inA)
            b = open_job("ik_tok")
            pe.wait_ge(chunk_freed, 1)
            for t in range(NT):
                ins = turn(b[:, t * P:(t + 1) * P], ik_s[:, t * P:(t + 1) * P])
            close_job(ins)
            chunks(5, 8, *inA)
            pe.wait_ge(chunk_freed, 13)
            for n, br in enumerate("ab"):
                b = open_job(("v_tok", br))
                for t in range(NT):
                    ins = turn(b[:, t * P:(t + 1) * P], vT[:, n, t * P:(t + 1) * P])
                close_job(ins)
            b = open_job("ik_t")
            pe.wait_ge(S("ik_roped"), 2)
            for t in range(NT):
                ins = turn(b[:, t * P:(t + 1) * P], ikrope[:, t, :])
            close_job(ins)
            chunks(13, 4, *inA)
            wait_freed(pe, "ik_t")
            pe.wait_ge(S("roped"), 4)
            for qt in range(1, NT):
                for h in range(HEADS):
                    rows = slice(HD * (h % 2), HD * (h % 2 + 1))
                    b = open_job(("index", qt, h))
                    close_job(mm(b[:, 0:(qt + 1) * P], iqT[rows, h // 2, qt * P:(qt + 1) * P],
                                 ikT[rows, 0:(qt + 1) * P], start=True, stop=True))
            chunks(17, 16, *inA)

            pe.wait_ge(S("roped"), len(ROPED))
            wait_freed(pe, ("v_tok", "b"))
            pe.wait_ge(chunk_freed, C_BR)
            for what, n in pe_attention():
                if what in ("logits", "probs_t", "values"):
                    br, qt, k0, nk, h = unit(n)
                    rows = slice(HD * (h % 2), HD * (h % 2 + 1))
                if what == "logits":
                    b = open_job((what, n))
                    close_job(mm(b[:, 0:nk * P], qT[br][rows, h // 2, qt * P:(qt + 1) * P],
                                 kT[br][rows, h // REP, k0 * P:(k0 + nk) * P], start=True, stop=True))
                elif what == "probs_t":
                    b = open_job((what, n))
                    pe.wait_ge(S("probs_made"), n + 1)
                    for j in range(nk):
                        ins = turn(b[:, j * P:(j + 1) * P], pbuf[:, n % 3, j * P:(j + 1) * P])
                    close_job(ins)
                elif what == "values":
                    g = n // HEADS
                    wait_freed(pe, ("probs_t", n))
                    if g >= RING and h == 0:
                        pe.wait_ge(S("outs_made"), g - RING + 1)
                    for j in range(nk):
                        ins = mm(bank[g % RING][:, h * HD:(h + 1) * HD], pT[:, n % 2, j * P:(j + 1) * P],
                                 v_tok[br][:, k0 + j, HD * (h // REP):HD * (h // REP + 1)],
                                 start=j == 0, stop=j == nk - 1)
                    ins.then_inc(S("values_done"), 1)
                else:
                    b = open_job((what, n))
                    pe.wait_ge(S("outs_made"), n + 1)
                    for f in range(4):
                        ins = turn(b[:, f * P:(f + 1) * P], o_n[:, n % 2, f * P:(f + 1) * P])
                    close_job(ins)

            wait_freed(pe, ("out_t", 2 * NT - 1))
            wait_freed(pe, ("probs_t", UNITS - 1))
            chunks(C_BR, NK, actB_hi, actB_lo, side_freed["dve"],
                   [jobs.freed[jobs.at[("out_t", 2 * NT - 1)]]] * NK, two=True)
            chunks(C_OUT, NK, actA_hi, actA_lo, S("ready_out"))
            for q in range(QUARTERS):
                chunks(C_MLP + 2 * NK * q, NK, actB_hi, actB_lo, S("ready_mlp"))
                if q == 0:
                    pe.wait_ge(chunk_freed, C_OUT)
                    total("sum1", ssum[:, :], S("sum_added"), 2 * NK)
                chunks(C_MLP + 2 * NK * q + NK, NK, actA_hi, actA_lo, S(f"ready_u{q}"))
            total("sum2", ssum[:, :], S("sum_added"), 4 * NK)
            total("sum3", ssum2[:, :], S("sum_added"), 4 * NK)

            inB = (actB_hi, actB_lo, S("ready_in2"))
            chunks(C_IN2, 1, *inB)
            chunks(C_IN2 + 1, 4, *inB)
            pe.wait_ge(S("small2_in"), 32)
            pe.wait_ge(S("alow_made"), 1)
            for j in range(2):
                b = open_job(("z", j))
                close_job(mm(b[:, :], wal[:, j * P:(j + 1) * P], alow[:, :], start=True, stop=True))
            chunks(C_IN2 + 5, 4, *inB)
            pe.wait_ge(chunk_freed, C_IN2 + 9)
            for h in range(GH):
                b = open_job(("gv_tok", h))
                for t in range(NT):
                    ins = turn(b[:, t * P:(t + 1) * P], gvT[:, h, t * P:(t + 1) * P])
                close_job(ins)
            chunks(C_IN2 + 9, 4, *inB)
            chunks(C_IN2 + 13, 4, *inB)
            pe.wait_ge(S("kend_made"), 2)
            for j in range(2):
                b = open_job(("kend_tok", j))
                for t in range(NT):
                    ins = turn(b[:, t * P:(t + 1) * P], kend[:, j, t * P:(t + 1) * P])
                close_job(ins)
            wait_freed(pe, ("kend_tok", 1))
            for n in range(NCH - 1):
                b = open_job(("inc", n))
                rows = slice(CHUNK * (n % 2), CHUNK * (n % 2 + 1))
                for j in range(2):
                    ins = mm(b[:, 256 * j:256 * (j + 1)], kend_tok[rows, n // 2, j * P:(j + 1) * P],
                             gv_tok[rows, n // 2, 256 * j:256 * (j + 1)], start=True, stop=True)
                close_job(ins)
            for h in range(GH):
                b = open_job(("scores", h))
                rows = slice(HD * (h % 2), HD * (h % 2 + 1))
                for t in range(NT):
                    cols = slice(t * P, (t + 1) * P)
                    ins = mm(b[:, cols], kdec[rows, h // 2, cols], qdec[rows, h // 2, cols], start=True, stop=True)
                close_job(ins)
            chunks(C_IN2 + 17, 4, *inB)
            wait_freed(pe, ("scores", GH - 1))
            for h in range(GH):
                b = open_job(("o", h))
                rows = slice(HD * (h % 2), HD * (h % 2 + 1))
                for t in range(NT):
                    cols = slice(t * P, (t + 1) * P)
                    mm(b[:, cols], gv_tok[:, t, h * DV:(h + 1) * DV], scT[:, h, cols], start=True, stop=False)
                    for n in range(2 * t, 2 * t + 2):
                        if n:
                            at_ = slice(n * CHUNK, (n + 1) * CHUNK)
                            ins = mm(b[:, at_], gst[rows, h // 2, n, :], qdec[rows, h // 2, at_], start=False, stop=n % 2 == 1)
                close_job(ins)
                total(("o_sum", h), sq[:, 0, :], S("o_squares"), h + 1)
            chunks(C_IN2 + 21, 4, *inB)
            pe.wait_ge(S("diff_made"), 4)
            for g in range(4):
                close_job(mm(open_job(("pool", g))[:, :], pw[:, g, :], diff[:, g, :], start=True, stop=True))
            chunks(C_IN2 + 25, 8, *inB)
            wait_freed(pe, ("pool", 3))
            chunks(C_BR2, NK, actA_hi, actA_lo, S("ready_branch2"), two=True)
            chunks(C_OUT2, NK, actB_hi, actB_lo, S("ready_out2"))

            total("sum4", ssum[:, :], S("sum4_added"), NK)
            pe.wait_ge(S("h2_made"), NK)
            pe.wait_ge(S("route_in"), 16 * (NG + 4))
            b = open_job("route")
            for i in range(NT):
                for k in range(NK):
                    ins = mm(b[:, i * (NG + NE):(i + 1) * (NG + NE)], h2T[:, k, i * P:(i + 1) * P], wr[:, k, :],
                             start=k == 0, stop=k == NK - 1)
            close_job(ins)
            for i in range(NT):
                for n in range(2):
                    b = open_job(("rows", i, n))
                    for k in range(4):
                        ins = turn(b[:, k * P:(k + 1) * P], h2T[:, 4 * n + k, i * P:(i + 1) * P])
                    close_job(ins)
            b = open_job("places")
            pe.wait_ge(S("picks_made"), 1)
            picks = rt[:, 1, :].rearrange("p (t e) -> p t e", e=NE)
            for i in range(NT):
                for j in range(i + 1):
                    mm(b[:, i * NE:(i + 1) * NE], const("earlier") if j == i else ones[:, :], picks[:, j, :],
                       start=j == 0, stop=j == i)
            for j in range(NT):
                ins = mm(b[:, NT * NE:NT * NE + NE], ones[:, :], picks[:, j, :], start=j == 0, stop=j == NT - 1)
            close_job(ins)
            wait_freed(pe, "places")
            wait_freed(pe, ("rows", NT - 1, 1))

            def turn_rows(i, u, gathered):
                j = (u + 1) % 2
                pe.wait_ge(S(f"gathered{j}"), gathered)
                if u >= 0:
                    pe.wait_ge(S("xe_t_by_act"), at(i, u, 1))
                    pe.wait_ge(S("xe_t_by_dve"), at(i, u, 1))
                for k in range(NK):
                    ins = turn(side[k // 4][:, (k % 4) * P:(k % 4 + 1) * P], xe[:, j, k * P:(k + 1) * P])
                ins.then_inc(S("xe_used"), 1)

            def expert(i, u):
                j = u % 2
                pe.wait_ge(S(f"expert_in{u}"), 48 if i is None else 48 * i + 48)
                pe.wait_ge(S("xe_t_by_act"), at(i, u, 1))
                pe.wait_ge(S("xe_t_by_dve"), at(i, u, 1))
                wait_from(pe, S("hid_made"), i, u, -1)
                for k in range(NK):
                    ins = mm(bank[j][:, :], xeT[:, j, k * P:(k + 1) * P], wring[:, u, k * 2 * DE:(k + 1) * 2 * DE],
                             start=k == 0, stop=k == NK - 1)
                ins.then_inc(S("gate_up_done"), 1)
                turn_rows(i, u, 16 * ((u + 1) // 2 + 1) if i is None else 32 * i + 16 * ((u + 1) // 2 + 1))
                pe.wait_ge(S("hid_made"), at(i, u, 1))
                wait_from(pe, S("hid_t_made"), i, u, 0)
                for k in range(2):
                    ins = turn(side[2][:, k * P:(k + 1) * P], hid[:, j, k * P:(k + 1) * P])
                ins.then_inc(S("hid_turned"), 1)
                pe.wait_ge(S("hid_t_made"), at(i, u, 1))
                wait_from(pe, S("y_by_act"), i, u, 0)
                wait_from(pe, S("y_by_dve"), i, u, 0)
                for n in range(2):
                    for k in range(2):
                        ins = mm(bank[2 + n][:, :], hidT[:, j, k * P:(k + 1) * P],
                                 wring[:, u, 4 * D + k * D + n * L:4 * D + k * D + (n + 1) * L],
                                 start=k == 0, stop=k == 1)
                ins.then_inc(S("down_done"), 1)

            turn_rows(None, -1, 16)
            for_experts(pe, expert)

            pe.wait_ge(S("experts_over"), 1)
            for i in range(NT):
                if i >= 2:
                    pe.wait_ge(S("x_taken"), i - 1)
                for k in range(NK):
                    ins = turn(bank[2 * (i % 2) + k // 4][:, (k % 4) * P:(k % 4 + 1) * P], xT[:, k, i * P:(i + 1) * P])
                ins.then_inc(S("x_back"), 1)


def kernel(**inputs):
    import numpy as _np
    import concourse.bacc as _bacc
    from concourse import mybir as _mybir
    from concourse.bass_utils import run_bass_kernel_spmd as _run

    f = _np.float32
    t, u = _np.arange(P)[:, None], _np.arange(P)[None, :]
    inv = (f(1.0) / (f(10000.0) ** (_np.arange(0, HD, 2, dtype=f) / f(HD)))).astype(f)
    angle = (_np.arange(L, dtype=f)[:, None] * inv[None, :]).astype(f)
    cos, sin = _np.cos(angle), _np.sin(angle)
    count = _np.concatenate([1.0 / _np.minimum(_np.arange(16) + 1.0, w) for w in WINDOWS])
    rows = lambda a: _np.broadcast_to(a, (P, a.shape[-1]))
    parts = {
        "ident": t == u, "causal": _np.where(u <= t, 0.0, NEG), "before": _np.where(u > t, 0.0, NEG),
        "earlier": t < u, "pair_causal": (t <= u) & (t // CHUNK == u // CHUNK),
        "cos": _np.tile(cos.T, (4, 1)), "sin": _np.tile(sin.T, (4, 1)),
        "cos_tok": cos.reshape(NT, P, 32).transpose(1, 0, 2).reshape(P, -1),
        "sin_tok": sin.reshape(NT, P, 32).transpose(1, 0, 2).reshape(P, -1),
        "inv_count": rows(count[None]), "iota_e": rows(_np.arange(NE)[None]),
        "down4": rows(_np.arange(NG, 0, -1)[None]), "down8": rows(_np.arange(EPG, 0, -1)[None]),
        "token": _np.arange(L).reshape(NT, P).T,
    }
    consts = _np.concatenate([parts[n].astype(f) for n in CONST_COLS], axis=1)

    nc = _bacc.Bacc("TRN2", target_bir_lowering=False, num_devices=1)
    arrays, args = {}, {}
    for name, a in (*inputs.items(), ("consts", consts)):
        a = _np.ascontiguousarray(a)
        arrays[f"in_{name}"] = a
        args[name] = nc.dram_tensor(f"in_{name}", a.shape, _mybir.dt.from_np(a.dtype), kind="ExternalInput").ap()
    out = nc.dram_tensor("out", (L, D), _mybir.dt.float32, kind="ExternalOutput").ap()
    gated_blocks(nc, args, out)
    r = _run(nc, [arrays], core_ids=[0])
    return r.results[0]["out"].reshape(1, L, D)
```

```python
from contextlib import ExitStack

import concourse.bass as bass
from concourse import mybir

F32 = mybir.dt.float32
F32R = mybir.dt.float32r
I32 = mybir.dt.int32
ALU = mybir.AluOpType
ACT = mybir.ActivationFunctionType
AX = mybir.AxisListType.X

P = 128
L = 512
D = 1024
NT, NK = L // P, D // P
HD, HEADS, REP = 64, 8, 4
TOPK = 128
FF = 4 * D
QUARTERS = FF // D
DV, GH, CHUNK = 128, 4, 64
NCH = L // CHUNK
WINDOWS = (2, 4, 8, 16)
NG, EPG, NE, DE = 4, 8, 32, 256
OVER = 8
NB = NE + OVER
SKIP = 1 << 20
EPS = 1e-6
NEG = -1e30
MASKED, TAKEN = -3.0e38, -3.3e38
ATT_SCALE = HD ** -0.5
W_SCALE = HEADS ** -0.5 * HD ** -0.5

CONST_COLS = {}
_at = 0
for _name, _n in (("ident", P), ("before", P), ("causal", P), ("earlier", P), ("pair_causal", P),
                  ("cos", L), ("sin", L), ("cos_tok", NT * 32), ("sin_tok", NT * 32),
                  ("inv_count", 4 * 16), ("iota", P), ("down4", NG), ("down8", EPG), ("row_id", 2 * NT)):
    CONST_COLS[_name] = (_at, _at + _n)
    _at += _n
CONST_WIDTH = _at

RING = 4
AHEAD = 3
C_IN, C_BR, C_OUT, C_MLP = 0, 33, 41, 49
C_IN2 = C_MLP + QUARTERS * 2 * NK
C_BR2, C_OUT2 = C_IN2 + 33, C_IN2 + 41
N_CHUNKS = C_OUT2 + NK
IN1_GROUPS = ((1, 4, 768), (5, 4, 0), (9, 2, 512), (11, 2, 1864), (13, 4, 1352), (17, 16, 2120))
IN2_GROUPS = ((1, 4, 0), (5, 4, 512), (9, 4, 1024), (13, 4, 1552), (17, 16, 2064))


def unit(u):
    g = u // HEADS
    b, qt = ("b", g) if g < NT else ("a", g - NT)
    k0 = max(0, qt - 1) if b == "b" else 0
    return b, qt, k0, qt + 1 - k0, u % HEADS


UNITS = 2 * NT * HEADS
STEPS = UNITS + 8


def pe_attention():
    for s in range(STEPS):
        if s < UNITS:
            yield "logits", s
        if 2 <= s < UNITS + 2:
            yield "probs_t", s - 2
        if 3 <= s < UNITS + 3:
            yield "values", s - 3
        if s >= 14 and s % 8 == 6:
            yield "out_t", s // 8 - 1


class Jobs:

    def __init__(self):
        self.at, self.freer, self.freed, self.count = {}, [], [], {"dve": 0, "act": 0}

    def add(self, name, freer):
        self.at[name] = len(self.freer)
        self.count[freer] += 1
        self.freer.append(freer)
        self.freed.append(self.count[freer])


def job_table():
    jobs = Jobs()
    for k in range(NK):
        jobs.add(("x_t", k), "act")
    jobs.add("sum0", "dve")
    jobs.add("ik_tok", "dve")
    jobs.add(("v_tok", "a"), "act")
    jobs.add(("v_tok", "b"), "act")
    jobs.add("ik_t", "act")
    for qt in range(1, NT):
        for h in range(HEADS):
            jobs.add(("index", qt, h), "act")
    for what, n in pe_attention():
        if what != "values":
            jobs.add((what, n), "act" if what == "probs_t" else "dve")
    for n in (1, 2, 3):
        jobs.add(f"sum{n}", "dve")
    for j in range(2):
        jobs.add(("z", j), "dve")
    for h in range(GH):
        jobs.add(("gv_tok", h), "act")
    for j in range(2):
        jobs.add(("kend_tok", j), "act")
    for n in range(NCH - 1):
        jobs.add(("inc", n), "dve")
    for h in range(GH):
        jobs.add(("scores", h), "dve")
    for h in range(GH):
        jobs.add(("o", h), "dve")
        jobs.add(("o_sum", h), "dve")
    for g in range(4):
        jobs.add(("pool", g), "dve")
    jobs.add("route", "act")
    jobs.add("sum4", "dve")
    jobs.add("route_t", "dve")
    for i in range(NT):
        for n in range(2):
            jobs.add(("rows", i, n), "act")
    jobs.add("places", "dve")
    jobs.add("table", "dve")
    for i in range(NT):
        for n in range(2):
            jobs.add(("resid", i, n), "act")
    return jobs


def gated_blocks(nc, A, out):
    sems, stack = {}, ExitStack()

    def S(name):
        if name not in sems:
            sems[name] = stack.enter_context(nc.semaphore(name))
        return sems[name]

    with stack:
        base = nc.sbuf_base() if callable(nc.sbuf_base) else nc.sbuf_base
        base = -(-base // 64) * 64

        def place(name, shape, offset, dt=F32):
            return nc.alloc_sbuf_tensor_at(name, shape, dt, offset=offset)

        def words(shape):
            n = 4
            for s in shape[1:]:
                n *= s
            return -(-n // 32) * 32

        def lay(at, *tensors):
            made = []
            for name, shape, *dt in tensors:
                made.append(place(name, shape, at, *dt))
                at += words(shape)
            return (*made, at)

        (con, small, ones, eps_t, rs, ssum, sq, nt0, ikstat, ikmv, ikr, iw, sinkb, top8, lnwb,
         mx, nm, den, es, xT, top) = lay(
            base, ("con", [P, CONST_WIDTH]), ("small", [P, 64]), ("ones", [P, P]), ("eps_t", [P, 1]),
            ("rs", [P, L]), ("ssum", [P, L]), ("sq", [P, 2, L]), ("nt0", [P, L]),
            ("ikstat", [P, NT, 6]), ("ikmv", [P, NT, 2]), ("ikr", [P, 4, NT]), ("iw", [P, NT, HEADS]),
            ("sinkb", [P, HEADS]), ("top8", [P, NT - 1, 8]), ("lnwb", [P, 2, HD]),
            ("mx", [P, 2 * NT, HEADS]), ("nm", [P, 2 * NT, HEADS]), ("den", [P, 2 * NT, HEADS]),
            ("es", [P, 2 * NT, HEADS]), ("xT", [P, NK, L]))
        KEEP_AT = {1: 0, 2: 2 * P, 3: 5 * P}
        keep = place("keep", [P, 9 * P], base + sum(words(x) for x in (
            [P, CONST_WIDTH], [P, 64], [P, P], [P, 1], [P, L], [P, L])))
        v_tok_a_at = base + sum(words(x) for x in ([P, CONST_WIDTH], [P, 64], [P, P], [P, 1], [P, L]))

        def const(name, rows=P):
            a, b = CONST_COLS[name]
            return con[0:rows, a:b]

        ident = const("ident")
        g_attn, g_mlp, g_fin, g_n1, g_n2 = (small[:, 8 * i:8 * i + 8] for i in range(5))
        b_alpha, g_gla, p_scale = small[:, 40:42], small[:, 42:46], small[:, 46:50]
        g_fin1 = small[:, 50:58]

        route_at = top - sum(words(x) for x in ([P, 2, HD], *[[P, 2 * NT, HEADS]] * 4, [P, NK, L]))
        wr, brt, route_end = lay(route_at, ("wr", [P, NK, NG + NE]), ("brt", [P, NG + NE]))
        assert route_end <= top - words([P, NK, L])

        raw, whi, wlo, a_at = lay(top, ("raw", [P, RING, D]), ("whi", [P, RING, D], F32R),
                                  ("wlo", [P, RING, D], F32R))
        actA_hi, actA_lo, b_at = lay(a_at, ("actA_hi", [P, NK, L], F32R), ("actA_lo", [P, NK, L], F32R))
        actB_hi, actB_lo, s_at = lay(b_at, ("actB_hi", [P, NK, L], F32R), ("actB_lo", [P, NK, L], F32R))
        pbuf, pT, o_n, _ = lay(a_at, ("pbuf", [P, 3, L]), ("pT", [P, 2, L]), ("o_n", [P, 2, L]))
        x_tok, _ = lay(b_at, ("x_tok", [P, NT, D]))
        iqT, score, rel, ik_s, ikn, ikrope, ikt, ikT, _ = lay(
            b_at, ("iqT", [P, 4, L]), ("score", [P, NT - 1, L]), ("rel", [P, 4, L]), ("ik_s", [P, L]),
            ("ikn", [P, NT, HD]), ("ikrope", [P, NT, 2 * HD]), ("ikt", [P, 4, NT * 32]), ("ikT", [P, L]))
        sg, aqT, bqT, akT, bkT, bv_tok, end1 = lay(
            s_at, ("sg", [P, 2, NK, L]), ("aqT", [P, 4, L]), ("bqT", [P, 4, L]), ("akT", [P, 2, L]),
            ("bkT", [P, 2, L]), ("bv_tok", [P, NT, P]))
        av_tok = place("av_tok", [P, NT, P], v_tok_a_at)
        rot, rt1, vT, _ = lay(s_at, ("rot", [P, 2, L]), ("rt1", [P, L]), ("vT", [P, 2, L]))
        mixb, mixt, _ = lay(s_at + words([P, 2, NK, L]), ("mixb", [P, 2, L]), ("mixt", [P, 2, L]))
        relu_u, u_sq, ytmp, _ = lay(s_at, ("relu_u", [P, 2, L]), ("u_sq", [P, 2, L]), ("ytmp", [P, L]))
        kT = {"a": akT, "b": bkT}
        qT = {"a": aqT, "b": bqT}
        v_tok = {"a": av_tok, "b": bv_tok}
        sg2, qdec, gv_tok, rsil, rsf, ssum2, go, end2 = lay(
            s_at, ("sg2", [P, 2, NK, L]), ("qdec", [P, 2, L]), ("gv_tok", [P, NT, GH * DV]),
            ("rsil", [P, GH, L]), ("rsf", [P, L]), ("ssum2", [P, L]), ("go", [P, L]))
        qs, ks, kend, pool_t, _ = lay(s_at, ("qs", [P, 2, L]), ("ks", [P, 2, L]), ("kend", [P, 2, L]),
                                      ("pool_t", [P, 2, L]))
        diff, alow, wal, pw, rs_o, dec, _ = lay(
            s_at + words([P, NK, L]), ("diff", [P, 4, L]), ("alow", [16, L]), ("wal", [16, 2 * P]),
            ("pw", [P, 4, P]), ("rs_o", [P, L]), ("dec", [P, 2, NCH]))
        gvT = place("gvT", [P, GH, L], s_at + words([P, 18, L]) + words([P, NT, GH * DV]))
        o_s = ssum2
        pool_t2 = place("pool_t2", [P, 2, L], base + sum(words(x) for x in (
            [P, CONST_WIDTH], [P, 64], [P, P], [P, 1], [P, L], [P, L])))
        half = words([P, 4, L])
        zs = place("zs", [P, 2, L], a_at)
        az = place("az", [P, 2, L], a_at + half // 2)
        kend_tok = place("kend_tok", [P, NT, 2 * P], a_at)
        gst = place("gst", [P, 2, NCH, DV], a_at + half)
        cs = place("cs", [P, 2, L], a_at + 2 * half)
        kdec = place("kdec", [P, 2, L], a_at + 2 * half + half // 2)
        scT = place("scT", [P, GH, L], a_at + 3 * half)
        (wring, xe, xeT, hid, hidT, ye, lg, rt, gw, tabi, gix, six, gfin, h2T, end3) = lay(
            top, ("wring", [P, RING, 6 * D]), ("xe", [P, RING, D]), ("xeT", [P, 2, D]), ("hid", [P, 2, DE]),
            ("hidT", [P, 2, DE]), ("ye", [P, 2, D]), 
            ("lg", [P, NT, NG + NE]), ("rt", [P, 12, NT * NE]), ("gw", [P, 16, NT]),
            ("tabi", [P, 2, NB + RING], I32), ("gix", [P, RING], I32), ("six", [P, 2], I32),
            ("gfin", [P, D]), ("h2T", [P, NK, L]))
        x_res, _ = lay(end3 - words([P, NK, L]), ("x_res", [P, NT, D]))
        y2, _ = lay(top, ("y2", [P, NT, 2 * D]))
        over_n, ones_r, earlier_r, picks_r, at_row, in_block, lgT, end4 = lay(
            end3, ("over_n", [1, 16], I32), ("ones_r", [P, P], F32R), ("earlier_r", [P, P], F32R),
            ("picks_r", [P, NT, NE], F32R), ("at_row", [P, NT, P], F32R), ("in_block", [P, NT, NB], F32R),
            ("lgT", [P, L]))
        assert max(end1, end2, end4) <= nc.sbuf_usable_end

        bank = [stack.enter_context(nc.psum_tensor(f"bank{i}", [P, L], F32)) for i in range(RING)]
        side = [stack.enter_context(nc.psum_tensor(f"side{i}", [P, L], F32)) for i in range(4)]
        jobs = job_table()

        h2_rows = nc.dram_tensor("h2_rows", [L, D], F32).ap()
        y2_rows = nc.dram_tensor("y2_rows", [2 * L, D], F32).ap()

        w_in_v = A["w_in"][0].rearrange("(k p) n -> p k n", p=P)
        w_in2_v = A["w_in_2"][0].rearrange("(k p) n -> p k n", p=P)
        br_v = [A[n][0].rearrange("(k p) n -> p k n", p=P) for n in ("w_branch_a", "w_branch_b")]
        br2_v = [A[n][0].rearrange("(k p) n -> p k n", p=P) for n in ("w_gla_branch_2", "w_pool_branch_2")]
        w_out_v = A["w_out"][0].rearrange("(k p) n -> p k n", p=P)
        w_out2_v = A["w_out_2"][0].rearrange("(k p) n -> p k n", p=P)
        w_up_v = A["w_up"][0].rearrange("(k p) n -> p k n", p=P)
        w_down_v = A["w_down"][0].rearrange("(k p) n -> p k n", p=P)

        def loads(c):
            return 2 if C_BR <= c < C_OUT or C_BR2 <= c < C_OUT2 else 1

        def raw_value(c):
            return 16 * sum(loads(j) for j in range(c % RING, c + 1, RING))

        raw_loaded = [S(f"raw_loaded{r}") for r in range(RING)]
        hi_made, lo_made, chunk_done, chunk_freed = S("hi_made"), S("lo_made"), S("chunk_done"), S("chunk_freed")
        side_full = S("side_full")
        side_freed = {"dve": S("side_freed_by_dve"), "act": S("side_freed_by_act")}
        STAGES = ("in", "branch", "out", "mlp", "in2", "branch2", "out2")

        def at(i, u, k):
            return u + k if i is None else RING * i + (u + k)

        def wait_from(e, sem, i, u, k):
            if i is not None or u + k > 0:
                e.wait_ge(sem, at(i, u, k))

        LAST = (NE // RING - 1, RING - 1)

        def before(i, u):
            return (i, u - 1) if u else (i - 1, RING - 1)

        def for_experts(e, expert, last, overflow, end=lambda: None):
            for u in range(RING):
                expert(None, u)
            with e.Fori(1, NE // RING) as i:
                for u in range(RING):
                    expert(i, u)
            last()
            e.wait_ge(S("over_ready"), 1)
            over = e.value_load(over_n[0:1, 0:1], min_val=0, max_val=OVER)
            with e.If(over > 0):
                with e.Fori(NE // RING, NB // RING) as i:
                    for u in range(RING):
                        overflow(i, u)
                end()

        block = stack.enter_context(nc.Block())

        def wait_job(e, name):
            e.wait_ge(side_full, jobs.at[name] + 1)

        def wait_freed(e, name):
            i = jobs.at[name]
            e.wait_ge(side_freed[jobs.freer[i]], jobs.freed[i])

        @block.sync
        def _(sp):
            sp.dma_start(ident, A["consts"][:, 0:P]).then_inc(S("x_in"), 16)
            for i in range(NT):
                sp.dma_start(x_tok[:, i, :], A["x"][0, i * P:(i + 1) * P, :]).then_inc(S("x_in"), 16)

            def load_chunk(c, wait, *views):
                if wait is not None:
                    sp.wait_ge(lo_made, wait)
                for k0, k1, v in views:
                    sp.dma_start(raw[:, c % RING, k0 * P:k1 * P].rearrange("p (k n) -> p k n", n=P), v)\
                      .then_inc(raw_loaded[c % RING], 16)

            def load_group(first, n, view, col, step=P):
                if n % RING or first < RING:
                    for j in range(n):
                        c = first + j
                        load_chunk(c, c - RING + 1 if c >= RING else None,
                                   (0, NK, view[:, :, col + P * j:col + P * (j + 1)]))
                    return
                with sp.Fori(0, n // RING) as i:
                    for u in range(RING):
                        load_chunk(first + u, first + u - RING + 1 + RING * i,
                                   (0, NK, view[:, :, bass.ds(i * (RING * P) + (col + u * P), P)]))

            def load_branches(first, views):
                with sp.Fori(0, NK // RING) as i:
                    for u in range(RING):
                        at = bass.ds(i * (RING * P) + u * P, P)
                        load_chunk(first + u, first + u - RING + 1 + RING * i,
                                   (0, 4, views[0][:, :, at]), (4, 8, views[1][:, :, at]))

            load_group(0, 1, w_in_v, 1280)
            sp.dma_start(con[:, P:], A["consts"][:, P:]).then_inc(S("const_in"), 16)
            for name, t in (("attn_norm_w", g_attn), ("mlp_norm_w", g_mlp), ("norm1_g_2", g_n1), ("norm2_g_2", g_n2)):
                sp.dma_start(t, A[name][0].rearrange("(k p) -> p k", p=P), allow_slow_non_contiguous=True)\
                  .then_inc(S("small_in"), 16)
            sp.dma_start(g_fin, A["final_norm_w"].rearrange("(k p) -> p k", p=P), allow_slow_non_contiguous=True)\
              .then_inc(S("small_in"), 16)
            for name, t in (("b_alpha_2", b_alpha), ("gla_norm_g_2", g_gla), ("pool_scale_2", p_scale)):
                sp.dma_start(t, A[name][0].rearrange("(k p) -> p k", p=P), allow_slow_non_contiguous=True)\
                  .then_inc(S("small_in"), 16)
            sp.dma_start(sinkb[:, :], A["sinks"][0].partition_broadcast(P)).then_inc(S("small_in"), 16)
            sp.dma_start(lnwb[:, 0, :], A["idx_k_norm_w"][0].partition_broadcast(P)).then_inc(S("small_in"), 16)
            sp.dma_start(lnwb[:, 1, :], A["idx_k_norm_b"][0].partition_broadcast(P)).then_inc(S("small_in"), 16)
            for j, n, col in IN1_GROUPS:
                load_group(C_IN + j, n, w_in_v, col)
            load_branches(C_BR, br_v)
            load_group(C_OUT, NK, w_out_v, 0)
            for q in range(QUARTERS):
                load_group(C_MLP + 2 * NK * q, NK, w_up_v, D * q)
                load_group(C_MLP + 2 * NK * q + NK, NK, w_down_v[:, NK * q:NK * (q + 1), :], 0)
            load_group(C_IN2, 1, w_in2_v, 1536)
            sp.wait_ge(chunk_freed, C_OUT)
            sp.dma_start(wal[:, :], A["w_alpha_up_2"][0]).then_inc(S("small2_in"), 16)
            sp.dma_start(pw[:, :, :], A["pool_w_2"][0].rearrange("g c d -> c g d")).then_inc(S("small2_in"), 16)
            sp.dma_start(wr[:, :, 0:NG], A["w_router_group_2"][0].rearrange("(k p) g -> p k g", p=P),
                         allow_slow_non_contiguous=True).then_inc(S("route_in"), 16)
            for g in range(NG):
                sp.dma_start(wr[:, :, NG + EPG * g:NG + EPG * (g + 1)],
                             A["w_router_expert_2"][0, g].rearrange("(k p) e -> p k e", p=P),
                             allow_slow_non_contiguous=True).then_inc(S("route_in"), 16)
            sp.dma_start(brt[:, 0:NG], A["b_router_group_2"][0].partition_broadcast(P)).then_inc(S("route_in"), 16)
            sp.dma_start(brt[:, NG:], A["b_router_expert_2"][0].rearrange("g e -> (g e)").partition_broadcast(P))\
              .then_inc(S("route_in"), 16)
            for j, n, col in IN2_GROUPS:
                load_group(C_IN2 + j, n, w_in2_v, col)
            load_branches(C_BR2, br2_v)
            load_group(C_OUT2, NK, w_out2_v, 0)

            sp.wait_ge(chunk_freed, N_CHUNKS)
            sp.dma_start(gfin[:, :], A["norm_f_g_2"].partition_broadcast(P)).then_inc(S("gain_in"), 16)

            wg_v = A["w_exp_gate_2"][0].rearrange("e (k p) n -> p e k n", p=P)
            wu_v = A["w_exp_up_2"][0].rearrange("e (k p) n -> p e k n", p=P)
            wd_v = A["w_exp_down_2"][0].rearrange("e (k p) n -> p e k n", p=P)

            def load_expert(slot, e):
                gu = wring[:, slot, 0:4 * D].rearrange("p (k h n) -> p k h n", h=2, n=DE)
                down = wring[:, slot, 4 * D:6 * D].rearrange("p (o k n) -> p o k n", o=1, n=D)
                at = slice(e, e + 1) if isinstance(e, int) else bass.ds(e, 1)
                for h, v in enumerate((wg_v, wu_v)):
                    sp.dma_start(gu[:, :, h, :], v[:, at, :, :].rearrange("p e k n -> p (e k) n"))\
                      .then_inc(S(f"expert_in{slot}"), 16)
                sp.dma_start(down, wd_v[:, at, :, :]).then_inc(S(f"expert_in{slot}"), 16)

            load_expert(0, 0)
            for i in range(NT):
                wait_freed(sp, ("rows", i, 1))
                sp.dma_start(h2_rows[i * P:(i + 1) * P, :], xe[:, i, :]).then_inc(S("h2_stored"), 16)
            load_expert(1, 1)
            sp.wait_ge(S("gathered0"), 16)
            for e in range(2, RING):
                load_expert(e, e)
            with sp.Fori(1, NE // RING) as i:
                for u in range(RING):
                    sp.wait_ge(S("down_done"), RING * i + (u - RING + 1))
                    load_expert(u, RING * i + u)
            sp.wait_ge(S("over_ready"), 1)
            over = sp.value_load(over_n[0:1, 0:1], min_val=0, max_val=OVER)
            with sp.If(over > 0):
                with sp.Fori(0, OVER // RING) as i:
                    for u in range(RING):
                        sp.wait_ge(S("down_done"), RING * i + (NE + u - RING + 1))
                        e = sp.value_load(over_n[0:1, bass.ds(RING * i + (1 + u), 1)], min_val=0, max_val=NE - 1)
                        load_expert(u, e)

            sp.wait_ge(S("experts_over"), 1)
            for i in range(NT):
                sp.dma_start(y2[:, i, :].rearrange("p (k n) -> p k n", k=2),
                             y2_rows.rearrange("(k t p) n -> t p k n", k=2, p=P)[i]).then_inc(S(f"y2_in{i}"), 16)
            for i in range(NT):
                sp.wait_ge(S("final_out"), i + 1)
                sp.dma_start(out[i * P:(i + 1) * P, :], x_res[:, i, :]).then_inc(S("stored"), 16)
            sp.wait_ge(S("stored"), 16 * NT)

        @block.gpsimd
        def _(pool):
            def second_part(slot, wait):
                pool.wait_ge(hi_made, wait)
                nc.gpsimd.tensor_tensor(wlo[:, slot, :], raw[:, slot, :], whi[:, slot, :].bitcast(F32),
                                        ALU.subtract).then_inc(lo_made, 1)

            with pool.Fori(0, N_CHUNKS // RING) as i:
                for u in range(RING):
                    second_part(u, RING * i + (u + 1))
            for c in range(N_CHUNKS // RING * RING, N_CHUNKS):
                second_part(c % RING, c + 1)

            pool.wait_ge(S("h2_stored"), 16 * NT)
            pool.wait_ge(S("rows_ready"), 1)
            row_bound, slot_bound = pool.to_reg(L - 1), pool.to_reg(2 * L - 1)

            def gather(u, b, column_set, copies):
                nc.gpsimd.tensor_copy(gix[:, u:u + 1], tabi[:, 1, bass.ds(b, 1)]).then_inc(S(column_set), 1)
                pool.wait_ge(S("rows_ready"), 1)
                pool.wait_ge(S(column_set), copies)
                pool.indirect_dma_start(xe[:, u, :], None, h2_rows,
                                        bass.IndirectOffsetOnAxis(ap=gix[:, u:u + 1], axis=0),
                                        bounds_check=row_bound, oob_is_err=False).then_inc(S(f"gathered{u}"), 16)

            def move_rows(i, u):
                j, b = u % 2, at(i, u, 0)
                pool.wait_ge(S("xe_used"), at(i, u, 1))
                gather(u, at(i, u, RING), "gix_set", at(i, u, 1))
                if i is not None or u >= 2:
                    pool.wait_ge(S(f"scattered{j}"), 16 * (u // 2) if i is None else 32 * i + 16 * (u // 2))
                pool.wait_ge(S("y_by_act"), at(i, u, 1))
                pool.wait_ge(S("y_by_dve"), at(i, u, 1))
                nc.gpsimd.tensor_copy(six[:, j:j + 1], tabi[:, 0, bass.ds(b, 1)]).then_inc(S("six_set"), 1)
                pool.wait_ge(S("rows_ready"), 1)
                pool.wait_ge(S("six_set"), at(i, u, 1))
                pool.indirect_dma_start(y2_rows, bass.IndirectOffsetOnAxis(ap=six[:, j:j + 1], axis=0),
                                        ye[:, j, :], None, bounds_check=slot_bound, oob_is_err=False)\
                    .then_inc(S(f"scattered{j}"), 16)

            def all_moved(blocks):
                for u in range(RING):
                    pool.wait_ge(S(f"gathered{u}"), 16 * (blocks // RING + 1))
                for j in range(2):
                    pool.wait_ge(S(f"scattered{j}"), 16 * blocks // 2)

            for u in range(RING):
                gather(u, u, "first_gix_set", u + 1)
            for_experts(pool, move_rows, lambda: all_moved(NE), move_rows, lambda: all_moved(NB))
            nc.gpsimd.memset(gix[:, :], 0).then_inc(S("experts_over"), 1)

        def side_of(name):
            return side[jobs.at[name] % 4]

        def out_bank(c):
            return bank[c % RING]

        class Chain:

            def __init__(self, e, sem):
                self.e, self.sem, self.n = e, sem, {}

            def __call__(self, ins, sem=None):
                sem = sem or self.sem
                self.n[id(sem)] = self.n.get(id(sem), 0) + 1
                ins.then_inc(sem, 1)
                self.e.wait_ge(sem, self.n[id(sem)])

        def rope_index(c):
            return [1, 2, 3, 4, 5, 6, 7, 8, 9, 11, 13, 14, 15, 16].index(c)

        ROPED = (1, 2, 3, 4, 5, 6, 7, 8, 9, 11, 13, 14, 15, 16)
        N_SMALL = 11

        @block.scalar
        def _(act):
            chain = Chain(act, S("act_step"))
            a = nc.scalar.activation

            def first_part(c):
                if c >= N_CHUNKS:
                    return
                act.wait_ge(raw_loaded[c % RING], raw_value(c))
                if c >= RING:
                    act.wait_ge(chunk_done, c - RING + 1)
                a(whi[:, c % RING, :], raw[:, c % RING, :], ACT.Copy).then_inc(hi_made, 1)

            def split_first(stage, hi, k, src, gain):
                ins = a(hi[:, k, :], src, ACT.Copy) if gain is None else \
                    a(hi[:, k, :], src, ACT.Copy, scale=gain[:, k:k + 1])
                ins.then_inc(S(f"hi_{stage}"), 1)

            def squares(n, src, gain=None, of="sq_made", added="sum_added"):
                if n >= 2:
                    act.wait_ge(S(added), n - 1)
                ins = a(sq[:, n % 2, :], src, ACT.Square) if gain is None else \
                    a(sq[:, n % 2, :], src, ACT.Square, scale=gain)
                ins.then_inc(S(of), 1)

            def guess(src, n, dst=None, width=D, tmp=None):
                dst = rs[:, :] if dst is None else dst
                tmp = nt0[:, :] if tmp is None else tmp
                nc.scalar.preload_act_table_set("natural_log_exp_and_others")
                chain(a(tmp, src, ACT.Ln, scale=1.0 / width, bias=eps_t[:, :]))
                chain(a(dst, tmp, ACT.Exp, scale=-0.5), S("guess_made"))

            act.wait_ge(S("eps_set"), 1)
            act.wait_ge(S("small_in"), 16 * N_SMALL)
            first_part(0)
            for k in range(NK):
                wait_job(act, ("x_t", k))
                chain(a(xT[:, k, :], side_of(("x_t", k))[:, :], ACT.Copy), side_freed["act"])
                split_first("in", actA_hi, k, xT[:, k, :], g_attn)
                squares(k, xT[:, k, :])
            first_part(1)
            first_part(2)
            wait_job(act, "sum0")
            guess(side_of("sum0")[:, :], 0)
            for c in range(C_IN, C_IN + 17):
                first_part(c + AHEAD)
                if c in ROPED:
                    r = ROPED.index(c)
                    act.wait_ge(chunk_done, c + 1)
                    if r >= 2:
                        act.wait_ge(S("roped"), r - 1)
                    for q in range(4):
                        other = 32 * (q ^ 1)
                        ins = a(rot[32 * q:32 * q + 32, r % 2, :], out_bank(c)[other:other + 32, :], ACT.Copy,
                                scale=-1.0 if q % 2 == 0 else 1.0)
                    ins.then_inc(S("rot_made"), 1)
                if c == 6:
                    act.wait_ge(S("ik_var"), 1)
                    guess(ikmv[:, :, 1], 1, ikr[:, 1, :], 1, ikr[:, 0, :])
                if c == 12:
                    for n, b in enumerate("ab"):
                        wait_job(act, ("v_tok", b))
                        a(v_tok[b][:, :, :].rearrange("p t f -> p (t f)"), side_of(("v_tok", b))[:, :], ACT.Copy)\
                            .then_inc(side_freed["act"], 1)
                    wait_job(act, "ik_t")
                    a(ikT[:, :], side_of("ik_t")[:, :], ACT.Copy).then_inc(side_freed["act"], 1)
            n = 0
            for qt in range(1, NT):
                for h in range(HEADS):
                    wait_job(act, ("index", qt, h))
                    if n >= 4:
                        act.wait_ge(S("index_added"), n - 3)
                    w = (qt + 1) * P
                    a(rel[:, n % 4, 0:w], side_of(("index", qt, h))[:, 0:w], ACT.Relu).then_inc(side_freed["act"], 1)
                    n += 1
            for c in range(C_IN + 17, C_IN + 33):
                if c + AHEAD < C_BR + AHEAD:
                    first_part(c + AHEAD)
                j = c - C_IN - 17
                act.wait_ge(chunk_freed, c + 1)
                t = sg[:, j // NK, j % NK, :]
                a(t, t, ACT.Sigmoid).then_inc(S("gate_made"), 1)

            nc.scalar.preload_act_table_set("natural_log_exp_and_others")
            for s in range(STEPS):
                if s % 8 == 7 and s >= 15:
                    g = s // 8 - 1
                    b, qt = unit(g * HEADS)[:2]
                    k = 4 if b == "b" else 0
                    wait_job(act, ("out_t", g))
                    a(actB_hi[:, k:k + 4, qt * P:(qt + 1) * P],
                      side_of(("out_t", g))[:, :].rearrange("p (f q) -> p f q", q=P), ACT.Copy)\
                        .then_inc(S("hi_branch"), 1)
                if s < UNITS:
                    b, qt, k0, nk, h = unit(s)
                    t = pbuf[:, s % 3, 0:nk * P]
                    act.wait_ge(S("logits_made"), s + 1)
                    a(t, t, ACT.Exp, bias=nm[:, s // HEADS, h:h + 1],
                      accum_out=den[:, s // HEADS, h:h + 1]).then_inc(S("probs_made"), 1)
                if 1 <= s < UNITS + 1:
                    u = s - 1
                    nk = unit(u)[3]
                    wait_job(act, ("probs_t", u))
                    if u >= 2:
                        act.wait_ge(S("values_done"), u - 1)
                    a(pT[:, u % 2, 0:nk * P], side_of(("probs_t", u))[:, 0:nk * P], ACT.Copy)\
                        .then_inc(side_freed["act"], 1)
                if s % 8 == 1 and 9 <= s <= 8 * NT + 1:
                    g = s // 8 - 1
                    act.wait_ge(S("sinks_shifted"), g + 1)
                    a(es[:, g, :], es[:, g, :], ACT.Exp).then_inc(S("sinks_exp"), 1)

            def mix_parts(first, stage, hi):
                for m in range(NK):
                    first_part(first + m + AHEAD)
                    act.wait_ge(S(f"mixed_{stage}"), m + 1)
                    split_first(stage, hi, m, mixb[:, m % 2, :], None)

            mix_parts(C_BR, "out", actA_hi)
            for m in range(NK):
                first_part(C_OUT + m + AHEAD)
                act.wait_ge(chunk_freed, C_OUT + m + 1)
                split_first("mlp", actB_hi, m, xT[:, m, :], g_mlp)
                squares(NK + m, xT[:, m, :])
            for q in range(QUARTERS):
                up = C_MLP + 2 * NK * q
                for m in range(NK):
                    first_part(up + m + AHEAD)
                    act.wait_ge(chunk_freed, up + m + 1)
                    chain(a(u_sq[:, m % 2, :], relu_u[:, m % 2, :], ACT.Square), S("u_made"))
                    split_first(f"u{q}", actA_hi, m, u_sq[:, m % 2, :], None)
                if q == 0:
                    wait_job(act, "sum1")
                    guess(side_of("sum1")[:, :], 2)
                for m in range(NK):
                    first_part(up + NK + m + AHEAD)
                    if q == QUARTERS - 1:
                        act.wait_ge(S("x1_made"), m + 1)
                        split_first("in2", actB_hi, m, xT[:, m, :], g_fin1)
                        squares(2 * NK + 2 * m, xT[:, m, :])
                        squares(2 * NK + 2 * m + 1, xT[:, m, :], g_fin[:, m:m + 1])
            wait_job(act, "sum2")
            guess(side_of("sum2")[:, :], 3, rsf[:, :])
            act.wait_ge(S("second_sum"), 1)
            guess(ssum2[:, :], 4)

            for c in range(C_IN2, C_IN2 + 5):
                first_part(c + AHEAD)
            for j in range(2):
                wait_freed(act, ("z", j))
                chain(a(az[:, j, :], zs[:, j, :], ACT.Abs))
                chain(a(az[:, j, :], az[:, j, :], ACT.Exp, scale=-1.0))
                a(az[:, j, :], az[:, j, :], ACT.Ln, bias=1.0).then_inc(S("log_made"), 1)
            for c in range(C_IN2 + 5, C_IN2 + 9):
                first_part(c + AHEAD)
            for j in range(2):
                act.wait_ge(S("decay_summed"), j + 1)
                a(az[:, j, :], cs[:, j, :], ACT.Exp, scale=1.0 / 16.0).then_inc(S("decays"), 1)
                a(zs[:, j, :], cs[:, j, :], ACT.Exp, scale=-1.0 / 16.0).then_inc(S("decays"), 1)
            for j in range(2):
                act.wait_ge(S("decay_left"), j + 1)
                a(cs[:, j, :], cs[:, j, :], ACT.Exp, scale=1.0 / 16.0).then_inc(S("decays"), 1)
            for h in range(GH):
                wait_job(act, ("gv_tok", h))
                a(gv_tok[:, :, h * DV:(h + 1) * DV], side_of(("gv_tok", h))[:, :].rearrange("p (t f) -> p t f", f=DV),
                  ACT.Copy).then_inc(side_freed["act"], 1)
            for c in range(C_IN2 + 9, C_IN2 + 13):
                first_part(c + AHEAD)
                h = c - C_IN2 - 9
                act.wait_ge(chunk_freed, c + 1)
                a(pool_t[:, h % 2, :], rsil[:, h, :], ACT.Sigmoid).then_inc(S("r_sigmoid"), 1)
                act.wait_ge(S("r_silu"), h + 1)
            for c in range(C_IN2 + 13, C_IN2 + 17):
                first_part(c + AHEAD)
            for j in range(2):
                wait_job(act, ("kend_tok", j))
                a(kend_tok[:, :, j * P:(j + 1) * P], side_of(("kend_tok", j))[:, :].rearrange("p (t f) -> p t f", f=P),
                  ACT.Copy).then_inc(side_freed["act"], 1)

            def gate(c):
                first_part(c + AHEAD)
                j = c - C_IN2 - 17
                act.wait_ge(chunk_freed, c + 1)
                t = sg2[:, j // NK, j % NK, :]
                a(t, t, ACT.Sigmoid).then_inc(S("gate_made"), 1)

            for c in range(C_IN2 + 17, C_IN2 + 21):
                gate(c)
            for h in range(GH):
                wait_job(act, ("o", h))
                if h:
                    act.wait_ge(S("o_sum_taken"), h)
                a(sq[:, 0, :], side_of(("o", h))[:, :], ACT.Square).then_inc(S("o_squares"), 1)
                gate(C_IN2 + 21 + h)
                wait_job(act, ("o_sum", h))
                guess(side_of(("o_sum", h))[:, :], 5 + h, rs_o[:, :], DV)
                act.wait_ge(S("o_normed"), h + 1)
                split_first("branch2", actA_hi, h, o_s[:, :], None)
            for g in range(4):
                wait_freed(act, ("pool", g))
                split_first("branch2", actA_hi, 4 + g, pool_t2[:, g % 2, :], None)
            for c in range(C_IN2 + 25, C_IN2 + 33):
                gate(c)
            mix_parts(C_BR2, "out2", actB_hi)
            for m in range(NK):
                first_part(C_OUT2 + m + AHEAD)
                act.wait_ge(chunk_freed, C_OUT2 + m + 1)
                squares(m, xT[:, m, :], None, "sq4_made", "sum4_added")
            wait_job(act, "route")
            a(lgT[0:NG + NE, :], side_of("route")[0:NG + NE, :], ACT.Copy).then_inc(side_freed["act"], 1)
            wait_job(act, "sum4")
            guess(side_of("sum4")[:, 0:NT], 9, gw[:, 13, :], D, gw[:, 14, :])

            act.wait_ge(S("norm_made"), 1)
            for i in range(NT):
                for n in range(2):
                    wait_job(act, ("rows", i, n))
                    a(xe[:, i, n * L:(n + 1) * L], side_of(("rows", i, n))[:, :], ACT.Copy, scale=gw[:, 13, i:i + 1])\
                        .then_inc(side_freed["act"], 1)
            act.wait_ge(S("group_shifted"), 1)
            a(rt[:, 0, 0:NT * NG], rt[:, 0, 0:NT * NG], ACT.Exp).then_inc(S("group_exp"), 1)
            act.wait_ge(S("expert_shifted"), 1)
            a(gw[:, 6, :], gw[:, 6, :], ACT.Exp).then_inc(S("expert_exp"), 1)
            for i in range(NT):
                for n in range(2):
                    wait_job(act, ("resid", i, n))
                    a(x_res[:, i, n * L:(n + 1) * L], side_of(("resid", i, n))[:, :], ACT.Copy)\
                        .then_inc(side_freed["act"], 1)

            def x_turned(i, u):
                act.wait_ge(S("xe_used"), at(i, u, 2))
                wait_from(act, S("gate_up_done"), i, u, 0)
                a(xeT[:, (u + 1) % 2, 0:L], side[0][:, :], ACT.Copy).then_inc(S("xe_t_by_act"), 1)

            def silu(i, u):
                act.wait_ge(S("gate_up_done"), at(i, u, 1))
                wait_from(act, S("hid_turned"), i, u, -1)
                a(hid[:, u % 2, :], bank[u % 2][:, 0:DE], ACT.Silu).then_inc(S("silu_made"), 1)

            def y_out(i, u):
                act.wait_ge(S("down_done"), at(i, u, 1))
                if i is not None or u >= 2:
                    act.wait_ge(S(f"scattered{u % 2}"), 16 * (u // 2) if i is None else 32 * i + 16 * (u // 2))
                a(ye[:, u % 2, 0:L], bank[2][:, :], ACT.Copy).then_inc(S("y_by_act"), 1)

            def expert(i, u):
                silu(i, u)
                x_turned(i, u)
                if i is not None or u > 0:
                    y_out(*before(i, u))

            def overflow(i, u):
                silu(i, u)
                x_turned(i, u)
                y_out(i, u)

            act.wait_ge(S("xe_used"), 1)
            a(xeT[:, 0, 0:L], side[0][:, :], ACT.Copy).then_inc(S("xe_t_by_act"), 1)
            for_experts(act, expert, lambda: y_out(*LAST), overflow)

            for i in range(NT):
                act.wait_ge(S("final_sum"), i + 1)
                chain(a(xe[:, 0, :], x_res[:, i, :], ACT.Square, accum_out=gw[:, 12, i:i + 1]))
                guess(gw[:, 12, i:i + 1], 10 + i, gw[:, 13, i:i + 1], D, gw[:, 14, i:i + 1])

        @block.vector
        def _(dve):
            chain = Chain(dve, S("dve_step"))
            v = nc.vector
            guesses = [0]

            def refine(src, dst=None, width=D, tmp=None, tmp2=None, freed=None):
                dst = rs[:, :] if dst is None else dst
                tmp = nt0[:, :] if tmp is None else tmp
                tmp2 = ssum[:, :] if tmp2 is None else tmp2
                guesses[0] += 1
                dve.wait_ge(S("guess_made"), guesses[0])
                chain(v.tensor_scalar(tmp, src, -0.5 / width, -0.5 * EPS, ALU.mult, ALU.add), freed)
                chain(v.tensor_tensor(tmp2, dst, dst, ALU.mult))
                chain(v.tensor_tensor(tmp2, tmp2, tmp, ALU.mult))
                chain(v.scalar_tensor_tensor(dst, tmp2, 1.5, dst, ALU.add, ALU.mult))

            def second(stage, hi, lo, k, src, gain):
                dve.wait_ge(S(f"hi_{stage}"), k + 1)
                first = hi[:, k, :].bitcast(F32)
                if gain is None:
                    ins = v.tensor_tensor(lo[:, k, :], src, first, ALU.subtract)
                else:
                    ins = v.scalar_tensor_tensor(lo[:, k, :], src, gain[:, k:k + 1], first, ALU.mult, ALU.subtract)
                chain(ins, S(f"ready_{stage}"))

            def add_squares(n, m, total=None, made="sq_made", added="sum_added"):
                total = ssum if total is None else total
                dve.wait_ge(S(made), n + 1)
                if m == 0:
                    chain(v.tensor_copy(total[:, :], sq[:, n % 2, :]), S(added))
                else:
                    chain(v.tensor_tensor(total[:, :], total[:, :], sq[:, n % 2, :], ALU.add), S(added))

            freed = side_freed["dve"]
            chain(v.memset(eps_t[:, :], EPS), S("eps_set"))
            chain(v.memset(ones[:, :], 1.0), S("ones_set"))
            dve.wait_ge(S("small_in"), 16 * N_SMALL)
            chain(v.tensor_tensor(g_fin1, g_fin, g_n1, ALU.mult), S("gain_set"))
            for k in range(NK + 1):
                if k < NK:
                    second("in", actA_hi, actA_lo, k, xT[:, k, :], g_attn)
                if k >= 1:
                    add_squares(k - 1, k - 1)
            refine(side_of("sum0")[:, :], freed=freed)
            dve.wait_ge(S("const_in"), 16)
            chain(v.tensor_tensor(const("cos"), const("cos"), rs[:, :], ALU.mult))
            chain(v.tensor_tensor(const("sin"), const("sin"), rs[:, :], ALU.mult))

            def take(c, dst, by=None):
                dve.wait_ge(chunk_done, c + 1)
                chain(v.tensor_tensor(dst, out_bank(c)[0:dst.shape[0], :], (rs[:, :] if by is None else by)[0:dst.shape[0], :],
                                      ALU.mult), chunk_freed)

            def rope(c, *dst):
                r = ROPED.index(c)
                dve.wait_ge(S("rot_made"), r + 1)
                chain(v.tensor_tensor(rt1[:, :], out_bank(c)[:, :], const("cos"), ALU.mult), chunk_freed)
                chain(v.tensor_tensor(rot[:, r % 2, :], rot[:, r % 2, :], const("sin"), ALU.mult))
                for n, (rows, out_rows, to) in enumerate(dst):
                    chain(v.tensor_tensor(to[out_rows, :], rt1[rows, :], rot[rows, r % 2, :], ALU.add),
                          S("roped") if n == len(dst) - 1 else None)

            ALL, LOW, HIGH = slice(0, P), slice(0, HD), slice(HD, P)

            def rope_keys(c, to):
                rope(c, (LOW, LOW, to[:, 0, :]), (LOW, HIGH, to[:, 0, :]),
                     (HIGH, HIGH, to[:, 1, :]), (HIGH, LOW, to[:, 1, :]))

            take(C_IN, ik_s[:, :])
            for c in range(1, 5):
                rope(c, (ALL, ALL, iqT[:, c - 1, :]))
            wait_job(dve, "ik_tok")
            by_tok = side_of("ik_tok")[:, :].rearrange("p (t f) -> p t f", f=P)
            chain(v.tensor_scalar(iw[:, :, :], by_tok[:, :, HD:HD + HEADS], W_SCALE, None, ALU.mult))
            for t in range(NT):
                chain(v.bn_stats(ikstat[:, t, :], by_tok[:, t, 0:HD]))
                chain(v.bn_aggr(ikmv[:, t, :], ikstat[:, t, :]), S("ik_var") if t == NT - 1 else None)
            for t in range(NT):
                chain(v.tensor_scalar(ikn[:, t, :], by_tok[:, t, 0:HD], ikmv[:, t, 0:1], None, ALU.subtract),
                      freed if t == NT - 1 else None)
            for c in range(5, 7):
                rope(c, (ALL, ALL, aqT[:, c - 5, :]))
            refine(ikmv[:, :, 1], ikr[:, 1, :], 1, ikr[:, 2, :], ikr[:, 3, :])
            for t in range(NT):
                chain(v.tensor_scalar(ikn[:, t, :], ikn[:, t, :], ikr[:, 1, t:t + 1], None, ALU.mult))
            for n, op in ((0, ALU.mult), (1, ALU.add)):
                chain(v.tensor_tensor(ikn[:, :, :], ikn[:, :, :],
                                      lnwb[:, n, :].unsqueeze(1).broadcast_to([P, NT, HD]), op))
            cos_t, sin_t = (const(n).rearrange("p (t f) -> p t f", f=32) for n in ("cos_tok", "sin_tok"))
            tmp = [ikt[:, n, :].rearrange("p (t f) -> p t f", f=32) for n in range(4)]
            x1, x2 = ikn[:, :, 0:32], ikn[:, :, 32:64]
            for n, (x, cs_) in enumerate(((x1, cos_t), (x2, sin_t), (x2, cos_t), (x1, sin_t))):
                chain(v.tensor_tensor(tmp[n], x, cs_, ALU.mult))
            for half in range(2):
                o = ikrope[:, :, half * HD:(half + 1) * HD]
                chain(v.tensor_tensor(o[:, :, 0:32], tmp[0], tmp[1], ALU.subtract))
                chain(v.tensor_tensor(o[:, :, 32:64], tmp[2], tmp[3], ALU.add), S("ik_roped"))
            for c in range(7, 9):
                rope(c, (ALL, ALL, aqT[:, c - 5, :]))
            rope_keys(9, akT)
            take(10, vT[:, 0, :])
            rope_keys(11, bkT)
            take(12, vT[:, 1, :])
            for c in range(13, 17):
                rope(c, (ALL, ALL, bqT[:, c - 13, :]))
            n = 0
            for qt in range(1, NT):
                w = (qt + 1) * P
                s = score[:, qt - 1, 0:w]
                for h in range(HEADS):
                    wait_freed(dve, ("index", qt, h))
                    r = rel[:, n % 4, 0:w]
                    if h == 0:
                        ins = v.tensor_scalar(s, r, iw[:, qt, h:h + 1], None, ALU.mult)
                    else:
                        ins = v.scalar_tensor_tensor(s, r, iw[:, qt, h:h + 1], s, ALU.mult, ALU.add)
                    chain(ins, S("index_added"))
                    n += 1
                own = score[:, qt - 1, qt * P:w]
                chain(v.tensor_tensor(own, own, const("causal"), ALU.add))
            for c in range(17, 33):
                take(c, sg[:, (c - 17) // NK, (c - 17) % NK, :])
                for qt in range(1, NT):
                    s = score[:, qt - 1, 0:(qt + 1) * P]
                    chain(v.max(top8[:, qt - 1, :], s))
                    chain(v.match_replace(s, top8[:, qt - 1, :], s, TAKEN))
            for qt in range(1, NT):
                w = (qt + 1) * P
                chain(v.tensor_scalar(keep[:, KEEP_AT[qt]:KEEP_AT[qt] + w], score[:, qt - 1, 0:w],
                                      TAKEN * 0.98, NEG, ALU.is_gt, ALU.mult))

            b0 = CONST_COLS["before"][0]
            for s in range(STEPS):
                if s % 8 == 0 and 8 <= s <= 8 * NT:
                    g = s // 8 - 1
                    chain(v.tensor_tensor(es[:, g, :], sinkb[:, :], nm[:, g, :], ALU.add), S("sinks_shifted"))
                if s % 8 == 7 and s >= 15:
                    g = s // 8 - 1
                    b, qt = unit(g * HEADS)[:2]
                    k = 4 if b == "b" else 0
                    cols = slice(qt * P, (qt + 1) * P)
                    dve.wait_ge(S("hi_branch"), g + 1)
                    chain(v.tensor_tensor(actB_lo[:, k:k + 4, cols],
                                          side_of(("out_t", g))[:, :].rearrange("p (f q) -> p f q", q=P),
                                          actB_hi[:, k:k + 4, cols].bitcast(F32), ALU.subtract), freed)
                if s < UNITS:
                    b, qt, k0, nk, h = unit(s)
                    g = s // HEADS
                    wait_job(dve, ("logits", s))
                    if s >= 3:
                        wait_job(dve, ("probs_t", s - 3))
                    if qt == 0:
                        bias = const("causal")
                    elif b == "b":
                        bias = con[:, b0:b0 + 2 * P]
                    else:
                        bias = keep[:, KEEP_AT[qt]:KEEP_AT[qt] + nk * P]
                    chain(v.tensor_tensor_reduce(
                        out=pbuf[:, s % 3, 0:nk * P], in0=side_of(("logits", s))[:, 0:nk * P], in1=bias,
                        scale=ATT_SCALE, scalar=-3.0e38, op0=ALU.add, op1=ALU.max,
                        accum_out=mx[:, g, h:h + 1]), freed)
                    if b == "b":
                        ins = v.tensor_scalar(nm[:, g, h:h + 1], mx[:, g, h:h + 1], sinkb[:, h:h + 1], -1.0,
                                              ALU.max, ALU.mult)
                    else:
                        ins = v.tensor_scalar(nm[:, g, h:h + 1], mx[:, g, h:h + 1], -1.0, None, ALU.mult)
                    chain(ins, S("logits_made"))
                if s % 8 == 3 and s >= 11:
                    g = s // 8 - 1
                    dve.wait_ge(S("probs_made"), (g + 1) * HEADS)
                    if g < NT:
                        dve.wait_ge(S("sinks_exp"), g + 1)
                        chain(v.tensor_tensor(den[:, g, :], den[:, g, :], es[:, g, :], ALU.add))
                    chain(v.reciprocal(mx[:, g, :], den[:, g, :]))
                    dve.wait_ge(S("values_done"), (g + 1) * HEADS)
                    if g >= 2:
                        wait_job(dve, ("out_t", g - 2))
                    chain(v.tensor_tensor(o_n[:, g % 2, :].rearrange("p (h d) -> p h d", d=HD),
                                          bank[g % RING][:, :].rearrange("p (h d) -> p h d", d=HD),
                                          mx[:, g, :].unsqueeze(2).broadcast_to([P, HEADS, HD]), ALU.mult),
                          S("outs_made"))

            def mix(first, stage, gates, hi, lo, gates_before):
                for m in range(NK + 1):
                    if m < NK:
                        c = first + m
                        dve.wait_ge(chunk_done, c + 1)
                        dve.wait_ge(S("gate_made"), gates_before + 2 * NK)
                        if m >= 2:
                            dve.wait_ge(S(f"hi_{stage}"), m - 1)
                        chain(v.tensor_tensor(mixb[:, m % 2, :], out_bank(c)[:, :], gates[:, 0, m, :], ALU.mult))
                        chain(v.tensor_tensor(mixt[:, m % 2, :], side[c % 4][:, :], gates[:, 1, m, :], ALU.mult), chunk_freed)
                        chain(v.tensor_tensor(mixb[:, m % 2, :], mixb[:, m % 2, :], mixt[:, m % 2, :], ALU.add),
                              S(f"mixed_{stage}"))
                    if m >= 1:
                        second(stage, hi, lo, m - 1, mixb[:, (m - 1) % 2, :], None)

            mix(C_BR, "out", sg, actA_hi, actA_lo, 0)
            for m in range(NK + 1):
                if m < NK:
                    dve.wait_ge(chunk_done, C_OUT + m + 1)
                    chain(v.tensor_tensor(xT[:, m, :], xT[:, m, :], out_bank(C_OUT + m)[:, :], ALU.add), chunk_freed)
                if m >= 1:
                    second("mlp", actB_hi, actB_lo, m - 1, xT[:, m - 1, :], g_mlp)
                    add_squares(NK + m - 1, m - 1)
            for q in range(QUARTERS):
                up = C_MLP + 2 * NK * q
                for m in range(NK + 1):
                    if m < NK:
                        dve.wait_ge(chunk_done, up + m + 1)
                        if NK * q + m >= 2:
                            dve.wait_ge(S("u_made"), NK * q + m - 1)
                        chain(v.tensor_scalar(relu_u[:, m % 2, :], out_bank(up + m)[:, :], 0.0, None, ALU.max), chunk_freed)
                    if m >= 1:
                        second(f"u{q}", actA_hi, actA_lo, m - 1, u_sq[:, (m - 1) % 2, :], None)
                if q == 0:
                    refine(side_of("sum1")[:, :], freed=freed)
                    chain(v.tensor_tensor(rs[:, :], rs[:, :], rs[:, :], ALU.mult))
                for m in range(NK + 1):
                    c = up + NK + m
                    if m < NK:
                        dve.wait_ge(chunk_done, c + 1)
                        chain(v.tensor_tensor(ytmp[:, :], out_bank(c)[:, :], rs[:, :], ALU.mult), chunk_freed)
                        chain(v.tensor_tensor(xT[:, m, :], xT[:, m, :], ytmp[:, :], ALU.add),
                              S("x1_made") if q == QUARTERS - 1 else None)
                    if m >= 1 and q == QUARTERS - 1:
                        second("in2", actB_hi, actB_lo, m - 1, xT[:, m - 1, :], g_fin1)
                        add_squares(2 * NK + 2 * (m - 1), m - 1)
                        add_squares(2 * NK + 2 * (m - 1) + 1, m - 1, ssum2)
            refine(side_of("sum2")[:, :], rsf[:, :], freed=freed)
            wait_job(dve, "sum3")
            chain(v.tensor_tensor(ssum2[:, :], side_of("sum3")[:, :], rsf[:, :], ALU.mult), freed)
            chain(v.tensor_tensor(ssum2[:, :], ssum2[:, :], rsf[:, :], ALU.mult), S("second_sum"))
            refine(ssum2[:, :])
            chain(v.tensor_tensor(rs[:, :], rs[:, :], rsf[:, :], ALU.mult))

            take(C_IN2, alow[:, :])
            chain(v.memset(go[:, :], 1.0))
            chain(v.memset(go[:, :].rearrange("p (c t) -> p c t", t=CHUNK)[:, :, 0:1], 0.0), S("alow_made"))
            for j in range(2):
                take(C_IN2 + 1 + j, qs[:, j, :])
            for j in range(2):
                take(C_IN2 + 3 + j, ks[:, j, :])
            for j in range(2):
                wait_job(dve, ("z", j))
                chain(v.tensor_scalar(zs[:, j, :], side_of(("z", j))[:, :], b_alpha[:, j:j + 1], None, ALU.add), freed)
            for m in range(NK):
                chain(v.scalar_tensor_tensor(xT[:, m, :], xT[:, m, :], g_fin[:, m:m + 1], rsf[:, :], ALU.mult, ALU.mult))
            for h in range(GH):
                take(C_IN2 + 5 + h, gvT[:, h, :])
            by_chunk = lambda t: t.rearrange("p (c t) -> p c t", t=CHUNK)
            for j in range(2):
                dve.wait_ge(S("log_made"), j + 1)
                chain(v.scalar_tensor_tensor(zs[:, j, :], zs[:, j, :], 0.0, az[:, j, :], ALU.min, ALU.subtract))
                chain(v.tensor_tensor_scan(cs[:, j, :], go[:, :], zs[:, j, :], 0.0, ALU.mult, ALU.add), S("decay_summed"))
            for j in range(2):
                dve.wait_ge(S("decays"), 2 * (j + 1))
                chain(v.tensor_copy(dec[:, j, :], by_chunk(az[:, j, :])[:, :, CHUNK - 1]))
                chain(v.scalar_tensor_tensor(qdec[:, j, :], qs[:, j, :], CHUNK ** -0.5, az[:, j, :], ALU.mult, ALU.mult))
                chain(v.tensor_tensor(kdec[:, j, :], ks[:, j, :], zs[:, j, :], ALU.mult))
                last = by_chunk(cs[:, j, :])[:, :, CHUNK - 1:CHUNK]
                chain(v.tensor_copy(top8[:, 0, :], last.rearrange("p c t -> p (c t)")))
                chain(v.tensor_tensor(by_chunk(cs[:, j, :]), top8[:, 0, :].unsqueeze(2).broadcast_to([P, NCH, CHUNK]),
                                      by_chunk(cs[:, j, :]), ALU.subtract), S("decay_left"))
            for j in range(2):
                dve.wait_ge(S("decays"), 5 + j)
                chain(v.tensor_tensor(kend[:, j, :], ks[:, j, :], cs[:, j, :], ALU.mult), S("kend_made"))
            for h in range(GH):
                take(C_IN2 + 9 + h, rsil[:, h, :])
                dve.wait_ge(S("r_sigmoid"), h + 1)
                chain(v.tensor_tensor(rsil[:, h, :], rsil[:, h, :], pool_t[:, h % 2, :], ALU.mult), S("r_silu"))
            inv = const("inv_count")
            for g, win in enumerate(WINDOWS):
                take(C_IN2 + 13 + g, diff[:, g, :])
                src, step, n = diff[:, g, :], 1, 0
                while step < win:
                    dst = pool_t[:, n % 2, :]
                    chain(v.tensor_copy(dst[:, 0:step], src[:, 0:step]))
                    chain(v.tensor_tensor(dst[:, step:], src[:, step:], src[:, 0:L - step], ALU.add))
                    src, step, n = dst, 2 * step, n + 1
                chain(v.tensor_tensor(src[:, 0:16], src[:, 0:16], inv[:, 16 * g:16 * g + 16], ALU.mult))
                chain(v.tensor_scalar(src[:, 16:], src[:, 16:], 1.0 / win, None, ALU.mult))
                chain(v.tensor_tensor(diff[:, g, :], src, diff[:, g, :], ALU.subtract), S("diff_made"))
            for n in range(NCH - 1):
                wait_job(dve, ("inc", n))
                for j in range(2):
                    for e in range(2):
                        rows = slice(HD * e, HD * (e + 1))
                        inc = side_of(("inc", n))[rows, 256 * j + DV * e:256 * j + DV * (e + 1)]
                        done = freed if (j, e) == (1, 1) else None
                        if n == 0:
                            chain(v.tensor_copy(gst[rows, j, 1, :], inc), done)
                        else:
                            chain(v.scalar_tensor_tensor(gst[rows, j, n + 1, :], gst[rows, j, n, :],
                                                         dec[rows, j, n:n + 1], inc, ALU.mult, ALU.add), done)
            for h in range(GH):
                wait_job(dve, ("scores", h))
                chain(v.tensor_tensor(scT[:, h, :].rearrange("p (j t) -> p j t", t=P),
                                      side_of(("scores", h))[:, :].rearrange("p (j t) -> p j t", t=P),
                                      const("pair_causal").unsqueeze(1).broadcast_to([P, NT, P]), ALU.mult), freed)

            def gate(c):
                j = c - C_IN2 - 17
                take(c, sg2[:, j // NK, j % NK, :])

            for c in range(C_IN2 + 17, C_IN2 + 21):
                gate(c)
            for h in range(GH):
                wait_job(dve, ("o", h))
                dve.wait_ge(S("o_squares"), h + 1)
                if h:
                    dve.wait_ge(S("ready_branch2"), h)
                chain(v.tensor_copy(o_s[:, :], side_of(("o", h))[:, :]), freed)
                gate(C_IN2 + 21 + h)
                refine(side_of(("o_sum", h))[:, :], rs_o[:, :], DV, freed=freed)
                chain(v.scalar_tensor_tensor(o_s[:, :], o_s[:, :], g_gla[:, h:h + 1], rs_o[:, :], ALU.mult, ALU.mult),
                      S("o_sum_taken"))
                chain(v.tensor_tensor(o_s[:, :], o_s[:, :], rsil[:, h, :], ALU.mult), S("o_normed"))
                second("branch2", actA_hi, actA_lo, h, o_s[:, :], None)
            for g in range(4):
                wait_job(dve, ("pool", g))
                if g >= 2:
                    dve.wait_ge(S("ready_branch2"), 4 + g - 1)
                chain(v.tensor_scalar(pool_t2[:, g % 2, :], side_of(("pool", g))[:, :], p_scale[:, g:g + 1], None, ALU.mult), freed)
                second("branch2", actA_hi, actA_lo, 4 + g, pool_t2[:, g % 2, :], None)
            for c in range(C_IN2 + 25, C_IN2 + 33):
                gate(c)
            mix(C_BR2, "out2", sg2, actB_hi, actB_lo, 2 * NK)
            for m in range(NK + 1):
                if m < NK:
                    dve.wait_ge(chunk_done, C_OUT2 + m + 1)
                    chain(v.tensor_tensor(xT[:, m, :], xT[:, m, :], out_bank(C_OUT2 + m)[:, :], ALU.add), chunk_freed)
                    chain(v.tensor_scalar(h2T[:, m, :], xT[:, m, :], g_n2[:, m:m + 1], None, ALU.mult), S("h2_made"))
                if m >= 1:
                    add_squares(m - 1, m - 1, None, "sq4_made", "sum4_added")

            chain(v.memset(tabi[:, :, :], SKIP))
            refine(side_of("sum4")[:, 0:NT], gw[:, 13, :], D, gw[:, 14, :], gw[:, 15, :], freed=freed)
            chain(v.tensor_copy(gw[:, 12, :], gw[:, 13, :]), S("norm_made"))
            chain(v.tensor_copy(ones_r[:, :], ones[:, :]))
            chain(v.tensor_copy(earlier_r[:, :], const("earlier")))
            wait_job(dve, "route_t")
            chain(v.tensor_tensor(lg[:, :, :], side_of("route_t")[:, 0:NT * (NG + NE)].rearrange("p (t e) -> p t e", t=NT),
                                  gw[:, 13, :].unsqueeze(2).broadcast_to([P, NT, NG + NE]), ALU.mult), freed)
            chain(v.tensor_tensor(lg[:, :, :], lg[:, :, :], brt[:, :].unsqueeze(1).broadcast_to([P, NT, NG + NE]), ALU.add))

            def tile3(n, w):
                return rt[:, n, 0:NT * w].rearrange("p (t w) -> p t w", w=w)

            def spread(t, w):
                return t.unsqueeze(2).broadcast_to([P, NT, w])

            def first_largest(x, w, peak, down, to):
                chain(v.tensor_reduce(gw[:, peak, :], x, AX, ALU.max))
                chain(v.tensor_tensor(to, x, spread(gw[:, peak, :], w), ALU.is_equal))
                chain(v.tensor_tensor(to, to, down.unsqueeze(1).broadcast_to([P, NT, w]), ALU.mult))
                chain(v.tensor_reduce(gw[:, 15, :], to, AX, ALU.max))
                chain(v.tensor_tensor(to, to, spread(gw[:, 15, :], w), ALU.is_equal))

            group = tile3(2, NG)
            first_largest(lg[:, :, 0:NG], NG, 0, const("down4"), group)
            chain(v.tensor_tensor(tile3(0, NG), lg[:, :, 0:NG], spread(gw[:, 0, :], NG), ALU.subtract), S("group_shifted"))
            own = rt[:, 3, :].rearrange("p (t e g) -> p t e g", t=NT, g=NG)
            chain(v.tensor_tensor(own, lg[:, :, NG:].rearrange("p t (g e) -> p t e g", e=EPG),
                                  group.unsqueeze(2).broadcast_to([P, NT, EPG, NG]), ALU.mult))
            logit = tile3(4, EPG)
            chain(v.tensor_reduce(logit, own, AX, ALU.add))
            one, two = tile3(5, EPG), tile3(7, EPG)
            first_largest(logit, EPG, 4, const("down8"), one)
            chain(v.scalar_tensor_tensor(tile3(6, EPG), one, -1.0e38, logit, ALU.mult, ALU.add))
            first_largest(tile3(6, EPG), EPG, 5, const("down8"), two)
            chain(v.tensor_tensor(gw[:, 6, :], gw[:, 5, :], gw[:, 4, :], ALU.subtract), S("expert_shifted"))
            M = [rt[:, 8 + k, :].rearrange("p (t g e) -> p t g e", t=NT, g=NG) for k in range(2)]
            for k, pick in enumerate((one, two)):
                chain(v.tensor_tensor(M[k], group.unsqueeze(3).broadcast_to([P, NT, NG, EPG]),
                                      pick.unsqueeze(2).broadcast_to([P, NT, NG, EPG]), ALU.mult))
            chain(v.tensor_tensor(picks_r[:, :, :].rearrange("p t e -> p (t e)"), rt[:, 8, :], rt[:, 9, :], ALU.add), S("picks_made"))
            dve.wait_ge(S("group_exp"), 1)
            chain(v.tensor_reduce(gw[:, 1, :], tile3(0, NG), AX, ALU.add))
            chain(v.reciprocal(gw[:, 2, :], gw[:, 1, :]))
            dve.wait_ge(S("expert_exp"), 1)
            chain(v.tensor_scalar(gw[:, 7, :], gw[:, 6, :], 1.0, None, ALU.add))
            chain(v.reciprocal(gw[:, 8, :], gw[:, 7, :]))
            chain(v.tensor_tensor(gw[:, 10, :], gw[:, 2, :], gw[:, 8, :], ALU.mult))
            chain(v.tensor_tensor(gw[:, 11, :], gw[:, 10, :], gw[:, 6, :], ALU.mult))
            wait_job(dve, "places")
            pos, q_, t1, sl = (rt[:, n, :] for n in (0, 2, 3, 4))
            cnt, o_e, o_in, o_at = (rt[:, 5, NE * n:NE * (n + 1)] for n in range(4))
            chain(v.tensor_copy(cnt, side_of("places")[:, NT * NE:NT * NE + NE]))
            chain(v.tensor_copy(pos, side_of("places")[:, 0:NT * NE]), freed)

            iota_e = const("iota")[:, 0:NE]

            def blocks_past(to, x, least):
                chain(v.tensor_scalar(to, x, float(P + least), None, ALU.is_ge))
                for n in (2, 3):
                    chain(v.scalar_tensor_tensor(to, x, float(n * P + least), to, ALU.is_ge, ALU.add))

            blocks_past(q_, pos, 0)
            blocks_past(o_e, cnt, 1)
            chain(v.tensor_tensor_scan(o_in, ones[:, 0:NE], o_e, 0.0, ALU.mult, ALU.add))
            chain(v.tensor_tensor(o_at, o_in, o_e, ALU.subtract))
            chain(v.tensor_tensor(o_at, o_at, iota_e, ALU.subtract))
            chain(v.tensor_scalar(o_at, o_at, float(NE - 1), None, ALU.add))
            by_e = lambda t: t.rearrange("p (t e) -> p t e", e=NE)
            over_e = lambda t: t.unsqueeze(1).broadcast_to([P, NT, NE])
            chain(v.tensor_tensor(by_e(t1), by_e(q_), over_e(o_at), ALU.add))
            chain(v.scalar_tensor_tensor(t1, q_, 1.0, t1, ALU.min, ALU.mult))
            chain(v.tensor_tensor(by_e(t1), by_e(t1), over_e(iota_e), ALU.add))
            in_blk = rt[:, 10:12, :].rearrange("p a b -> p (a b)")[:, 0:NT * NB].rearrange("p (t b) -> p t b", b=NB)
            chain(v.scalar_tensor_tensor(sl, q_, -float(P), pos, ALU.mult, ALU.add))
            every = lambda x, w: x.unsqueeze(2).broadcast_to([P, NT, w])
            for k in range(2):
                pick = rt[:, 8 + k, :]
                for x, to in ((sl, 3), (t1, 9)):
                    chain(v.tensor_tensor(rt[:, 6, :], x, pick, ALU.mult))
                    chain(v.tensor_reduce(gw[:, to, :], by_e(rt[:, 6, :]), AX, ALU.add))
                if k:
                    dve.wait_ge(S("table_half"), 1)
                chain(v.tensor_tensor(at_row[:, :, :], const("iota").unsqueeze(1).broadcast_to([P, NT, P]),
                                      every(gw[:, 3, :], P), ALU.is_equal))
                chain(v.tensor_tensor(in_blk, const("iota")[:, 0:NB].unsqueeze(1).broadcast_to([P, NT, NB]),
                                      every(gw[:, 9, :], NB), ALU.is_equal))
                chain(v.tensor_tensor(in_block[:, :, :], in_blk, every(const("row_id")[:, NT * k:NT * (k + 1)], NB),
                                      ALU.mult), S("picks_placed"))
            wait_job(dve, "table")
            ids = rt[:, 0, 0:NB]
            chain(v.tensor_copy(ids, side_of("table")[:, 0:NB]), freed)
            chain(v.tensor_scalar(rt[:, 2, 0:NB], ids, 0.0, float(SKIP), ALU.is_equal, ALU.mult))
            chain(v.scalar_tensor_tensor(ids, ids, -1.0, rt[:, 2, 0:NB], ALU.add, ALU.add))
            chain(v.tensor_copy(tabi[:, 0, 0:NB], ids))
            chain(v.tensor_scalar(rt[:, 2, 0:NB], ids, float(L), -float(L), ALU.is_ge, ALU.mult))
            chain(v.tensor_tensor(ids, ids, rt[:, 2, 0:NB], ALU.add))
            chain(v.tensor_copy(tabi[:, 1, 0:NB], ids), S("rows_ready"))
            below = rt[0:1, 6, :].rearrange("p (j e) -> p j e", e=NE)
            for part in range(2):
                w = OVER // 2
                chain(v.tensor_tensor(below[:, 0:w, :], o_in[0:1, :].unsqueeze(1).broadcast_to([1, w, NE]),
                                      const("iota", 1)[:, part * w:(part + 1) * w].unsqueeze(2).broadcast_to([1, w, NE]),
                                      ALU.is_le))
                chain(v.tensor_reduce(rt[0:1, 7, part * w:(part + 1) * w], below[:, 0:w, :], AX, ALU.add))
            chain(v.tensor_scalar(rt[0:1, 7, 0:OVER], rt[0:1, 7, 0:OVER], float(NE - 1), None, ALU.min))
            chain(v.tensor_copy(over_n[0:1, 1:1 + OVER], rt[0:1, 7, 0:OVER]))
            chain(v.tensor_copy(over_n[0:1, 0:1], o_in[0:1, NE - 1:NE]), S("over_ready"))
            def x_turned(i, u):
                dve.wait_ge(S("xe_used"), at(i, u, 2))
                wait_from(dve, S("gate_up_done"), i, u, 0)
                v.tensor_copy(xeT[:, (u + 1) % 2, L:], side[1][:, :]).then_inc(S("xe_t_by_dve"), 1)

            def hidden(i, u):
                dve.wait_ge(S("silu_made"), at(i, u, 1))
                v.tensor_tensor(hid[:, u % 2, :], hid[:, u % 2, :], bank[u % 2][:, DE:], ALU.mult)\
                    .then_inc(S("hid_made"), 1)

            def hidden_turned(i, u):
                dve.wait_ge(S("hid_turned"), at(i, u, 1))
                wait_from(dve, S("down_done"), i, u, -1)
                v.tensor_copy(hidT[:, u % 2, :], side[2][:, 0:DE]).then_inc(S("hid_t_made"), 1)

            def y_out(i, u):
                dve.wait_ge(S("down_done"), at(i, u, 1))
                if i is not None or u >= 2:
                    dve.wait_ge(S(f"scattered{u % 2}"), 16 * (u // 2) if i is None else 32 * i + 16 * (u // 2))
                v.tensor_copy(ye[:, u % 2, L:], bank[3][:, :]).then_inc(S("y_by_dve"), 1)

            def expert(i, u):
                if i is not None or u > 0:
                    hidden_turned(*before(i, u))
                hidden(i, u)
                x_turned(i, u)
                if i is not None or u > 0:
                    y_out(*before(i, u))

            def last():
                hidden_turned(*LAST)
                y_out(*LAST)

            def overflow(i, u):
                hidden(i, u)
                x_turned(i, u)
                hidden_turned(i, u)
                y_out(i, u)

            dve.wait_ge(S("xe_used"), 1)
            v.tensor_copy(xeT[:, 0, L:], side[1][:, :]).then_inc(S("xe_t_by_dve"), 1)
            for_experts(dve, expert, last, overflow)

            wait_freed(dve, ("resid", NT - 1, 1))
            dve.wait_ge(S("gain_in"), 16)
            for i in range(NT + 1):
                if i < NT:
                    t = x_res[:, i, :]
                    dve.wait_ge(S(f"y2_in{i}"), 16)
                    chain(v.scalar_tensor_tensor(t, y2[:, i, 0:D], gw[:, 10, i:i + 1], t, ALU.mult, ALU.add))
                    chain(v.scalar_tensor_tensor(t, y2[:, i, D:], gw[:, 11, i:i + 1], t, ALU.mult, ALU.add), S("final_sum"))
                if i >= 1:
                    t, one = x_res[:, i - 1, :], slice(i - 1, i)
                    refine(gw[:, 12, one], gw[:, 13, one], D, gw[:, 14, one], gw[:, 15, one])
                    chain(v.scalar_tensor_tensor(t, t, gw[:, 13, one], gfin[:, :], ALU.mult, ALU.mult), S("final_out"))

        @block.tensor
        def _(pe):
            mm = nc.tensor.matmul

            def open_job(name):
                i = jobs.at[name]
                if i >= 4:
                    pe.wait_ge(side_freed[jobs.freer[i - 4]], jobs.freed[i - 4])
                return side[i % 4]

            def close_job(ins):
                ins.then_inc(side_full, 1)

            def chunk(slot, done, hi, lo, ready, counts, two, free):
                pe.wait_ge(lo_made, done)
                if free is not None:
                    pe.wait_ge(chunk_freed, free)
                for k in range(NK):
                    pe.wait_ge(ready, counts[k])
                    b = side[slot] if two and k >= 4 else bank[slot]
                    w_hi, w_lo = (w[:, slot, k * P:(k + 1) * P] for w in (whi, wlo))
                    first, last = k in ((0, 4) if two else (0,)), k in ((3, 7) if two else (7,))
                    mm(b[:, :], w_hi, hi[:, k, :], start=first, stop=False)
                    mm(b[:, :], w_hi, lo[:, k, :], start=False, stop=False)
                    ins = mm(b[:, :], w_lo, hi[:, k, :], start=False, stop=last)
                ins.then_inc(chunk_done, 1)

            def chunks(first, n, hi, lo, ready, counts=tuple(range(1, NK + 1)), two=False):
                if n % RING or first < RING:
                    for c in range(first, first + n):
                        chunk(c % RING, c + 1, hi, lo, ready, counts, two, c - RING + 1 if c >= RING else None)
                    return
                with pe.Fori(0, n // RING) as i:
                    for u in range(RING):
                        chunk((first + u) % RING, RING * i + (first + u + 1), hi, lo, ready, counts, two,
                              RING * i + (first + u - RING + 1))

            def turn(dst, src, last=False):
                return nc.tensor.transpose(dst, src, ident[0:src.shape[0], 0:src.shape[0]])

            def total(name, src, sem, count):
                pe.wait_ge(sem, count)
                close_job(mm(open_job(name)[:, :], ones[:, :], src, start=True, stop=True))

            pe.wait_ge(S("x_in"), 16 * (NT + 1))
            pe.wait_ge(S("ones_set"), 1)
            for k in range(NK):
                b = open_job(("x_t", k))
                for i in range(NT):
                    ins = turn(b[:, i * P:(i + 1) * P], x_tok[:, i, k * P:(k + 1) * P])
                close_job(ins)

            inA = (actA_hi, actA_lo, S("ready_in"))
            chunks(C_IN, 1, *inA)
            total("sum0", ssum[:, :], S("sum_added"), NK)
            chunks(1, 4, *inA)
            b = open_job("ik_tok")
            pe.wait_ge(chunk_freed, 1)
            for t in range(NT):
                ins = turn(b[:, t * P:(t + 1) * P], ik_s[:, t * P:(t + 1) * P])
            close_job(ins)
            chunks(5, 8, *inA)
            pe.wait_ge(chunk_freed, 13)
            for n, br in enumerate("ab"):
                b = open_job(("v_tok", br))
                for t in range(NT):
                    ins = turn(b[:, t * P:(t + 1) * P], vT[:, n, t * P:(t + 1) * P])
                close_job(ins)
            b = open_job("ik_t")
            pe.wait_ge(S("ik_roped"), 2)
            for t in range(NT):
                ins = turn(b[:, t * P:(t + 1) * P], ikrope[:, t, :])
            close_job(ins)
            chunks(13, 4, *inA)
            wait_freed(pe, "ik_t")
            pe.wait_ge(S("roped"), 4)
            for qt in range(1, NT):
                for h in range(HEADS):
                    rows = slice(HD * (h % 2), HD * (h % 2 + 1))
                    b = open_job(("index", qt, h))
                    close_job(mm(b[:, 0:(qt + 1) * P], iqT[rows, h // 2, qt * P:(qt + 1) * P],
                                 ikT[rows, 0:(qt + 1) * P], start=True, stop=True))
            chunks(17, 16, *inA)

            pe.wait_ge(S("roped"), len(ROPED))
            wait_freed(pe, ("v_tok", "b"))
            pe.wait_ge(chunk_freed, C_BR)
            for what, n in pe_attention():
                if what in ("logits", "probs_t", "values"):
                    br, qt, k0, nk, h = unit(n)
                    rows = slice(HD * (h % 2), HD * (h % 2 + 1))
                if what == "logits":
                    b = open_job((what, n))
                    close_job(mm(b[:, 0:nk * P], qT[br][rows, h // 2, qt * P:(qt + 1) * P],
                                 kT[br][rows, h // REP, k0 * P:(k0 + nk) * P], start=True, stop=True))
                elif what == "probs_t":
                    b = open_job((what, n))
                    pe.wait_ge(S("probs_made"), n + 1)
                    for j in range(nk):
                        ins = turn(b[:, j * P:(j + 1) * P], pbuf[:, n % 3, j * P:(j + 1) * P])
                    close_job(ins)
                elif what == "values":
                    g = n // HEADS
                    wait_freed(pe, ("probs_t", n))
                    if g >= RING and h == 0:
                        pe.wait_ge(S("outs_made"), g - RING + 1)
                    for j in range(nk):
                        ins = mm(bank[g % RING][:, h * HD:(h + 1) * HD], pT[:, n % 2, j * P:(j + 1) * P],
                                 v_tok[br][:, k0 + j, HD * (h // REP):HD * (h // REP + 1)],
                                 start=j == 0, stop=j == nk - 1)
                    ins.then_inc(S("values_done"), 1)
                else:
                    b = open_job((what, n))
                    pe.wait_ge(S("outs_made"), n + 1)
                    for f in range(4):
                        ins = turn(b[:, f * P:(f + 1) * P], o_n[:, n % 2, f * P:(f + 1) * P])
                    close_job(ins)

            wait_freed(pe, ("out_t", 2 * NT - 1))
            wait_freed(pe, ("probs_t", UNITS - 1))
            chunks(C_BR, NK, actB_hi, actB_lo, side_freed["dve"],
                   [jobs.freed[jobs.at[("out_t", 2 * NT - 1)]]] * NK, two=True)
            chunks(C_OUT, NK, actA_hi, actA_lo, S("ready_out"))
            for q in range(QUARTERS):
                chunks(C_MLP + 2 * NK * q, NK, actB_hi, actB_lo, S("ready_mlp"))
                if q == 0:
                    pe.wait_ge(chunk_freed, C_OUT)
                    total("sum1", ssum[:, :], S("sum_added"), 2 * NK)
                chunks(C_MLP + 2 * NK * q + NK, NK, actA_hi, actA_lo, S(f"ready_u{q}"))
            total("sum2", ssum[:, :], S("sum_added"), 4 * NK)
            total("sum3", ssum2[:, :], S("sum_added"), 4 * NK)

            inB = (actB_hi, actB_lo, S("ready_in2"))
            chunks(C_IN2, 1, *inB)
            chunks(C_IN2 + 1, 4, *inB)
            pe.wait_ge(S("small2_in"), 32)
            pe.wait_ge(S("alow_made"), 1)
            for j in range(2):
                b = open_job(("z", j))
                close_job(mm(b[:, :], wal[:, j * P:(j + 1) * P], alow[:, :], start=True, stop=True))
            chunks(C_IN2 + 5, 4, *inB)
            pe.wait_ge(chunk_freed, C_IN2 + 9)
            for h in range(GH):
                b = open_job(("gv_tok", h))
                for t in range(NT):
                    ins = turn(b[:, t * P:(t + 1) * P], gvT[:, h, t * P:(t + 1) * P])
                close_job(ins)
            chunks(C_IN2 + 9, 4, *inB)
            chunks(C_IN2 + 13, 4, *inB)
            pe.wait_ge(S("kend_made"), 2)
            for j in range(2):
                b = open_job(("kend_tok", j))
                for t in range(NT):
                    ins = turn(b[:, t * P:(t + 1) * P], kend[:, j, t * P:(t + 1) * P])
                close_job(ins)
            wait_freed(pe, ("kend_tok", 1))
            for n in range(NCH - 1):
                b = open_job(("inc", n))
                rows = slice(CHUNK * (n % 2), CHUNK * (n % 2 + 1))
                for j in range(2):
                    ins = mm(b[:, 256 * j:256 * (j + 1)], kend_tok[rows, n // 2, j * P:(j + 1) * P],
                             gv_tok[rows, n // 2, 256 * j:256 * (j + 1)], start=True, stop=True)
                close_job(ins)
            for h in range(GH):
                b = open_job(("scores", h))
                rows = slice(HD * (h % 2), HD * (h % 2 + 1))
                for t in range(NT):
                    cols = slice(t * P, (t + 1) * P)
                    ins = mm(b[:, cols], kdec[rows, h // 2, cols], qdec[rows, h // 2, cols], start=True, stop=True)
                close_job(ins)
            chunks(C_IN2 + 17, 4, *inB)
            wait_freed(pe, ("scores", GH - 1))
            for h in range(GH):
                b = open_job(("o", h))
                rows = slice(HD * (h % 2), HD * (h % 2 + 1))
                for t in range(NT):
                    cols = slice(t * P, (t + 1) * P)
                    mm(b[:, cols], gv_tok[:, t, h * DV:(h + 1) * DV], scT[:, h, cols], start=True, stop=False)
                    for n in range(2 * t, 2 * t + 2):
                        if n:
                            at_ = slice(n * CHUNK, (n + 1) * CHUNK)
                            ins = mm(b[:, at_], gst[rows, h // 2, n, :], qdec[rows, h // 2, at_], start=False, stop=n % 2 == 1)
                close_job(ins)
                chunks(C_IN2 + 21 + h, 1, *inB)
                total(("o_sum", h), sq[:, 0, :], S("o_squares"), h + 1)
            pe.wait_ge(S("diff_made"), 4)
            for g in range(4):
                close_job(mm(open_job(("pool", g))[:, :], pw[:, g, :], diff[:, g, :], start=True, stop=True))
            chunks(C_IN2 + 25, 8, *inB)
            wait_freed(pe, ("pool", 3))
            chunks(C_BR2, NK, actA_hi, actA_lo, S("ready_branch2"), two=True)
            inR = (actB_hi, actB_lo, S("ready_out2"))
            chunks(C_OUT2, 4, *inR)
            pe.wait_ge(S("route_in"), 16 * (NG + 3))
            b = open_job("route")
            for k in range(NK):
                if k == 3:
                    chunks(C_OUT2 + 4, 4, *inR)
                pe.wait_ge(S("h2_made"), k + 1)
                ins = mm(b[0:NG + NE, :], wr[:, k, :], h2T[:, k, :], start=k == 0, stop=k == NK - 1)
            close_job(ins)

            b = open_job("sum4")
            pe.wait_ge(S("sum4_added"), NK)
            for i in range(NT):
                ins = mm(b[:, i:i + 1], ssum[:, i * P:(i + 1) * P], ones[:, 0:1], start=True, stop=True)
            close_job(ins)
            b = open_job("route_t")
            wait_freed(pe, "route")
            for i in range(NT):
                ins = turn(b[:, i * (NG + NE):(i + 1) * (NG + NE)], lgT[0:NG + NE, i * P:(i + 1) * P])
            close_job(ins)
            for i in range(NT):
                for n in range(2):
                    b = open_job(("rows", i, n))
                    for k in range(4):
                        ins = turn(b[:, k * P:(k + 1) * P], h2T[:, 4 * n + k, i * P:(i + 1) * P])
                    close_job(ins)
            b = open_job("places")
            pe.wait_ge(S("picks_made"), 1)
            for i in range(NT):
                for j in range(i + 1):
                    mm(b[:, i * NE:(i + 1) * NE], earlier_r[:, :] if j == i else ones_r[:, :], picks_r[:, j, :],
                       start=j == 0, stop=j == i)
            for j in range(NT):
                ins = mm(b[:, NT * NE:NT * NE + NE], ones_r[:, :], picks_r[:, j, :], start=j == 0, stop=j == NT - 1)
            close_job(ins)
            b = open_job("table")
            for k in range(2):
                pe.wait_ge(S("picks_placed"), k + 1)
                for i in range(NT):
                    ins = mm(b[:, 0:NB], at_row[:, i, :], in_block[:, i, :], start=(k, i) == (0, 0), stop=(k, i) == (1, NT - 1))
                if k == 0:
                    ins.then_inc(S("table_half"), 1)
            close_job(ins)
            for i in range(NT):
                for n in range(2):
                    b = open_job(("resid", i, n))
                    for k in range(4):
                        ins = turn(b[:, k * P:(k + 1) * P], xT[:, 4 * n + k, i * P:(i + 1) * P])
                    close_job(ins)
            wait_freed(pe, "places")
            wait_freed(pe, ("resid", NT - 1, 1))

            def turn_rows(i, u):
                j = (u + 1) % RING
                pe.wait_ge(S(f"gathered{j}"), 16 * ((u + 1) // RING + 1) if i is None else
                           16 * i + 16 * ((u + 1) // RING + 1))
                wait_from(pe, S("xe_t_by_act"), i, u, 1)
                wait_from(pe, S("xe_t_by_dve"), i, u, 1)
                for k in range(NK):
                    ins = turn(side[k // 4][:, (k % 4) * P:(k % 4 + 1) * P], xe[:, j, k * P:(k + 1) * P])
                ins.then_inc(S("xe_used"), 1)

            def gate_up(i, u):
                j = u % 2
                pe.wait_ge(S(f"expert_in{u}"), 48 if i is None else 48 * i + 48)
                pe.wait_ge(S("xe_t_by_act"), at(i, u, 1))
                pe.wait_ge(S("xe_t_by_dve"), at(i, u, 1))
                wait_from(pe, S("hid_made"), i, u, -1)
                for k in range(NK):
                    ins = mm(bank[j][:, :], xeT[:, j, k * P:(k + 1) * P], wring[:, u, k * 2 * DE:(k + 1) * 2 * DE],
                             start=k == 0, stop=k == NK - 1)
                ins.then_inc(S("gate_up_done"), 1)

            def turn_hidden(i, u):
                j = u % 2
                pe.wait_ge(S("hid_made"), at(i, u, 1))
                wait_from(pe, S("hid_t_made"), i, u, 0)
                for k in range(2):
                    ins = turn(side[2][:, k * P:(k + 1) * P], hid[:, j, k * P:(k + 1) * P])
                ins.then_inc(S("hid_turned"), 1)

            def down(i, u):
                j = u % 2
                pe.wait_ge(S("hid_t_made"), at(i, u, 1))
                wait_from(pe, S("y_by_act"), i, u, 0)
                wait_from(pe, S("y_by_dve"), i, u, 0)
                for n in range(2):
                    for k in range(2):
                        ins = mm(bank[2 + n][:, :], hidT[:, j, k * P:(k + 1) * P],
                                 wring[:, u, 4 * D + k * D + n * L:4 * D + k * D + (n + 1) * L],
                                 start=k == 0, stop=k == 1)
                ins.then_inc(S("down_done"), 1)

            def expert(i, u):
                gate_up(i, u)
                if i is not None or u > 0:
                    turn_hidden(*before(i, u))
                turn_rows(i, u)
                if i is not None or u > 0:
                    down(*before(i, u))

            def last():
                turn_hidden(*LAST)
                down(*LAST)

            def overflow(i, u):
                gate_up(i, u)
                turn_rows(i, u)
                turn_hidden(i, u)
                down(i, u)

            turn_rows(None, -1)
            for_experts(pe, expert, last, overflow)


def kernel(**inputs):
    import numpy as _np
    import concourse.bacc as _bacc
    from concourse import mybir as _mybir
    from concourse.bass_utils import run_bass_kernel_spmd as _run

    f = _np.float32
    t, u = _np.arange(P)[:, None], _np.arange(P)[None, :]
    inv = (f(1.0) / (f(10000.0) ** (_np.arange(0, HD, 2, dtype=f) / f(HD)))).astype(f)
    angle = (_np.arange(L, dtype=f)[:, None] * inv[None, :]).astype(f)
    cos, sin = _np.cos(angle), _np.sin(angle)
    count = _np.concatenate([1.0 / _np.minimum(_np.arange(16) + 1.0, w) for w in WINDOWS])
    rows = lambda a: _np.broadcast_to(a, (P, a.shape[-1]))
    parts = {
        "ident": t == u, "causal": _np.where(u <= t, 0.0, NEG), "before": _np.where(u > t, 0.0, NEG),
        "earlier": t < u, "pair_causal": (t <= u) & (t // CHUNK == u // CHUNK),
        "cos": _np.tile(cos.T, (4, 1)), "sin": _np.tile(sin.T, (4, 1)),
        "cos_tok": cos.reshape(NT, P, 32).transpose(1, 0, 2).reshape(P, -1),
        "sin_tok": sin.reshape(NT, P, 32).transpose(1, 0, 2).reshape(P, -1),
        "inv_count": rows(count[None]), "iota": rows(_np.arange(P)[None]),
        "down4": rows(_np.arange(NG, 0, -1)[None]), "down8": rows(_np.arange(EPG, 0, -1)[None]),
        "row_id": _np.arange(1, 2 * L + 1).reshape(2 * NT, P).T,
    }
    consts = _np.concatenate([parts[n].astype(f) for n in CONST_COLS], axis=1)

    nc = _bacc.Bacc("TRN2", target_bir_lowering=False, num_devices=1)
    arrays, args = {}, {}
    for name, a in (*inputs.items(), ("consts", consts)):
        a = _np.ascontiguousarray(a)
        arrays[f"in_{name}"] = a
        args[name] = nc.dram_tensor(f"in_{name}", a.shape, _mybir.dt.from_np(a.dtype), kind="ExternalInput").ap()
    out = nc.dram_tensor("out", (L, D), _mybir.dt.float32, kind="ExternalOutput").ap()
    gated_blocks(nc, args, out)
    r = _run(nc, [arrays], core_ids=[0])
    return r.results[0]["out"].reshape(1, L, D)
```

```python
from contextlib import ExitStack

import concourse.bass as bass
from concourse import mybir

F32 = mybir.dt.float32
F32R = mybir.dt.float32r
I32 = mybir.dt.int32
ALU = mybir.AluOpType
ACT = mybir.ActivationFunctionType
AX = mybir.AxisListType.X

P = 128
L = 512
D = 1024
NT, NK = L // P, D // P
HD, HEADS, REP = 64, 8, 4
TOPK = 128
FF = 4 * D
QUARTERS = FF // D
DV, GH, CHUNK = 128, 4, 64
NCH = L // CHUNK
WINDOWS = (2, 4, 8, 16)
NG, EPG, NE, DE = 4, 8, 32, 256
ROWS = 96
OVER = 12
NB = NE + OVER
SKIP = 1 << 20
EPS = 1e-6
NEG = -1e30
TAKEN = -3.3e38
ATT_SCALE = HD ** -0.5
W_SCALE = HEADS ** -0.5 * HD ** -0.5

CONST_COLS = {}
_at = 0
for _name, _n in (("ident", P), ("before", P), ("causal", P), ("earlier", P), ("pair_causal", P),
                  ("cos", L), ("sin", L), ("cos_tok", NT * 32), ("sin_tok", NT * 32),
                  ("inv_count", 4 * 16), ("iota", P), ("down4", NG), ("down8", EPG), ("row_id", 2 * NT)):
    CONST_COLS[_name] = (_at, _at + _n)
    _at += _n
CONST_WIDTH = _at

RING = 4
AHEAD = 3
C_IN, C_BR, C_OUT, C_MLP = 0, 33, 41, 49
C_IN2 = C_MLP + QUARTERS * 2 * NK
C_BR2, C_OUT2 = C_IN2 + 33, C_IN2 + 41
N_CHUNKS = C_OUT2 + NK
IN1_GROUPS = ((1, 4, 768), (5, 4, 0), (9, 2, 512), (11, 2, 1864), (13, 4, 1352), (17, 16, 2120))
IN2_GROUPS = ((1, 4, 0), (5, 4, 512), (9, 4, 1024), (13, 4, 1552), (17, 16, 2064))


def unit(u):
    g = u // HEADS
    b, qt = ("b", g) if g < NT else ("a", g - NT)
    k0 = max(0, qt - 1) if b == "b" else 0
    return b, qt, k0, qt + 1 - k0, u % HEADS


UNITS = 2 * NT * HEADS
STEPS = UNITS + 8


def pe_attention():
    for s in range(STEPS):
        if s < UNITS:
            yield "logits", s
        if 2 <= s < UNITS + 2:
            yield "probs_t", s - 2
        if 3 <= s < UNITS + 3:
            yield "values", s - 3
        if s >= 14 and s % 8 == 6:
            yield "out_t", s // 8 - 1


class Jobs:

    def __init__(self):
        self.at, self.freer, self.freed, self.count = {}, [], [], {"dve": 0, "act": 0}

    def add(self, name, freer):
        self.at[name] = len(self.freer)
        self.count[freer] += 1
        self.freer.append(freer)
        self.freed.append(self.count[freer])

    def free_first(self, late, early):
        i, j = self.at[late], self.at[early]
        self.freed[i], self.freed[j] = self.freed[j], self.freed[i]


def job_table():
    jobs = Jobs()
    for k in range(NK):
        jobs.add(("x_t", k), "act")
    jobs.add("sum0", "dve")
    jobs.add("ik_tok", "dve")
    jobs.add(("v_tok", "a"), "act")
    jobs.add(("v_tok", "b"), "act")
    jobs.add("ik_t", "act")
    for qt in range(1, NT):
        for h in range(HEADS):
            jobs.add(("index", qt, h), "act")
    for what, n in pe_attention():
        if what != "values":
            jobs.add((what, n), "act" if what == "probs_t" else "dve")
    for n in (1, 2, 3):
        jobs.add(f"sum{n}", "dve")
    for j in range(2):
        jobs.add(("z", j), "dve")
    for h in range(GH):
        jobs.add(("gv_tok", h), "act")
    for j in range(2):
        jobs.add(("kend_tok", j), "act")
    for n in range(NCH - 1):
        jobs.add(("inc", n), "dve")
    for h in range(GH):
        jobs.add(("scores", h), "dve")
    for g in range(4):
        jobs.add(("pool", g), "dve")
    for h in range(GH):
        jobs.add(("o", h), "dve")
        jobs.add(("o_sum", h), "dve")
    for h in range(1, GH):
        jobs.free_first(("o", h), ("o_sum", h - 1))
    jobs.add("route", "act")
    jobs.add("sum4", "dve")
    jobs.add("route_t", "dve")
    for i in range(NT):
        for n in range(2):
            jobs.add(("rows", i, n), "act")
    jobs.add("places", "dve")
    jobs.add("table", "dve")
    for i in range(NT):
        for n in range(2):
            jobs.add(("resid", i, n), "act")
    return jobs


def gated_blocks(nc, A, out):
    sems, stack = {}, ExitStack()

    def S(name):
        if name not in sems:
            sems[name] = stack.enter_context(nc.semaphore(name))
        return sems[name]

    with stack:
        base = nc.sbuf_base() if callable(nc.sbuf_base) else nc.sbuf_base
        base = -(-base // 64) * 64

        def place(name, shape, offset, dt=F32):
            return nc.alloc_sbuf_tensor_at(name, shape, dt, offset=offset)

        def words(shape):
            n = 4
            for s in shape[1:]:
                n *= s
            return -(-n // 32) * 32

        def lay(at, *tensors):
            made = []
            for name, shape, *dt in tensors:
                made.append(place(name, shape, at, *dt))
                at += words(shape)
            return (*made, at)

        (con, small, ones, eps_t, rs, ssum, sq, nt0, ikstat, ikmv, ikr, iw, sinkb, top8, lnwb,
         mx, nm, den, es, xT, top) = lay(
            base, ("con", [P, CONST_WIDTH]), ("small", [P, 64]), ("ones", [P, P]), ("eps_t", [P, 1]),
            ("rs", [P, L]), ("ssum", [P, L]), ("sq", [P, 2, L]), ("nt0", [P, L]),
            ("ikstat", [P, NT, 6]), ("ikmv", [P, NT, 2]), ("ikr", [P, 4, NT]), ("iw", [P, NT, HEADS]),
            ("sinkb", [P, HEADS]), ("top8", [P, NT - 1, 8]), ("lnwb", [P, 2, HD]),
            ("mx", [P, 2 * NT, HEADS]), ("nm", [P, 2 * NT, HEADS]), ("den", [P, 2 * NT, HEADS]),
            ("es", [P, 2 * NT, HEADS]), ("xT", [P, NK, L]))
        KEEP_AT = {1: 0, 2: 2 * P, 3: 5 * P}
        keep = place("keep", [P, 9 * P], base + sum(words(x) for x in (
            [P, CONST_WIDTH], [P, 64], [P, P], [P, 1], [P, L], [P, L])))
        v_tok_a_at = base + sum(words(x) for x in ([P, CONST_WIDTH], [P, 64], [P, P], [P, 1], [P, L]))

        def const(name, rows=P):
            a, b = CONST_COLS[name]
            return con[0:rows, a:b]

        ident = const("ident")
        g_attn, g_mlp, g_fin, g_n1, g_n2 = (small[:, 8 * i:8 * i + 8] for i in range(5))
        b_alpha, g_gla, p_scale = small[:, 40:42], small[:, 42:46], small[:, 46:50]
        g_fin1 = small[:, 50:58]

        route_at = top - sum(words(x) for x in ([P, 2, HD], *[[P, 2 * NT, HEADS]] * 4, [P, NK, L]))
        wr, brt, route_end = lay(route_at, ("wr", [P, NK, NG + NE]), ("brt", [P, NG + NE]))
        assert route_end <= top - words([P, NK, L])

        raw, whi, wlo, a_at = lay(top, ("raw", [P, RING, D]), ("whi", [P, RING, D], F32R),
                                  ("wlo", [P, RING, D], F32R))
        actA_hi, actA_lo, b_at = lay(a_at, ("actA_hi", [P, NK, L], F32R), ("actA_lo", [P, NK, L], F32R))
        actB_hi, actB_lo, s_at = lay(b_at, ("actB_hi", [P, NK, L], F32R), ("actB_lo", [P, NK, L], F32R))
        pbuf, pT, o_n, _ = lay(a_at, ("pbuf", [P, 3, L]), ("pT", [P, 2, L]), ("o_n", [P, 2, L]))
        x_tok, _ = lay(b_at, ("x_tok", [P, NT, D]))
        iqT, score, rel, ik_s, ikn, ikrope, ikt, ikT, _ = lay(
            b_at, ("iqT", [P, 4, L]), ("score", [P, NT - 1, L]), ("rel", [P, 4, L]), ("ik_s", [P, L]),
            ("ikn", [P, NT, HD]), ("ikrope", [P, NT, 2 * HD]), ("ikt", [P, 4, NT * 32]), ("ikT", [P, L]))
        sg, aqT, bqT, akT, bkT, bv_tok, end1 = lay(
            s_at, ("sg", [P, 2, NK, L]), ("aqT", [P, 4, L]), ("bqT", [P, 4, L]), ("akT", [P, 2, L]),
            ("bkT", [P, 2, L]), ("bv_tok", [P, NT, P]))
        av_tok = place("av_tok", [P, NT, P], v_tok_a_at)
        rot, rt1, vT, _ = lay(s_at, ("rot", [P, 2, L]), ("rt1", [P, L]), ("vT", [P, 2, L]))
        mixb, mixt, _ = lay(s_at + words([P, 2, NK, L]), ("mixb", [P, 2, L]), ("mixt", [P, 2, L]))
        relu_u, u_sq, ytmp, _ = lay(s_at, ("relu_u", [P, 2, L]), ("u_sq", [P, 2, L]), ("ytmp", [P, L]))
        kT = {"a": akT, "b": bkT}
        qT = {"a": aqT, "b": bqT}
        v_tok = {"a": av_tok, "b": bv_tok}
        sg2, qdec, gv_tok, rsil, rsf, ssum2, go, end2 = lay(
            s_at, ("sg2", [P, 2, NK, L]), ("qdec", [P, 2, L]), ("gv_tok", [P, NT, GH * DV]),
            ("rsil", [P, GH, L]), ("rsf", [P, L]), ("ssum2", [P, L]), ("go", [P, L]))
        qs, ks, kend, pool_t, _ = lay(s_at, ("qs", [P, 2, L]), ("ks", [P, 2, L]), ("kend", [P, 2, L]),
                                      ("pool_t", [P, 2, L]))
        diff, alow, wal, pw, rs_o, dec, _ = lay(
            s_at + words([P, NK, L]), ("diff", [P, 4, L]), ("alow", [16, L]), ("wal", [16, 2 * P]),
            ("pw", [P, 4, P]), ("rs_o", [P, L]), ("dec", [P, 2, NCH]))
        gvT = place("gvT", [P, GH, L], s_at + words([P, 18, L]) + words([P, NT, GH * DV]))
        o_s, rs_h = (ssum2, go), (rs_o, rsf)
        half = words([P, 4, L])
        zs = place("zs", [P, 2, L], a_at)
        az = place("az", [P, 2, L], a_at + half // 2)
        kend_tok = place("kend_tok", [P, NT, 2 * P], a_at)
        gst = place("gst", [P, 2, NCH, DV], a_at + half)
        cs = place("cs", [P, 2, L], a_at + 2 * half)
        kdec = place("kdec", [P, 2, L], a_at + 2 * half + half // 2)
        scT = place("scT", [P, GH, L], a_at + 3 * half)
        xe, gu_hi, gu_lo, _ = lay(top, ("xe", [P, RING, D]), ("gu_hi", [P, 4 * D], F32R), ("gu_lo", [P, 4 * D], F32R))
        xeT_hi, hid, hidT, ye, lg, gw, ones_r, earlier_r, picks_r, at_row, in_block, lgT, small_end = lay(
            b_at, ("xeT_hi", [P, 2, D], F32R), ("hid", [P, 2, DE]), ("hidT", [P, 2, DE]), ("ye", [P, 2, D]),
            ("lg", [P, NT, NG + NE]), ("gw", [P, 16, NT]), ("ones_r", [P, P], F32R), ("earlier_r", [P, P], F32R),
            ("picks_r", [P, NT, NE], F32R), ("at_row", [P, NT, P], F32R), ("in_block", [P, NT, NB], F32R),
            ("lgT", [P, L]))
        gu_raw, _ = lay(a_at, ("gu_raw", [P, 2, 4 * D]))
        d_raw, rt, tabi, gix, six, gfin, h2T, end3 = lay(
            s_at, ("d_raw", [P, RING, 2 * D]), ("rt", [P, 12, NT * NE]),
            ("tabi", [P, 2, NB + RING], I32), ("gix", [P, RING], I32), ("six", [P, 2], I32),
            ("gfin", [P, D]), ("h2T", [P, NK, L]))
        x_res, _ = lay(end3 - words([P, NK, L]), ("x_res", [P, NT, D]))
        y2, _ = lay(a_at, ("y2", [P, NT, 2 * D]))
        xeT_lo = place("xeT_lo", [P, 2, D], v_tok_a_at, F32R)
        over_n = place("over_n", [1, 16], end3, I32)
        assert small_end <= s_at and max(end1, end2, end3 + 64) <= nc.sbuf_usable_end

        bank = [stack.enter_context(nc.psum_tensor(f"bank{i}", [P, L], F32)) for i in range(RING)]
        side = [stack.enter_context(nc.psum_tensor(f"side{i}", [P, L], F32)) for i in range(4)]
        jobs = job_table()

        h2_rows = nc.dram_tensor("h2_rows", [L, D], F32).ap()
        y2_rows = nc.dram_tensor("y2_rows", [2 * L, D], F32).ap()

        w_in_v = A["w_in"][0].rearrange("(k p) n -> p k n", p=P)
        w_in2_v = A["w_in_2"][0].rearrange("(k p) n -> p k n", p=P)
        br_v = [A[n][0].rearrange("(k p) n -> p k n", p=P) for n in ("w_branch_a", "w_branch_b")]
        br2_v = [A[n][0].rearrange("(k p) n -> p k n", p=P) for n in ("w_gla_branch_2", "w_pool_branch_2")]
        w_out_v = A["w_out"][0].rearrange("(k p) n -> p k n", p=P)
        w_out2_v = A["w_out_2"][0].rearrange("(k p) n -> p k n", p=P)
        w_up_v = A["w_up"][0].rearrange("(k p) n -> p k n", p=P)
        w_down_v = A["w_down"][0].rearrange("(k p) n -> p k n", p=P)

        def loads(c):
            return 2 if C_BR <= c < C_OUT or C_BR2 <= c < C_OUT2 else 1

        def raw_value(c):
            return 16 * sum(loads(j) for j in range(c % RING, c + 1, RING))

        raw_loaded = [S(f"raw_loaded{r}") for r in range(RING)]
        hi_made, lo_made, chunk_done, chunk_freed = S("hi_made"), S("lo_made"), S("chunk_done"), S("chunk_freed")
        side_full = S("side_full")
        side_freed = {"dve": S("side_freed_by_dve"), "act": S("side_freed_by_act")}
        STAGES = ("in", "branch", "out", "mlp", "in2", "branch2", "out2")

        def at(i, u, k):
            return u + k if i is None else RING * i + (u + k)

        def wait_from(e, sem, i, u, k, each=1):
            if i is not None or u + k > 0:
                e.wait_ge(sem, at(i, u, k) * each)

        def slot_count(i, u, each):
            return each * (u // 2 + 1) if i is None else 2 * each * i + each * (u // 2 + 1)

        LAST = (NE // RING - 1, RING - 1)

        def exists(i, u):
            return i is not None or u >= 0

        def for_experts(e, expert, last, overflow, end=lambda: None):
            for u in range(RING):
                expert(None, u)
            with e.Fori(1, NE // RING) as i:
                for u in range(RING):
                    expert(i, u)
            last()
            e.wait_ge(S("over_ready"), 1)
            over = e.value_load(over_n[0:1, 0:1], min_val=0, max_val=OVER)
            with e.If(over > 0):
                with e.Fori(NE // RING, NB // RING) as i:
                    for u in range(RING):
                        overflow(i, u)
                end()

        block = stack.enter_context(nc.Block())

        def wait_job(e, name):
            e.wait_ge(side_full, jobs.at[name] + 1)

        def wait_freed(e, name):
            i = jobs.at[name]
            e.wait_ge(side_freed[jobs.freer[i]], jobs.freed[i])

        @block.sync
        def _(sp):
            sp.dma_start(ident, A["consts"][:, 0:P]).then_inc(S("x_in"), 16)
            for i in range(NT):
                sp.dma_start(x_tok[:, i, :], A["x"][0, i * P:(i + 1) * P, :]).then_inc(S("x_in"), 16)

            def load_chunk(c, wait, *views):
                if wait is not None:
                    sp.wait_ge(lo_made, wait)
                for k0, k1, v in views:
                    sp.dma_start(raw[:, c % RING, k0 * P:k1 * P].rearrange("p (k n) -> p k n", n=P), v)\
                      .then_inc(raw_loaded[c % RING], 16)

            def load_group(first, n, view, col, step=P):
                if n % RING or first < RING:
                    for j in range(n):
                        c = first + j
                        load_chunk(c, c - RING + 1 if c >= RING else None,
                                   (0, NK, view[:, :, col + P * j:col + P * (j + 1)]))
                    return
                with sp.Fori(0, n // RING) as i:
                    for u in range(RING):
                        load_chunk(first + u, first + u - RING + 1 + RING * i,
                                   (0, NK, view[:, :, bass.ds(i * (RING * P) + (col + u * P), P)]))

            def load_branches(first, views):
                with sp.Fori(0, NK // RING) as i:
                    for u in range(RING):
                        at = bass.ds(i * (RING * P) + u * P, P)
                        load_chunk(first + u, first + u - RING + 1 + RING * i,
                                   (0, 4, views[0][:, :, at]), (4, 8, views[1][:, :, at]))

            load_group(0, 1, w_in_v, 1280)
            sp.dma_start(con[:, P:], A["consts"][:, P:]).then_inc(S("const_in"), 16)
            for name, t in (("attn_norm_w", g_attn), ("mlp_norm_w", g_mlp), ("norm1_g_2", g_n1), ("norm2_g_2", g_n2)):
                sp.dma_start(t, A[name][0].rearrange("(k p) -> p k", p=P), allow_slow_non_contiguous=True)\
                  .then_inc(S("small_in"), 16)
            sp.dma_start(g_fin, A["final_norm_w"].rearrange("(k p) -> p k", p=P), allow_slow_non_contiguous=True)\
              .then_inc(S("small_in"), 16)
            for name, t in (("b_alpha_2", b_alpha), ("gla_norm_g_2", g_gla), ("pool_scale_2", p_scale)):
                sp.dma_start(t, A[name][0].rearrange("(k p) -> p k", p=P), allow_slow_non_contiguous=True)\
                  .then_inc(S("small_in"), 16)
            sp.dma_start(sinkb[:, :], A["sinks"][0].partition_broadcast(P)).then_inc(S("small_in"), 16)
            sp.dma_start(lnwb[:, 0, :], A["idx_k_norm_w"][0].partition_broadcast(P)).then_inc(S("small_in"), 16)
            sp.dma_start(lnwb[:, 1, :], A["idx_k_norm_b"][0].partition_broadcast(P)).then_inc(S("small_in"), 16)
            for j, n, col in IN1_GROUPS:
                load_group(C_IN + j, n, w_in_v, col)
            load_branches(C_BR, br_v)
            load_group(C_OUT, NK, w_out_v, 0)
            for q in range(QUARTERS):
                load_group(C_MLP + 2 * NK * q, NK, w_up_v, D * q)
                load_group(C_MLP + 2 * NK * q + NK, NK, w_down_v[:, NK * q:NK * (q + 1), :], 0)
            load_group(C_IN2, 1, w_in2_v, 1536)
            sp.wait_ge(chunk_freed, C_OUT)
            sp.dma_start(wal[:, :], A["w_alpha_up_2"][0]).then_inc(S("small2_in"), 16)
            sp.dma_start(pw[:, :, :], A["pool_w_2"][0].rearrange("g c d -> c g d")).then_inc(S("small2_in"), 16)
            sp.dma_start(wr[:, :, 0:NG], A["w_router_group_2"][0].rearrange("(k p) g -> p k g", p=P),
                         allow_slow_non_contiguous=True).then_inc(S("route_in"), 16)
            for g in range(NG):
                sp.dma_start(wr[:, :, NG + EPG * g:NG + EPG * (g + 1)],
                             A["w_router_expert_2"][0, g].rearrange("(k p) e -> p k e", p=P),
                             allow_slow_non_contiguous=True).then_inc(S("route_in"), 16)
            sp.dma_start(brt[:, 0:NG], A["b_router_group_2"][0].partition_broadcast(P)).then_inc(S("route_in"), 16)
            sp.dma_start(brt[:, NG:], A["b_router_expert_2"][0].rearrange("g e -> (g e)").partition_broadcast(P))\
              .then_inc(S("route_in"), 16)
            for j, n, col in IN2_GROUPS:
                load_group(C_IN2 + j, n, w_in2_v, col)
            load_branches(C_BR2, br2_v)
            load_group(C_OUT2, NK, w_out2_v, 0)

            sp.wait_ge(chunk_freed, C_OUT2)

            wg_v = A["w_exp_gate_2"][0].rearrange("e (k p) n -> p e k n", p=P)
            wu_v = A["w_exp_up_2"][0].rearrange("e (k p) n -> p e k n", p=P)
            wd_v = A["w_exp_down_2"][0].rearrange("e (k p) n -> p e k n", p=P)

            def load_gate_up(u, e, former=None):
                gu = gu_raw[:, u % 2, :].rearrange("p (k h n) -> p k h n", h=2, n=DE)
                at_ = slice(e, e + 1) if isinstance(e, int) else bass.ds(e, 1)
                for part in range(2):
                    if former is not None:
                        sp.wait_ge(S(f"gu_lo{part}"), former * 2)
                    rows = slice(4 * part, 4 * part + 4)
                    for h, v in enumerate((wg_v, wu_v)):
                        sp.dma_start(gu[:, rows, h, :], v[:, at_, rows, :].rearrange("p e k n -> p (e k) n"))\
                          .then_inc(S(f"gu_in{u % 2}{part}"), 16)

            def load_down(u, e, former=None):
                if former is not None:
                    sp.wait_ge(S("down_done"), former)
                at_ = slice(e, e + 1) if isinstance(e, int) else bass.ds(e, 1)
                sp.dma_start(d_raw[:, u, :].rearrange("p (o k n) -> p o k n", o=1, n=D), wd_v[:, at_, :, :])\
                  .then_inc(S(f"down_in{u}"), 16)

            for e in range(2):
                load_gate_up(e, e)
            for e in range(RING):
                load_down(e, e)
            sp.wait_ge(S("ready_out2"), NK)
            sp.dma_start(gfin[:, :], A["norm_f_g_2"].partition_broadcast(P)).then_inc(S("gain_in"), 16)
            for i in range(NT):
                wait_freed(sp, ("rows", i, 1))
                sp.dma_start(h2_rows[i * P:(i + 1) * P, :], xe[:, i, :]).then_inc(S("h2_stored"), 16)
            sp.wait_ge(S("gathered0"), 16)
            for e in (2, 3):
                load_gate_up(e, e, e - 1)
            with sp.Fori(1, NE // RING) as i:
                for u in range(RING):
                    load_gate_up(u, RING * i + u, at(i, u, -1))
                    load_down(u, RING * i + u, at(i, u, -3))
            sp.wait_ge(S("over_ready"), 1)
            over = sp.value_load(over_n[0:1, 0:1], min_val=0, max_val=OVER)
            with sp.If(over > 0):
                with sp.Fori(NE // RING, NB // RING) as i:
                    for u in range(RING):
                        e = sp.value_load(over_n[0:1, bass.ds(RING * i + (u + 1 - NE), 1)], min_val=0, max_val=NE - 1)
                        load_gate_up(u, e, at(i, u, -1))
                        load_down(u, e, at(i, u, -3))

            sp.wait_ge(S("experts_over"), 1)
            for i in range(NT):
                sp.dma_start(y2[:, i, :].rearrange("p (k n) -> p k n", k=2),
                             y2_rows.rearrange("(k t p) n -> t p k n", k=2, p=P)[i]).then_inc(S(f"y2_in{i}"), 16)
            for i in range(NT):
                sp.wait_ge(S("final_out"), i + 1)
                sp.dma_start(out[i * P:(i + 1) * P, :], x_res[:, i, :]).then_inc(S("stored"), 16)
            sp.wait_ge(S("stored"), 16 * NT)

        @block.gpsimd
        def _(pool):
            def second_part(slot, wait):
                pool.wait_ge(hi_made, wait)
                nc.gpsimd.tensor_tensor(wlo[:, slot, :], raw[:, slot, :], whi[:, slot, :].bitcast(F32),
                                        ALU.subtract).then_inc(lo_made, 1)

            with pool.Fori(0, N_CHUNKS // RING) as i:
                for u in range(RING):
                    second_part(u, RING * i + (u + 1))
            for c in range(N_CHUNKS // RING * RING, N_CHUNKS):
                second_part(c % RING, c + 1)

            for n in range(4):
                pool.wait_ge(S(f"gu_hi{n // 2}"), n % 2 + 1)
                cols = slice(n * D, (n + 1) * D)
                nc.gpsimd.tensor_tensor(gu_lo[:, cols], gu_raw[:, 0, cols], gu_hi[:, cols].bitcast(F32), ALU.subtract)\
                    .then_inc(S(f"gu_lo{n // 2}"), 1)
            pool.wait_ge(S("h2_stored"), 16 * NT)
            pool.wait_ge(S("rows_ready"), 1)
            row_bound, slot_bound = pool.to_reg(L - 1), pool.to_reg(2 * L - 1)

            def gather(u, b, column_set, copies):
                nc.gpsimd.tensor_copy(gix[:, u:u + 1], tabi[:, 1, bass.ds(b, 1)]).then_inc(S(column_set), 1)
                pool.wait_ge(S("rows_ready"), 1)
                pool.wait_ge(S(column_set), copies)
                pool.indirect_dma_start(xe[0:ROWS, u, :], None, h2_rows,
                                        bass.IndirectOffsetOnAxis(ap=gix[0:ROWS, u:u + 1], axis=0),
                                        bounds_check=row_bound, oob_is_err=False).then_inc(S(f"gathered{u}"), 16)

            def move_rows(i, u):
                j, b = u % 2, at(i, u, 0)
                pool.wait_ge(S("xe_used"), at(i, u, 1))
                gather(u, at(i, u, RING), "gix_set", at(i, u, 1))
                if i is not None or u >= 2:
                    pool.wait_ge(S(f"scattered{j}"), 16 * (u // 2) if i is None else 32 * i + 16 * (u // 2))
                pool.wait_ge(S("y_by_act"), at(i, u, 1))
                pool.wait_ge(S("y_by_dve"), at(i, u, 1))
                nc.gpsimd.tensor_copy(six[:, j:j + 1], tabi[:, 0, bass.ds(b, 1)]).then_inc(S("six_set"), 1)
                pool.wait_ge(S("rows_ready"), 1)
                pool.wait_ge(S("six_set"), at(i, u, 1))
                pool.indirect_dma_start(y2_rows, bass.IndirectOffsetOnAxis(ap=six[0:ROWS, j:j + 1], axis=0),
                                        ye[0:ROWS, j, :], None, bounds_check=slot_bound, oob_is_err=False)\
                    .then_inc(S(f"scattered{j}"), 16)

            def all_moved(blocks):
                for u in range(RING):
                    pool.wait_ge(S(f"gathered{u}"), 16 * (blocks // RING + 1))
                for j in range(2):
                    pool.wait_ge(S(f"scattered{j}"), 16 * blocks // 2)

            for u in range(RING):
                gather(u, u, "first_gix_set", u + 1)
            for_experts(pool, move_rows, lambda: all_moved(NE), move_rows, lambda: all_moved(NB))
            nc.gpsimd.memset(gix[:, :], 0).then_inc(S("experts_over"), 1)

        def side_of(name):
            return side[jobs.at[name] % 4]

        def out_bank(c):
            return bank[c % RING]

        class Chain:

            def __init__(self, e, sem):
                self.e, self.sem, self.n = e, sem, {}

            def __call__(self, ins, sem=None):
                sem = sem or self.sem
                self.n[id(sem)] = self.n.get(id(sem), 0) + 1
                ins.then_inc(sem, 1)
                self.e.wait_ge(sem, self.n[id(sem)])

        def rope_index(c):
            return [1, 2, 3, 4, 5, 6, 7, 8, 9, 11, 13, 14, 15, 16].index(c)

        ROPED = (1, 2, 3, 4, 5, 6, 7, 8, 9, 11, 13, 14, 15, 16)
        N_SMALL = 11

        @block.scalar
        def _(act):
            chain = Chain(act, S("act_step"))
            a = nc.scalar.activation

            def first_part(c):
                if c >= N_CHUNKS:
                    return
                act.wait_ge(raw_loaded[c % RING], raw_value(c))
                if c >= RING:
                    act.wait_ge(chunk_done, c - RING + 1)
                a(whi[:, c % RING, :], raw[:, c % RING, :], ACT.Copy).then_inc(hi_made, 1)

            def split_first(stage, hi, k, src, gain):
                ins = a(hi[:, k, :], src, ACT.Copy) if gain is None else \
                    a(hi[:, k, :], src, ACT.Copy, scale=gain[:, k:k + 1])
                ins.then_inc(S(f"hi_{stage}"), 1)

            def squares(n, src, gain=None, of="sq_made", added="sum_added"):
                if n >= 2:
                    act.wait_ge(S(added), n - 1)
                ins = a(sq[:, n % 2, :], src, ACT.Square) if gain is None else \
                    a(sq[:, n % 2, :], src, ACT.Square, scale=gain)
                ins.then_inc(S(of), 1)

            def guess(src, n, dst=None, width=D, tmp=None):
                dst = rs[:, :] if dst is None else dst
                tmp = nt0[:, :] if tmp is None else tmp
                nc.scalar.preload_act_table_set("natural_log_exp_and_others")
                chain(a(tmp, src, ACT.Ln, scale=1.0 / width, bias=eps_t[:, :]))
                chain(a(dst, tmp, ACT.Exp, scale=-0.5), S("guess_made"))

            act.wait_ge(S("eps_set"), 1)
            act.wait_ge(S("small_in"), 16 * N_SMALL)
            first_part(0)
            for k in range(NK):
                wait_job(act, ("x_t", k))
                chain(a(xT[:, k, :], side_of(("x_t", k))[:, :], ACT.Copy), side_freed["act"])
                split_first("in", actA_hi, k, xT[:, k, :], g_attn)
                squares(k, xT[:, k, :])
            first_part(1)
            first_part(2)
            wait_job(act, "sum0")
            guess(side_of("sum0")[:, :], 0)
            for c in range(C_IN, C_IN + 17):
                first_part(c + AHEAD)
                if c in ROPED:
                    r = ROPED.index(c)
                    act.wait_ge(chunk_done, c + 1)
                    if r >= 2:
                        act.wait_ge(S("roped"), r - 1)
                    for q in range(4):
                        other = 32 * (q ^ 1)
                        ins = a(rot[32 * q:32 * q + 32, r % 2, :], out_bank(c)[other:other + 32, :], ACT.Copy,
                                scale=-1.0 if q % 2 == 0 else 1.0)
                    ins.then_inc(S("rot_made"), 1)
                if c == 6:
                    act.wait_ge(S("ik_var"), 1)
                    guess(ikmv[:, :, 1], 1, ikr[:, 1, :], 1, ikr[:, 0, :])
                if c == 12:
                    for n, b in enumerate("ab"):
                        wait_job(act, ("v_tok", b))
                        a(v_tok[b][:, :, :].rearrange("p t f -> p (t f)"), side_of(("v_tok", b))[:, :], ACT.Copy)\
                            .then_inc(side_freed["act"], 1)
                    wait_job(act, "ik_t")
                    a(ikT[:, :], side_of("ik_t")[:, :], ACT.Copy).then_inc(side_freed["act"], 1)
            n = 0
            for qt in range(1, NT):
                for h in range(HEADS):
                    wait_job(act, ("index", qt, h))
                    if n >= 4:
                        act.wait_ge(S("index_added"), n - 3)
                    w = (qt + 1) * P
                    a(rel[:, n % 4, 0:w], side_of(("index", qt, h))[:, 0:w], ACT.Relu).then_inc(side_freed["act"], 1)
                    n += 1
            for c in range(C_IN + 17, C_IN + 33):
                if c + AHEAD < C_BR + AHEAD:
                    first_part(c + AHEAD)
                j = c - C_IN - 17
                act.wait_ge(chunk_freed, c + 1)
                t = sg[:, j // NK, j % NK, :]
                a(t, t, ACT.Sigmoid).then_inc(S("gate_made"), 1)

            nc.scalar.preload_act_table_set("natural_log_exp_and_others")
            for s in range(STEPS):
                if s % 8 == 7 and s >= 15:
                    g = s // 8 - 1
                    b, qt = unit(g * HEADS)[:2]
                    k = 4 if b == "b" else 0
                    wait_job(act, ("out_t", g))
                    a(actB_hi[:, k:k + 4, qt * P:(qt + 1) * P],
                      side_of(("out_t", g))[:, :].rearrange("p (f q) -> p f q", q=P), ACT.Copy)\
                        .then_inc(S("hi_branch"), 1)
                if s < UNITS:
                    b, qt, k0, nk, h = unit(s)
                    t = pbuf[:, s % 3, 0:nk * P]
                    act.wait_ge(S("logits_made"), s + 1)
                    a(t, t, ACT.Exp, bias=nm[:, s // HEADS, h:h + 1],
                      accum_out=den[:, s // HEADS, h:h + 1]).then_inc(S("probs_made"), 1)
                if 1 <= s < UNITS + 1:
                    u = s - 1
                    nk = unit(u)[3]
                    wait_job(act, ("probs_t", u))
                    if u >= 2:
                        act.wait_ge(S("values_done"), u - 1)
                    a(pT[:, u % 2, 0:nk * P], side_of(("probs_t", u))[:, 0:nk * P], ACT.Copy)\
                        .then_inc(side_freed["act"], 1)
                if s % 8 == 1 and 9 <= s <= 8 * NT + 1:
                    g = s // 8 - 1
                    act.wait_ge(S("sinks_shifted"), g + 1)
                    a(es[:, g, :], es[:, g, :], ACT.Exp).then_inc(S("sinks_exp"), 1)

            def mix_parts(first, stage, hi):
                for m in range(NK):
                    first_part(first + m + AHEAD)
                    act.wait_ge(S(f"mixed_{stage}"), m + 1)
                    split_first(stage, hi, m, mixb[:, m % 2, :], None)

            mix_parts(C_BR, "out", actA_hi)
            for m in range(NK):
                first_part(C_OUT + m + AHEAD)
                act.wait_ge(chunk_freed, C_OUT + m + 1)
                split_first("mlp", actB_hi, m, xT[:, m, :], g_mlp)
                squares(NK + m, xT[:, m, :])
            for q in range(QUARTERS):
                up = C_MLP + 2 * NK * q
                for m in range(NK):
                    first_part(up + m + AHEAD)
                    act.wait_ge(chunk_freed, up + m + 1)
                    chain(a(u_sq[:, m % 2, :], relu_u[:, m % 2, :], ACT.Square), S("u_made"))
                    split_first(f"u{q}", actA_hi, m, u_sq[:, m % 2, :], None)
                if q == 0:
                    wait_job(act, "sum1")
                    guess(side_of("sum1")[:, :], 2)
                for m in range(NK):
                    first_part(up + NK + m + AHEAD)
                    if q == QUARTERS - 1:
                        act.wait_ge(S("x1_made"), m + 1)
                        split_first("in2", actB_hi, m, xT[:, m, :], g_fin1)
                        squares(2 * NK + 2 * m, xT[:, m, :])
                        squares(2 * NK + 2 * m + 1, xT[:, m, :], g_fin[:, m:m + 1])
            wait_job(act, "sum2")
            guess(side_of("sum2")[:, :], 3, rsf[:, :])
            act.wait_ge(S("second_sum"), 1)
            guess(ssum2[:, :], 4)

            for c in range(C_IN2, C_IN2 + 5):
                first_part(c + AHEAD)
            for j in range(2):
                wait_freed(act, ("z", j))
                chain(a(az[:, j, :], zs[:, j, :], ACT.Abs))
                chain(a(az[:, j, :], az[:, j, :], ACT.Exp, scale=-1.0))
                a(az[:, j, :], az[:, j, :], ACT.Ln, bias=1.0).then_inc(S("log_made"), 1)
            for c in range(C_IN2 + 5, C_IN2 + 9):
                first_part(c + AHEAD)
            for j in range(2):
                act.wait_ge(S("decay_summed"), j + 1)
                a(az[:, j, :], cs[:, j, :], ACT.Exp, scale=1.0 / 16.0).then_inc(S("decays"), 1)
                a(zs[:, j, :], cs[:, j, :], ACT.Exp, scale=-1.0 / 16.0).then_inc(S("decays"), 1)
            for j in range(2):
                act.wait_ge(S("decay_left"), j + 1)
                a(cs[:, j, :], cs[:, j, :], ACT.Exp, scale=1.0 / 16.0).then_inc(S("decays"), 1)
            for h in range(GH):
                wait_job(act, ("gv_tok", h))
                a(gv_tok[:, :, h * DV:(h + 1) * DV], side_of(("gv_tok", h))[:, :].rearrange("p (t f) -> p t f", f=DV),
                  ACT.Copy).then_inc(side_freed["act"], 1)
            for c in range(C_IN2 + 9, C_IN2 + 13):
                first_part(c + AHEAD)
                h = c - C_IN2 - 9
                act.wait_ge(chunk_freed, c + 1)
                a(pool_t[:, h % 2, :], rsil[:, h, :], ACT.Sigmoid).then_inc(S("r_sigmoid"), 1)
                act.wait_ge(S("r_silu"), h + 1)
            for c in range(C_IN2 + 13, C_IN2 + 17):
                first_part(c + AHEAD)
            for j in range(2):
                wait_job(act, ("kend_tok", j))
                a(kend_tok[:, :, j * P:(j + 1) * P], side_of(("kend_tok", j))[:, :].rearrange("p (t f) -> p t f", f=P),
                  ACT.Copy).then_inc(side_freed["act"], 1)

            def gate(c):
                first_part(c + AHEAD)
                j = c - C_IN2 - 17
                act.wait_ge(chunk_freed, c + 1)
                t = sg2[:, j // NK, j % NK, :]
                a(t, t, ACT.Sigmoid).then_inc(S("gate_made"), 1)

            for c in range(C_IN2 + 17, C_IN2 + 21):
                gate(c)
            def head_first(h):
                act.wait_ge(S("o_normed"), h + 1)
                split_first("branch2", actA_hi, h, o_s[h % 2][:, :], None)

            for h in range(GH):
                wait_job(act, ("o", h))
                a(sq[:, 0, :], side_of(("o", h))[:, :], ACT.Square).then_inc(S("o_squares"), 1)
                gate(C_IN2 + 21 + h)
                wait_job(act, ("o_sum", h))
                if h >= 2:
                    act.wait_ge(S("o_normed"), h - 1)
                guess(side_of(("o_sum", h))[:, :], 5 + h, rs_h[h % 2][:, :], DV, sq[:, 1, :])
                if h:
                    head_first(h - 1)
            head_first(GH - 1)
            for g in range(4):
                wait_freed(act, ("pool", g))
                split_first("branch2", actA_hi, 4 + g, diff[:, g, :], None)
            for c in range(C_IN2 + 25, C_IN2 + 33):
                gate(c)
            mix_parts(C_BR2, "out2", actB_hi)
            for m in range(NK):
                first_part(C_OUT2 + m + AHEAD)
                act.wait_ge(chunk_freed, C_OUT2 + m + 1)
                squares(m, xT[:, m, :], None, "sq4_made", "sum4_added")
            wait_job(act, "route")
            a(lgT[0:NG + NE, :], side_of("route")[0:NG + NE, :], ACT.Copy).then_inc(side_freed["act"], 1)
            wait_job(act, "sum4")
            guess(side_of("sum4")[:, 0:NT], 9, gw[:, 13, :], D, gw[:, 14, :])

            act.wait_ge(S("norm_made"), 1)
            for i in range(NT):
                for n in range(2):
                    wait_job(act, ("rows", i, n))
                    a(xe[:, i, n * L:(n + 1) * L], side_of(("rows", i, n))[:, :], ACT.Copy, scale=gw[:, 13, i:i + 1])\
                        .then_inc(side_freed["act"], 1)
            act.wait_ge(S("group_shifted"), 1)
            a(rt[:, 0, 0:NT * NG], rt[:, 0, 0:NT * NG], ACT.Exp).then_inc(S("group_exp"), 1)
            act.wait_ge(S("expert_shifted"), 1)
            a(gw[:, 6, :], gw[:, 6, :], ACT.Exp).then_inc(S("expert_exp"), 1)
            def gate_up_first(i, u, part):
                act.wait_ge(S(f"gu_in{u % 2}{part}"), slot_count(i, u, 32))
                wait_from(act, S(("gate_up_half_done", "gate_up_done")[part]), i, u, 0)
                for n in (2 * part, 2 * part + 1):
                    cols = slice(n * D, (n + 1) * D)
                    a(gu_hi[:, cols], gu_raw[:, u % 2, cols], ACT.Copy).then_inc(S(f"gu_hi{part}"), 1)

            for part in range(2):
                gate_up_first(None, 0, part)
            for i in range(NT):
                for n in range(2):
                    wait_job(act, ("resid", i, n))
                    a(x_res[:, i, n * L:(n + 1) * L], side_of(("resid", i, n))[:, :], ACT.Copy)\
                        .then_inc(side_freed["act"], 1)

            def x_turned(i, u):
                act.wait_ge(S("xe_used"), at(i, u, 1))
                wait_from(act, S("gate_up_done"), i, u, -1)
                for n in range(2):
                    a(xeT_hi[:, u % 2, n * L:(n + 1) * L], side[n][:, :], ACT.Copy).then_inc(S("xe_hi"), 1)

            def silu(i, u):
                act.wait_ge(S("gate_up_done"), at(i, u, 1))
                wait_from(act, S("hid_turned"), i, u, -1)
                a(hid[:, u % 2, :], bank[u % 2][:, 0:DE], ACT.Silu).then_inc(S("silu_made"), 1)

            def y_out(i, u):
                act.wait_ge(S("down_done"), at(i, u, 1))
                if exists(i, u - 2):
                    act.wait_ge(S(f"scattered{u % 2}"), slot_count(i, u - 2, 16))
                a(ye[:, u % 2, 0:L], bank[2][:, :], ACT.Copy).then_inc(S("y_by_act"), 1)

            def expert(i, u):
                if exists(i, u - 1):
                    gate_up_first(i, u, 0)
                    silu(i, u - 1)
                    gate_up_first(i, u, 1)
                x_turned(i, u)
                if exists(i, u - 2):
                    y_out(i, u - 2)

            def last():
                i, u = LAST
                silu(i, u)
                x_turned(i, u + 1)
                y_out(i, u - 1)
                y_out(i, u)

            def overflow(i, u):
                gate_up_first(i, u, 0)
                gate_up_first(i, u, 1)
                silu(i, u)
                x_turned(i, u + 1)
                y_out(i, u)

            for_experts(act, expert, last, overflow)

            for n in range(NT):
                act.wait_ge(S("final_sum"), n + 1)
                chain(a(xe[:, 0, :], x_res[:, n, :], ACT.Square, accum_out=gw[:, 12, n:n + 1]))
                guess(gw[:, 12, n:n + 1], 10 + n, gw[:, 13, n:n + 1], D, gw[:, 14, n:n + 1])

        @block.vector
        def _(dve):
            chain = Chain(dve, S("dve_step"))
            v = nc.vector
            guesses = [0]

            def refine(src, dst=None, width=D, tmp=None, tmp2=None, freed=None, made=None):
                dst = rs[:, :] if dst is None else dst
                tmp = nt0[:, :] if tmp is None else tmp
                tmp2 = ssum[:, :] if tmp2 is None else tmp2
                guesses[0] += 1
                dve.wait_ge(S("guess_made"), guesses[0])
                chain(v.tensor_scalar(tmp, src, -0.5 / width, -0.5 * EPS, ALU.mult, ALU.add), freed)
                chain(v.tensor_tensor(tmp2, dst, dst, ALU.mult))
                chain(v.tensor_tensor(tmp2, tmp2, tmp, ALU.mult))
                chain(v.scalar_tensor_tensor(dst, tmp2, 1.5, dst, ALU.add, ALU.mult), made)

            def second(stage, hi, lo, k, src, gain):
                dve.wait_ge(S(f"hi_{stage}"), k + 1)
                first = hi[:, k, :].bitcast(F32)
                if gain is None:
                    ins = v.tensor_tensor(lo[:, k, :], src, first, ALU.subtract)
                else:
                    ins = v.scalar_tensor_tensor(lo[:, k, :], src, gain[:, k:k + 1], first, ALU.mult, ALU.subtract)
                chain(ins, S(f"ready_{stage}"))

            def add_squares(n, m, total=None, made="sq_made", added="sum_added"):
                total = ssum if total is None else total
                dve.wait_ge(S(made), n + 1)
                if m == 0:
                    chain(v.tensor_copy(total[:, :], sq[:, n % 2, :]), S(added))
                else:
                    chain(v.tensor_tensor(total[:, :], total[:, :], sq[:, n % 2, :], ALU.add), S(added))

            freed = side_freed["dve"]
            chain(v.memset(eps_t[:, :], EPS), S("eps_set"))
            chain(v.memset(ones[:, :], 1.0), S("ones_set"))
            dve.wait_ge(S("small_in"), 16 * N_SMALL)
            chain(v.tensor_tensor(g_fin1, g_fin, g_n1, ALU.mult), S("gain_set"))
            for k in range(NK + 1):
                if k < NK:
                    second("in", actA_hi, actA_lo, k, xT[:, k, :], g_attn)
                if k >= 1:
                    add_squares(k - 1, k - 1)
            refine(side_of("sum0")[:, :], freed=freed)
            dve.wait_ge(S("const_in"), 16)
            chain(v.tensor_tensor(const("cos"), const("cos"), rs[:, :], ALU.mult))
            chain(v.tensor_tensor(const("sin"), const("sin"), rs[:, :], ALU.mult))

            def take(c, dst, by=None):
                dve.wait_ge(chunk_done, c + 1)
                chain(v.tensor_tensor(dst, out_bank(c)[0:dst.shape[0], :], (rs[:, :] if by is None else by)[0:dst.shape[0], :],
                                      ALU.mult), chunk_freed)

            def rope(c, *dst):
                r = ROPED.index(c)
                dve.wait_ge(S("rot_made"), r + 1)
                chain(v.tensor_tensor(rt1[:, :], out_bank(c)[:, :], const("cos"), ALU.mult), chunk_freed)
                chain(v.tensor_tensor(rot[:, r % 2, :], rot[:, r % 2, :], const("sin"), ALU.mult))
                for n, (rows, out_rows, to) in enumerate(dst):
                    chain(v.tensor_tensor(to[out_rows, :], rt1[rows, :], rot[rows, r % 2, :], ALU.add),
                          S("roped") if n == len(dst) - 1 else None)

            ALL, LOW, HIGH = slice(0, P), slice(0, HD), slice(HD, P)

            def rope_keys(c, to):
                rope(c, (LOW, LOW, to[:, 0, :]), (LOW, HIGH, to[:, 0, :]),
                     (HIGH, HIGH, to[:, 1, :]), (HIGH, LOW, to[:, 1, :]))

            take(C_IN, ik_s[:, :])
            for c in range(1, 5):
                rope(c, (ALL, ALL, iqT[:, c - 1, :]))
            wait_job(dve, "ik_tok")
            by_tok = side_of("ik_tok")[:, :].rearrange("p (t f) -> p t f", f=P)
            chain(v.tensor_scalar(iw[:, :, :], by_tok[:, :, HD:HD + HEADS], W_SCALE, None, ALU.mult))
            for t in range(NT):
                chain(v.bn_stats(ikstat[:, t, :], by_tok[:, t, 0:HD]))
                chain(v.bn_aggr(ikmv[:, t, :], ikstat[:, t, :]), S("ik_var") if t == NT - 1 else None)
            for t in range(NT):
                chain(v.tensor_scalar(ikn[:, t, :], by_tok[:, t, 0:HD], ikmv[:, t, 0:1], None, ALU.subtract),
                      freed if t == NT - 1 else None)
            for c in range(5, 7):
                rope(c, (ALL, ALL, aqT[:, c - 5, :]))
            refine(ikmv[:, :, 1], ikr[:, 1, :], 1, ikr[:, 2, :], ikr[:, 3, :])
            for t in range(NT):
                chain(v.tensor_scalar(ikn[:, t, :], ikn[:, t, :], ikr[:, 1, t:t + 1], None, ALU.mult))
            for n, op in ((0, ALU.mult), (1, ALU.add)):
                chain(v.tensor_tensor(ikn[:, :, :], ikn[:, :, :],
                                      lnwb[:, n, :].unsqueeze(1).broadcast_to([P, NT, HD]), op))
            cos_t, sin_t = (const(n).rearrange("p (t f) -> p t f", f=32) for n in ("cos_tok", "sin_tok"))
            tmp = [ikt[:, n, :].rearrange("p (t f) -> p t f", f=32) for n in range(4)]
            x1, x2 = ikn[:, :, 0:32], ikn[:, :, 32:64]
            for n, (x, cs_) in enumerate(((x1, cos_t), (x2, sin_t), (x2, cos_t), (x1, sin_t))):
                chain(v.tensor_tensor(tmp[n], x, cs_, ALU.mult))
            for half in range(2):
                o = ikrope[:, :, half * HD:(half + 1) * HD]
                chain(v.tensor_tensor(o[:, :, 0:32], tmp[0], tmp[1], ALU.subtract))
                chain(v.tensor_tensor(o[:, :, 32:64], tmp[2], tmp[3], ALU.add), S("ik_roped"))
            for c in range(7, 9):
                rope(c, (ALL, ALL, aqT[:, c - 5, :]))
            rope_keys(9, akT)
            take(10, vT[:, 0, :])
            rope_keys(11, bkT)
            take(12, vT[:, 1, :])
            for c in range(13, 17):
                rope(c, (ALL, ALL, bqT[:, c - 13, :]))
            n = 0
            for qt in range(1, NT):
                w = (qt + 1) * P
                s = score[:, qt - 1, 0:w]
                for h in range(HEADS):
                    wait_freed(dve, ("index", qt, h))
                    r = rel[:, n % 4, 0:w]
                    if h == 0:
                        ins = v.tensor_scalar(s, r, iw[:, qt, h:h + 1], None, ALU.mult)
                    else:
                        ins = v.scalar_tensor_tensor(s, r, iw[:, qt, h:h + 1], s, ALU.mult, ALU.add)
                    chain(ins, S("index_added"))
                    n += 1
                own = score[:, qt - 1, qt * P:w]
                chain(v.tensor_tensor(own, own, const("causal"), ALU.add))
            for c in range(17, 33):
                for qt in range(1, NT):
                    s = score[:, qt - 1, 0:(qt + 1) * P]
                    chain(v.max(top8[:, qt - 1, :], s))
                    chain(v.match_replace(s, top8[:, qt - 1, :], s, TAKEN))
                take(c, sg[:, (c - 17) // NK, (c - 17) % NK, :])
            for qt in range(1, NT):
                w = (qt + 1) * P
                chain(v.tensor_scalar(keep[:, KEEP_AT[qt]:KEEP_AT[qt] + w], score[:, qt - 1, 0:w],
                                      TAKEN * 0.98, NEG, ALU.is_gt, ALU.mult))

            b0 = CONST_COLS["before"][0]
            for s in range(STEPS):
                if s % 8 == 0 and 8 <= s <= 8 * NT:
                    g = s // 8 - 1
                    chain(v.tensor_tensor(es[:, g, :], sinkb[:, :], nm[:, g, :], ALU.add), S("sinks_shifted"))
                if s % 8 == 7 and s >= 15:
                    g = s // 8 - 1
                    b, qt = unit(g * HEADS)[:2]
                    k = 4 if b == "b" else 0
                    cols = slice(qt * P, (qt + 1) * P)
                    dve.wait_ge(S("hi_branch"), g + 1)
                    chain(v.tensor_tensor(actB_lo[:, k:k + 4, cols],
                                          side_of(("out_t", g))[:, :].rearrange("p (f q) -> p f q", q=P),
                                          actB_hi[:, k:k + 4, cols].bitcast(F32), ALU.subtract), freed)
                if s < UNITS:
                    b, qt, k0, nk, h = unit(s)
                    g = s // HEADS
                    wait_job(dve, ("logits", s))
                    if s >= 3:
                        wait_job(dve, ("probs_t", s - 3))
                    if qt == 0:
                        bias = const("causal")
                    elif b == "b":
                        bias = con[:, b0:b0 + 2 * P]
                    else:
                        bias = keep[:, KEEP_AT[qt]:KEEP_AT[qt] + nk * P]
                    chain(v.tensor_tensor_reduce(
                        out=pbuf[:, s % 3, 0:nk * P], in0=side_of(("logits", s))[:, 0:nk * P], in1=bias,
                        scale=ATT_SCALE, scalar=-3.0e38, op0=ALU.add, op1=ALU.max,
                        accum_out=mx[:, g, h:h + 1]), freed)
                    if b == "b":
                        ins = v.tensor_scalar(nm[:, g, h:h + 1], mx[:, g, h:h + 1], sinkb[:, h:h + 1], -1.0,
                                              ALU.max, ALU.mult)
                    else:
                        ins = v.tensor_scalar(nm[:, g, h:h + 1], mx[:, g, h:h + 1], -1.0, None, ALU.mult)
                    chain(ins, S("logits_made"))
                if s % 8 == 3 and s >= 11:
                    g = s // 8 - 1
                    dve.wait_ge(S("probs_made"), (g + 1) * HEADS)
                    if g < NT:
                        dve.wait_ge(S("sinks_exp"), g + 1)
                        chain(v.tensor_tensor(den[:, g, :], den[:, g, :], es[:, g, :], ALU.add))
                    chain(v.reciprocal(mx[:, g, :], den[:, g, :]))
                    dve.wait_ge(S("values_done"), (g + 1) * HEADS)
                    if g >= 2:
                        wait_job(dve, ("out_t", g - 2))
                    chain(v.tensor_tensor(o_n[:, g % 2, :].rearrange("p (h d) -> p h d", d=HD),
                                          bank[g % RING][:, :].rearrange("p (h d) -> p h d", d=HD),
                                          mx[:, g, :].unsqueeze(2).broadcast_to([P, HEADS, HD]), ALU.mult),
                          S("outs_made"))

            def mix(first, stage, gates, hi, lo, gates_before):
                for m in range(NK + 1):
                    if m < NK:
                        c = first + m
                        dve.wait_ge(chunk_done, c + 1)
                        dve.wait_ge(S("gate_made"), gates_before + 2 * NK)
                        if m >= 2:
                            dve.wait_ge(S(f"hi_{stage}"), m - 1)
                        chain(v.tensor_tensor(mixb[:, m % 2, :], out_bank(c)[:, :], gates[:, 0, m, :], ALU.mult))
                        chain(v.tensor_tensor(mixt[:, m % 2, :], side[c % 4][:, :], gates[:, 1, m, :], ALU.mult), chunk_freed)
                        chain(v.tensor_tensor(mixb[:, m % 2, :], mixb[:, m % 2, :], mixt[:, m % 2, :], ALU.add),
                              S(f"mixed_{stage}"))
                    if m >= 1:
                        second(stage, hi, lo, m - 1, mixb[:, (m - 1) % 2, :], None)

            mix(C_BR, "out", sg, actA_hi, actA_lo, 0)
            for m in range(NK + 1):
                if m < NK:
                    dve.wait_ge(chunk_done, C_OUT + m + 1)
                    chain(v.tensor_tensor(xT[:, m, :], xT[:, m, :], out_bank(C_OUT + m)[:, :], ALU.add), chunk_freed)
                if m >= 1:
                    second("mlp", actB_hi, actB_lo, m - 1, xT[:, m - 1, :], g_mlp)
                    add_squares(NK + m - 1, m - 1)
            for q in range(QUARTERS):
                up = C_MLP + 2 * NK * q
                for m in range(NK + 1):
                    if m < NK:
                        dve.wait_ge(chunk_done, up + m + 1)
                        if NK * q + m >= 2:
                            dve.wait_ge(S("u_made"), NK * q + m - 1)
                        chain(v.tensor_scalar(relu_u[:, m % 2, :], out_bank(up + m)[:, :], 0.0, None, ALU.max), chunk_freed)
                    if m >= 1:
                        second(f"u{q}", actA_hi, actA_lo, m - 1, u_sq[:, (m - 1) % 2, :], None)
                if q == 0:
                    refine(side_of("sum1")[:, :], freed=freed)
                    chain(v.tensor_tensor(rs[:, :], rs[:, :], rs[:, :], ALU.mult))
                for m in range(NK + 1):
                    c = up + NK + m
                    if m < NK:
                        dve.wait_ge(chunk_done, c + 1)
                        chain(v.tensor_tensor(ytmp[:, :], out_bank(c)[:, :], rs[:, :], ALU.mult), chunk_freed)
                        chain(v.tensor_tensor(xT[:, m, :], xT[:, m, :], ytmp[:, :], ALU.add),
                              S("x1_made") if q == QUARTERS - 1 else None)
                    if m >= 1 and q == QUARTERS - 1:
                        second("in2", actB_hi, actB_lo, m - 1, xT[:, m - 1, :], g_fin1)
                        add_squares(2 * NK + 2 * (m - 1), m - 1)
                        add_squares(2 * NK + 2 * (m - 1) + 1, m - 1, ssum2)
            refine(side_of("sum2")[:, :], rsf[:, :], freed=freed)
            wait_job(dve, "sum3")
            chain(v.tensor_tensor(ssum2[:, :], side_of("sum3")[:, :], rsf[:, :], ALU.mult), freed)
            chain(v.tensor_tensor(ssum2[:, :], ssum2[:, :], rsf[:, :], ALU.mult), S("second_sum"))
            refine(ssum2[:, :])
            chain(v.tensor_tensor(rs[:, :], rs[:, :], rsf[:, :], ALU.mult))

            take(C_IN2, alow[:, :])
            chain(v.memset(go[:, :], 1.0))
            chain(v.memset(go[:, :].rearrange("p (c t) -> p c t", t=CHUNK)[:, :, 0:1], 0.0), S("alow_made"))
            for j in range(2):
                take(C_IN2 + 1 + j, qs[:, j, :])
            for j in range(2):
                take(C_IN2 + 3 + j, ks[:, j, :])
            for j in range(2):
                wait_job(dve, ("z", j))
                chain(v.tensor_scalar(zs[:, j, :], side_of(("z", j))[:, :], b_alpha[:, j:j + 1], None, ALU.add), freed)
            for m in range(NK):
                chain(v.scalar_tensor_tensor(xT[:, m, :], xT[:, m, :], g_fin[:, m:m + 1], rsf[:, :], ALU.mult, ALU.mult))
            for h in range(GH):
                take(C_IN2 + 5 + h, gvT[:, h, :])
            by_chunk = lambda t: t.rearrange("p (c t) -> p c t", t=CHUNK)
            for j in range(2):
                dve.wait_ge(S("log_made"), j + 1)
                chain(v.scalar_tensor_tensor(zs[:, j, :], zs[:, j, :], 0.0, az[:, j, :], ALU.min, ALU.subtract))
                chain(v.tensor_tensor_scan(cs[:, j, :], go[:, :], zs[:, j, :], 0.0, ALU.mult, ALU.add), S("decay_summed"))
            for j in range(2):
                dve.wait_ge(S("decays"), 2 * (j + 1))
                chain(v.tensor_copy(dec[:, j, :], by_chunk(az[:, j, :])[:, :, CHUNK - 1]))
                chain(v.scalar_tensor_tensor(qdec[:, j, :], qs[:, j, :], CHUNK ** -0.5, az[:, j, :], ALU.mult, ALU.mult))
                chain(v.tensor_tensor(kdec[:, j, :], ks[:, j, :], zs[:, j, :], ALU.mult))
                last = by_chunk(cs[:, j, :])[:, :, CHUNK - 1:CHUNK]
                chain(v.tensor_copy(top8[:, 0, :], last.rearrange("p c t -> p (c t)")))
                chain(v.tensor_tensor(by_chunk(cs[:, j, :]), top8[:, 0, :].unsqueeze(2).broadcast_to([P, NCH, CHUNK]),
                                      by_chunk(cs[:, j, :]), ALU.subtract), S("decay_left"))
            for j in range(2):
                dve.wait_ge(S("decays"), 5 + j)
                chain(v.tensor_tensor(kend[:, j, :], ks[:, j, :], cs[:, j, :], ALU.mult), S("kend_made"))
            for h in range(GH):
                take(C_IN2 + 9 + h, rsil[:, h, :])
                dve.wait_ge(S("r_sigmoid"), h + 1)
                chain(v.tensor_tensor(rsil[:, h, :], rsil[:, h, :], pool_t[:, h % 2, :], ALU.mult), S("r_silu"))
            inv = const("inv_count")
            for g, win in enumerate(WINDOWS):
                take(C_IN2 + 13 + g, diff[:, g, :])
                src, step, n = diff[:, g, :], 1, 0
                while step < win:
                    dst = pool_t[:, n % 2, :]
                    chain(v.tensor_copy(dst[:, 0:step], src[:, 0:step]))
                    chain(v.tensor_tensor(dst[:, step:], src[:, step:], src[:, 0:L - step], ALU.add))
                    src, step, n = dst, 2 * step, n + 1
                chain(v.tensor_tensor(src[:, 0:16], src[:, 0:16], inv[:, 16 * g:16 * g + 16], ALU.mult))
                chain(v.tensor_scalar(src[:, 16:], src[:, 16:], 1.0 / win, None, ALU.mult))
                chain(v.tensor_tensor(diff[:, g, :], src, diff[:, g, :], ALU.subtract), S("diff_made"))
            for n in range(NCH - 1):
                wait_job(dve, ("inc", n))
                for j in range(2):
                    for e in range(2):
                        rows = slice(HD * e, HD * (e + 1))
                        inc = side_of(("inc", n))[rows, 256 * j + DV * e:256 * j + DV * (e + 1)]
                        done = freed if (j, e) == (1, 1) else None
                        if n == 0:
                            chain(v.tensor_copy(gst[rows, j, 1, :], inc), done)
                        else:
                            chain(v.scalar_tensor_tensor(gst[rows, j, n + 1, :], gst[rows, j, n, :],
                                                         dec[rows, j, n:n + 1], inc, ALU.mult, ALU.add), done)
            for h in range(GH):
                wait_job(dve, ("scores", h))
                chain(v.tensor_tensor(scT[:, h, :].rearrange("p (j t) -> p j t", t=P),
                                      side_of(("scores", h))[:, :].rearrange("p (j t) -> p j t", t=P),
                                      const("pair_causal").unsqueeze(1).broadcast_to([P, NT, P]), ALU.mult), freed)

            for g in range(4):
                wait_job(dve, ("pool", g))
                chain(v.tensor_scalar(diff[:, g, :], side_of(("pool", g))[:, :], p_scale[:, g:g + 1], None, ALU.mult), freed)

            def gate(c):
                j = c - C_IN2 - 17
                take(c, sg2[:, j // NK, j % NK, :])

            for c in range(C_IN2 + 17, C_IN2 + 21):
                gate(c)
            def head_norm(h):
                refine(side_of(("o_sum", h))[:, :], rs_h[h % 2][:, :], DV, freed=freed)
                t = o_s[h % 2][:, :]
                chain(v.scalar_tensor_tensor(t, t, g_gla[:, h:h + 1], rs_h[h % 2][:, :], ALU.mult, ALU.mult))
                chain(v.tensor_tensor(t, t, rsil[:, h, :], ALU.mult), S("o_normed"))

            for h in range(GH + 1):
                if h >= 2:
                    second("branch2", actA_hi, actA_lo, h - 2, o_s[h % 2][:, :], None)
                if h < GH:
                    wait_job(dve, ("o", h))
                    dve.wait_ge(S("o_squares"), h + 1)
                    chain(v.tensor_copy(o_s[h % 2][:, :], side_of(("o", h))[:, :]), freed)
                    gate(C_IN2 + 21 + h)
                if h:
                    head_norm(h - 1)
            second("branch2", actA_hi, actA_lo, GH - 1, o_s[(GH - 1) % 2][:, :], None)
            for g in range(4):
                second("branch2", actA_hi, actA_lo, 4 + g, diff[:, g, :], None)
            for c in range(C_IN2 + 25, C_IN2 + 33):
                gate(c)
            mix(C_BR2, "out2", sg2, actB_hi, actB_lo, 2 * NK)
            for m in range(NK + 1):
                if m < NK:
                    dve.wait_ge(chunk_done, C_OUT2 + m + 1)
                    chain(v.tensor_tensor(xT[:, m, :], xT[:, m, :], out_bank(C_OUT2 + m)[:, :], ALU.add), chunk_freed)
                    chain(v.tensor_scalar(h2T[:, m, :], xT[:, m, :], g_n2[:, m:m + 1], None, ALU.mult), S("h2_made"))
                if m >= 1:
                    add_squares(m - 1, m - 1, None, "sq4_made", "sum4_added")

            chain(v.memset(tabi[:, :, :], SKIP))
            refine(side_of("sum4")[:, 0:NT], gw[:, 13, :], D, gw[:, 14, :], gw[:, 15, :], freed, S("norm_made"))
            chain(v.tensor_copy(ones_r[:, :], ones[:, :]))
            chain(v.tensor_copy(earlier_r[:, :], const("earlier")))
            wait_job(dve, "route_t")
            chain(v.tensor_tensor(lg[:, :, :], side_of("route_t")[:, 0:NT * (NG + NE)].rearrange("p (t e) -> p t e", t=NT),
                                  gw[:, 13, :].unsqueeze(2).broadcast_to([P, NT, NG + NE]), ALU.mult), freed)
            chain(v.tensor_tensor(lg[:, :, :], lg[:, :, :], brt[:, :].unsqueeze(1).broadcast_to([P, NT, NG + NE]), ALU.add))

            def tile3(n, w):
                return rt[:, n, 0:NT * w].rearrange("p (t w) -> p t w", w=w)

            def spread(t, w):
                return t.unsqueeze(2).broadcast_to([P, NT, w])

            def first_largest(x, w, peak, down, to):
                chain(v.tensor_reduce(gw[:, peak, :], x, AX, ALU.max))
                chain(v.tensor_tensor(to, x, spread(gw[:, peak, :], w), ALU.is_equal))
                chain(v.tensor_tensor(to, to, down.unsqueeze(1).broadcast_to([P, NT, w]), ALU.mult))
                chain(v.tensor_reduce(gw[:, 15, :], to, AX, ALU.max))
                chain(v.tensor_tensor(to, to, spread(gw[:, 15, :], w), ALU.is_equal))

            group = tile3(2, NG)
            first_largest(lg[:, :, 0:NG], NG, 0, const("down4"), group)
            chain(v.tensor_tensor(tile3(0, NG), lg[:, :, 0:NG], spread(gw[:, 0, :], NG), ALU.subtract), S("group_shifted"))
            own = rt[:, 3, :].rearrange("p (t e g) -> p t e g", t=NT, g=NG)
            chain(v.tensor_tensor(own, lg[:, :, NG:].rearrange("p t (g e) -> p t e g", e=EPG),
                                  group.unsqueeze(2).broadcast_to([P, NT, EPG, NG]), ALU.mult))
            logit = tile3(4, EPG)
            chain(v.tensor_reduce(logit, own, AX, ALU.add))
            one, two = tile3(5, EPG), tile3(7, EPG)
            first_largest(logit, EPG, 4, const("down8"), one)
            chain(v.scalar_tensor_tensor(tile3(6, EPG), one, -1.0e38, logit, ALU.mult, ALU.add))
            first_largest(tile3(6, EPG), EPG, 5, const("down8"), two)
            chain(v.tensor_tensor(gw[:, 6, :], gw[:, 5, :], gw[:, 4, :], ALU.subtract), S("expert_shifted"))
            M = [rt[:, 8 + k, :].rearrange("p (t g e) -> p t g e", t=NT, g=NG) for k in range(2)]
            for k, pick in enumerate((one, two)):
                chain(v.tensor_tensor(M[k], group.unsqueeze(3).broadcast_to([P, NT, NG, EPG]),
                                      pick.unsqueeze(2).broadcast_to([P, NT, NG, EPG]), ALU.mult))
            chain(v.tensor_tensor(picks_r[:, :, :].rearrange("p t e -> p (t e)"), rt[:, 8, :], rt[:, 9, :], ALU.add), S("picks_made"))
            dve.wait_ge(S("group_exp"), 1)
            chain(v.tensor_reduce(gw[:, 1, :], tile3(0, NG), AX, ALU.add))
            chain(v.reciprocal(gw[:, 2, :], gw[:, 1, :]))
            dve.wait_ge(S("expert_exp"), 1)
            chain(v.tensor_scalar(gw[:, 7, :], gw[:, 6, :], 1.0, None, ALU.add))
            chain(v.reciprocal(gw[:, 8, :], gw[:, 7, :]))
            chain(v.tensor_tensor(gw[:, 10, :], gw[:, 2, :], gw[:, 8, :], ALU.mult))
            chain(v.tensor_tensor(gw[:, 11, :], gw[:, 10, :], gw[:, 6, :], ALU.mult))
            wait_job(dve, "places")
            pos, q_, t1, sl = (rt[:, n, :] for n in (0, 2, 3, 4))
            cnt, o_e, o_in, o_at = (rt[:, 5, NE * n:NE * (n + 1)] for n in range(4))
            chain(v.tensor_copy(cnt, side_of("places")[:, NT * NE:NT * NE + NE]))
            chain(v.tensor_copy(pos, side_of("places")[:, 0:NT * NE]), freed)

            iota_e = const("iota")[:, 0:NE]

            def blocks_past(to, x, least):
                chain(v.tensor_scalar(to, x, float(ROWS + least), None, ALU.is_ge))
                for n in range(2, L // ROWS + 1):
                    chain(v.scalar_tensor_tensor(to, x, float(n * ROWS + least), to, ALU.is_ge, ALU.add))

            blocks_past(q_, pos, 0)
            blocks_past(o_e, cnt, 1)
            chain(v.tensor_tensor_scan(o_in, ones[:, 0:NE], o_e, 0.0, ALU.mult, ALU.add))
            chain(v.tensor_tensor(o_at, o_in, o_e, ALU.subtract))
            chain(v.tensor_tensor(o_at, o_at, iota_e, ALU.subtract))
            chain(v.tensor_scalar(o_at, o_at, float(NE - 1), None, ALU.add))
            by_e = lambda t: t.rearrange("p (t e) -> p t e", e=NE)
            over_e = lambda t: t.unsqueeze(1).broadcast_to([P, NT, NE])
            chain(v.tensor_tensor(by_e(t1), by_e(q_), over_e(o_at), ALU.add))
            chain(v.scalar_tensor_tensor(t1, q_, 1.0, t1, ALU.min, ALU.mult))
            chain(v.tensor_tensor(by_e(t1), by_e(t1), over_e(iota_e), ALU.add))
            in_blk = rt[:, 10:12, :].rearrange("p a b -> p (a b)")[:, 0:NT * NB].rearrange("p (t b) -> p t b", b=NB)
            chain(v.scalar_tensor_tensor(sl, q_, -float(ROWS), pos, ALU.mult, ALU.add))
            every = lambda x, w: x.unsqueeze(2).broadcast_to([P, NT, w])
            for k in range(2):
                pick = rt[:, 8 + k, :]
                for x, to in ((sl, 3), (t1, 9)):
                    chain(v.tensor_tensor(rt[:, 6, :], x, pick, ALU.mult))
                    chain(v.tensor_reduce(gw[:, to, :], by_e(rt[:, 6, :]), AX, ALU.add))
                if k:
                    dve.wait_ge(S("table_half"), 1)
                chain(v.tensor_tensor(at_row[:, :, :], const("iota").unsqueeze(1).broadcast_to([P, NT, P]),
                                      every(gw[:, 3, :], P), ALU.is_equal))
                chain(v.tensor_tensor(in_blk, const("iota")[:, 0:NB].unsqueeze(1).broadcast_to([P, NT, NB]),
                                      every(gw[:, 9, :], NB), ALU.is_equal))
                chain(v.tensor_tensor(in_block[:, :, :], in_blk, every(const("row_id")[:, NT * k:NT * (k + 1)], NB),
                                      ALU.mult), S("picks_placed"))
            wait_job(dve, "table")
            ids = rt[:, 0, 0:NB]
            chain(v.tensor_copy(ids, side_of("table")[:, 0:NB]), freed)
            chain(v.tensor_scalar(rt[:, 2, 0:NB], ids, 0.0, float(SKIP), ALU.is_equal, ALU.mult))
            chain(v.scalar_tensor_tensor(ids, ids, -1.0, rt[:, 2, 0:NB], ALU.add, ALU.add))
            chain(v.tensor_copy(tabi[:, 0, 0:NB], ids))
            chain(v.tensor_scalar(rt[:, 2, 0:NB], ids, float(L), -float(L), ALU.is_ge, ALU.mult))
            chain(v.tensor_tensor(ids, ids, rt[:, 2, 0:NB], ALU.add))
            chain(v.tensor_copy(tabi[:, 1, 0:NB], ids), S("rows_ready"))
            def gate_up_second(i, u, part, halves):
                for n in halves:
                    dve.wait_ge(S(f"gu_hi{part}"), at(i, u, 0) * 2 + (n + 1))
                    cols = slice((2 * part + n) * D, (2 * part + n + 1) * D)
                    v.tensor_tensor(gu_lo[:, cols], gu_raw[:, u % 2, cols], gu_hi[:, cols].bitcast(F32), ALU.subtract)\
                        .then_inc(S(f"gu_lo{part}"), 1)

            below = rt[0:1, 6, :].rearrange("p (j e) -> p j e", e=NE)
            for part in range(4):
                w = OVER // 4
                chain(v.tensor_tensor(below[:, 0:w, :], o_in[0:1, :].unsqueeze(1).broadcast_to([1, w, NE]),
                                      const("iota", 1)[:, part * w:(part + 1) * w].unsqueeze(2).broadcast_to([1, w, NE]),
                                      ALU.is_le))
                chain(v.tensor_reduce(rt[0:1, 7, part * w:(part + 1) * w], below[:, 0:w, :], AX, ALU.add))
            chain(v.tensor_scalar(rt[0:1, 7, 0:OVER], rt[0:1, 7, 0:OVER], float(NE - 1), None, ALU.min))
            chain(v.tensor_copy(over_n[0:1, 1:1 + OVER], rt[0:1, 7, 0:OVER]))
            chain(v.tensor_copy(over_n[0:1, 0:1], o_in[0:1, NE - 1:NE]), S("over_ready"))
            def x_turned(i, u):
                for n in range(2):
                    dve.wait_ge(S("xe_hi"), at(i, u, 0) * 2 + (n + 1))
                    cols = slice(n * L, (n + 1) * L)
                    v.tensor_tensor(xeT_lo[:, u % 2, cols], side[n][:, :], xeT_hi[:, u % 2, cols].bitcast(F32),
                                    ALU.subtract).then_inc(S("xe_t_made"), 1)

            def hidden(i, u):
                dve.wait_ge(S("silu_made"), at(i, u, 1))
                v.tensor_tensor(hid[:, u % 2, :], hid[:, u % 2, :], bank[u % 2][:, DE:], ALU.mult)\
                    .then_inc(S("hid_made"), 1)

            def hidden_turned(i, u):
                dve.wait_ge(S("hid_turned"), at(i, u, 1))
                wait_from(dve, S("down_done"), i, u, -1)
                v.tensor_copy(hidT[:, u % 2, :], side[2][:, 0:DE]).then_inc(S("hid_t_made"), 1)

            def y_out(i, u):
                dve.wait_ge(S("down_done"), at(i, u, 1))
                if exists(i, u - 2):
                    dve.wait_ge(S(f"scattered{u % 2}"), slot_count(i, u - 2, 16))
                v.tensor_copy(ye[:, u % 2, L:], bank[3][:, :]).then_inc(S("y_by_dve"), 1)

            def expert(i, u):
                first = not exists(i, u - 1)
                if not first:
                    gate_up_second(i, u, 0, (0, 1))
                if exists(i, u - 2):
                    hidden_turned(i, u - 2)
                if not first:
                    hidden(i, u - 1)
                    gate_up_second(i, u, 1, (0,))
                x_turned(i, u)
                if not first:
                    gate_up_second(i, u, 1, (1,))
                if exists(i, u - 2):
                    y_out(i, u - 2)

            def last():
                i, u = LAST
                hidden_turned(i, u - 1)
                hidden(i, u)
                x_turned(i, u + 1)
                y_out(i, u - 1)
                hidden_turned(i, u)
                y_out(i, u)

            def overflow(i, u):
                gate_up_second(i, u, 0, (0, 1))
                gate_up_second(i, u, 1, (0, 1))
                hidden(i, u)
                x_turned(i, u + 1)
                hidden_turned(i, u)
                y_out(i, u)

            for_experts(dve, expert, last, overflow)

            dve.wait_ge(S("gain_in"), 16)
            wait_freed(dve, ("resid", NT - 1, 1))
            for i in range(NT + 1):
                if i < NT:
                    t = x_res[:, i, :]
                    dve.wait_ge(S(f"y2_in{i}"), 16)
                    chain(v.scalar_tensor_tensor(t, y2[:, i, 0:D], gw[:, 10, i:i + 1], t, ALU.mult, ALU.add))
                    chain(v.scalar_tensor_tensor(t, y2[:, i, D:], gw[:, 11, i:i + 1], t, ALU.mult, ALU.add), S("final_sum"))
                if i >= 1:
                    t, one = x_res[:, i - 1, :], slice(i - 1, i)
                    refine(gw[:, 12, one], gw[:, 13, one], D, gw[:, 14, one], gw[:, 15, one])
                    chain(v.scalar_tensor_tensor(t, t, gw[:, 13, one], gfin[:, :], ALU.mult, ALU.mult), S("final_out"))

        @block.tensor
        def _(pe):
            mm = nc.tensor.matmul

            def open_job(name):
                i = jobs.at[name]
                if i >= 4:
                    pe.wait_ge(side_freed[jobs.freer[i - 4]], jobs.freed[i - 4])
                return side[i % 4]

            def close_job(ins):
                ins.then_inc(side_full, 1)

            def chunk(slot, done, hi, lo, ready, counts, two, free):
                pe.wait_ge(lo_made, done)
                if free is not None:
                    pe.wait_ge(chunk_freed, free)
                for k in range(NK):
                    pe.wait_ge(ready, counts[k])
                    b = side[slot] if two and k >= 4 else bank[slot]
                    w_hi, w_lo = (w[:, slot, k * P:(k + 1) * P] for w in (whi, wlo))
                    first, last = k in ((0, 4) if two else (0,)), k in ((3, 7) if two else (7,))
                    mm(b[:, :], w_hi, hi[:, k, :], start=first, stop=False)
                    mm(b[:, :], w_hi, lo[:, k, :], start=False, stop=False)
                    ins = mm(b[:, :], w_lo, hi[:, k, :], start=False, stop=last)
                ins.then_inc(chunk_done, 1)

            def chunks(first, n, hi, lo, ready, counts=tuple(range(1, NK + 1)), two=False):
                if n % RING or first < RING:
                    for c in range(first, first + n):
                        chunk(c % RING, c + 1, hi, lo, ready, counts, two, c - RING + 1 if c >= RING else None)
                    return
                with pe.Fori(0, n // RING) as i:
                    for u in range(RING):
                        chunk((first + u) % RING, RING * i + (first + u + 1), hi, lo, ready, counts, two,
                              RING * i + (first + u - RING + 1))

            def turn(dst, src):
                return nc.tensor.transpose(dst, src, ident[0:src.shape[0], 0:src.shape[0]])

            def total(name, src, sem, count):
                pe.wait_ge(sem, count)
                close_job(mm(open_job(name)[:, :], ones[:, :], src, start=True, stop=True))

            pe.wait_ge(S("x_in"), 16 * (NT + 1))
            pe.wait_ge(S("ones_set"), 1)
            for k in range(NK):
                b = open_job(("x_t", k))
                for i in range(NT):
                    ins = turn(b[:, i * P:(i + 1) * P], x_tok[:, i, k * P:(k + 1) * P])
                close_job(ins)

            inA = (actA_hi, actA_lo, S("ready_in"))
            chunks(C_IN, 1, *inA)
            total("sum0", ssum[:, :], S("sum_added"), NK)
            chunks(1, 4, *inA)
            b = open_job("ik_tok")
            pe.wait_ge(chunk_freed, 1)
            for t in range(NT):
                ins = turn(b[:, t * P:(t + 1) * P], ik_s[:, t * P:(t + 1) * P])
            close_job(ins)
            chunks(5, 8, *inA)
            pe.wait_ge(chunk_freed, 13)
            for n, br in enumerate("ab"):
                b = open_job(("v_tok", br))
                for t in range(NT):
                    ins = turn(b[:, t * P:(t + 1) * P], vT[:, n, t * P:(t + 1) * P])
                close_job(ins)
            b = open_job("ik_t")
            pe.wait_ge(S("ik_roped"), 2)
            for t in range(NT):
                ins = turn(b[:, t * P:(t + 1) * P], ikrope[:, t, :])
            close_job(ins)
            chunks(13, 4, *inA)
            wait_freed(pe, "ik_t")
            pe.wait_ge(S("roped"), 4)
            for qt in range(1, NT):
                for h in range(HEADS):
                    rows = slice(HD * (h % 2), HD * (h % 2 + 1))
                    b = open_job(("index", qt, h))
                    close_job(mm(b[:, 0:(qt + 1) * P], iqT[rows, h // 2, qt * P:(qt + 1) * P],
                                 ikT[rows, 0:(qt + 1) * P], start=True, stop=True))
            chunks(17, 16, *inA)

            pe.wait_ge(S("roped"), len(ROPED))
            wait_freed(pe, ("v_tok", "b"))
            pe.wait_ge(chunk_freed, C_BR)
            for what, n in pe_attention():
                if what in ("logits", "probs_t", "values"):
                    br, qt, k0, nk, h = unit(n)
                    rows = slice(HD * (h % 2), HD * (h % 2 + 1))
                if what == "logits":
                    b = open_job((what, n))
                    close_job(mm(b[:, 0:nk * P], qT[br][rows, h // 2, qt * P:(qt + 1) * P],
                                 kT[br][rows, h // REP, k0 * P:(k0 + nk) * P], start=True, stop=True))
                elif what == "probs_t":
                    b = open_job((what, n))
                    pe.wait_ge(S("probs_made"), n + 1)
                    for j in range(nk):
                        ins = turn(b[:, j * P:(j + 1) * P], pbuf[:, n % 3, j * P:(j + 1) * P])
                    close_job(ins)
                elif what == "values":
                    g = n // HEADS
                    wait_freed(pe, ("probs_t", n))
                    if g >= RING and h == 0:
                        pe.wait_ge(S("outs_made"), g - RING + 1)
                    for j in range(nk):
                        ins = mm(bank[g % RING][:, h * HD:(h + 1) * HD], pT[:, n % 2, j * P:(j + 1) * P],
                                 v_tok[br][:, k0 + j, HD * (h // REP):HD * (h // REP + 1)],
                                 start=j == 0, stop=j == nk - 1)
                    ins.then_inc(S("values_done"), 1)
                else:
                    b = open_job((what, n))
                    pe.wait_ge(S("outs_made"), n + 1)
                    for f in range(4):
                        ins = turn(b[:, f * P:(f + 1) * P], o_n[:, n % 2, f * P:(f + 1) * P])
                    close_job(ins)

            wait_freed(pe, ("out_t", 2 * NT - 1))
            wait_freed(pe, ("probs_t", UNITS - 1))
            chunks(C_BR, NK, actB_hi, actB_lo, side_freed["dve"],
                   [jobs.freed[jobs.at[("out_t", 2 * NT - 1)]]] * NK, two=True)
            chunks(C_OUT, NK, actA_hi, actA_lo, S("ready_out"))
            for q in range(QUARTERS):
                chunks(C_MLP + 2 * NK * q, NK, actB_hi, actB_lo, S("ready_mlp"))
                if q == 0:
                    pe.wait_ge(chunk_freed, C_OUT)
                    total("sum1", ssum[:, :], S("sum_added"), 2 * NK)
                chunks(C_MLP + 2 * NK * q + NK, NK, actA_hi, actA_lo, S(f"ready_u{q}"))

            inB = (actB_hi, actB_lo, S("ready_in2"))
            chunks(C_IN2, 1, *inB)
            total("sum2", ssum[:, :], S("sum_added"), 4 * NK)
            total("sum3", ssum2[:, :], S("sum_added"), 4 * NK)
            chunks(C_IN2 + 1, 4, *inB)
            pe.wait_ge(S("small2_in"), 32)
            pe.wait_ge(S("alow_made"), 1)
            for j in range(2):
                b = open_job(("z", j))
                close_job(mm(b[:, :], wal[:, j * P:(j + 1) * P], alow[:, :], start=True, stop=True))
            chunks(C_IN2 + 5, 4, *inB)
            pe.wait_ge(chunk_freed, C_IN2 + 9)
            for h in range(GH):
                b = open_job(("gv_tok", h))
                for t in range(NT):
                    ins = turn(b[:, t * P:(t + 1) * P], gvT[:, h, t * P:(t + 1) * P])
                close_job(ins)
            chunks(C_IN2 + 9, 4, *inB)
            chunks(C_IN2 + 13, 4, *inB)
            pe.wait_ge(S("kend_made"), 2)
            for j in range(2):
                b = open_job(("kend_tok", j))
                for t in range(NT):
                    ins = turn(b[:, t * P:(t + 1) * P], kend[:, j, t * P:(t + 1) * P])
                close_job(ins)
            wait_freed(pe, ("kend_tok", 1))
            for n in range(NCH - 1):
                b = open_job(("inc", n))
                rows = slice(CHUNK * (n % 2), CHUNK * (n % 2 + 1))
                for j in range(2):
                    ins = mm(b[:, 256 * j:256 * (j + 1)], kend_tok[rows, n // 2, j * P:(j + 1) * P],
                             gv_tok[rows, n // 2, 256 * j:256 * (j + 1)], start=True, stop=True)
                close_job(ins)
            for h in range(GH):
                b = open_job(("scores", h))
                rows = slice(HD * (h % 2), HD * (h % 2 + 1))
                for t in range(NT):
                    cols = slice(t * P, (t + 1) * P)
                    ins = mm(b[:, cols], kdec[rows, h // 2, cols], qdec[rows, h // 2, cols], start=True, stop=True)
                close_job(ins)
            pe.wait_ge(S("diff_made"), 4)
            for g in range(4):
                close_job(mm(open_job(("pool", g))[:, :], pw[:, g, :], diff[:, g, :], start=True, stop=True))
            chunks(C_IN2 + 17, 4, *inB)
            wait_freed(pe, ("scores", GH - 1))
            for h in range(GH):
                b = open_job(("o", h))
                rows = slice(HD * (h % 2), HD * (h % 2 + 1))
                for t in range(NT):
                    cols = slice(t * P, (t + 1) * P)
                    mm(b[:, cols], gv_tok[:, t, h * DV:(h + 1) * DV], scT[:, h, cols], start=True, stop=False)
                    for n in range(2 * t, 2 * t + 2):
                        if n:
                            at_ = slice(n * CHUNK, (n + 1) * CHUNK)
                            ins = mm(b[:, at_], gst[rows, h // 2, n, :], qdec[rows, h // 2, at_], start=False, stop=n % 2 == 1)
                close_job(ins)
                chunks(C_IN2 + 21 + h, 1, *inB)
                total(("o_sum", h), sq[:, 0, :], S("o_squares"), h + 1)
            chunks(C_IN2 + 25, 8, *inB)
            wait_freed(pe, ("o_sum", GH - 1))
            chunks(C_BR2, NK, actA_hi, actA_lo, S("ready_branch2"), two=True)
            inR = (actB_hi, actB_lo, S("ready_out2"))
            chunks(C_OUT2, 4, *inR)
            pe.wait_ge(S("route_in"), 16 * (NG + 3))
            b = open_job("route")
            for k in range(NK):
                if k == 3:
                    chunks(C_OUT2 + 4, 4, *inR)
                pe.wait_ge(S("h2_made"), k + 1)
                ins = mm(b[0:NG + NE, :], wr[:, k, :], h2T[:, k, :], start=k == 0, stop=k == NK - 1)
            close_job(ins)

            b = open_job("sum4")
            pe.wait_ge(S("sum4_added"), NK)
            for i in range(NT):
                ins = mm(b[:, i:i + 1], ssum[:, i * P:(i + 1) * P], ones[:, 0:1], start=True, stop=True)
            close_job(ins)
            b = open_job("route_t")
            wait_freed(pe, "route")
            for i in range(NT):
                ins = turn(b[:, i * (NG + NE):(i + 1) * (NG + NE)], lgT[0:NG + NE, i * P:(i + 1) * P])
            close_job(ins)
            for i in range(NT):
                for n in range(2):
                    b = open_job(("rows", i, n))
                    for k in range(4):
                        ins = turn(b[:, k * P:(k + 1) * P], h2T[:, 4 * n + k, i * P:(i + 1) * P])
                    close_job(ins)
            b = open_job("places")
            pe.wait_ge(S("picks_made"), 1)
            for i in range(NT):
                for j in range(i + 1):
                    mm(b[:, i * NE:(i + 1) * NE], earlier_r[:, :] if j == i else ones_r[:, :], picks_r[:, j, :],
                       start=j == 0, stop=j == i)
            for j in range(NT):
                ins = mm(b[:, NT * NE:NT * NE + NE], ones_r[:, :], picks_r[:, j, :], start=j == 0, stop=j == NT - 1)
            close_job(ins)
            b = open_job("table")
            for k in range(2):
                pe.wait_ge(S("picks_placed"), k + 1)
                for i in range(NT):
                    ins = mm(b[:, 0:NB], at_row[:, i, :], in_block[:, i, :], start=(k, i) == (0, 0), stop=(k, i) == (1, NT - 1))
                if k == 0:
                    ins.then_inc(S("table_half"), 1)
            close_job(ins)
            for i in range(NT):
                for n in range(2):
                    b = open_job(("resid", i, n))
                    for k in range(4):
                        ins = turn(b[:, k * P:(k + 1) * P], xT[:, 4 * n + k, i * P:(i + 1) * P])
                    close_job(ins)
            wait_freed(pe, "places")
            wait_freed(pe, ("resid", NT - 1, 1))

            def turn_rows(i, u):
                pe.wait_ge(S(f"gathered{u % RING}"), 16 * (u // RING + 1) if i is None else
                           16 * i + 16 * (u // RING + 1))
                wait_from(pe, S("xe_t_made"), i, u, 0, 2)
                for k in range(NK):
                    ins = turn(side[k // 4][:, (k % 4) * P:(k % 4 + 1) * P], xe[:, u % RING, k * P:(k + 1) * P])
                ins.then_inc(S("xe_used"), 1)

            def gate_up(i, u):
                j = u % 2
                pe.wait_ge(S("xe_t_made"), at(i, u, 1) * 2)
                wait_from(pe, S("hid_made"), i, u, -1)
                for part in range(2):
                    pe.wait_ge(S(f"gu_lo{part}"), at(i, u, 1) * 2)
                    for k in range(4 * part, 4 * part + 4):
                        x, w = slice(k * P, (k + 1) * P), slice(k * 2 * DE, (k + 1) * 2 * DE)
                        mm(bank[j][:, :], xeT_hi[:, j, x], gu_hi[:, w], start=k == 0, stop=False)
                        mm(bank[j][:, :], xeT_hi[:, j, x], gu_lo[:, w], start=False, stop=False)
                        ins = mm(bank[j][:, :], xeT_lo[:, j, x], gu_hi[:, w], start=False, stop=k == NK - 1)
                    ins.then_inc(S(("gate_up_half_done", "gate_up_done")[part]), 1)

            def turn_hidden(i, u):
                pe.wait_ge(S("hid_made"), at(i, u, 1))
                wait_from(pe, S("hid_t_made"), i, u, 0)
                for k in range(2):
                    ins = turn(side[2][:, k * P:(k + 1) * P], hid[:, u % 2, k * P:(k + 1) * P])
                ins.then_inc(S("hid_turned"), 1)

            def down(i, u):
                pe.wait_ge(S("hid_t_made"), at(i, u, 1))
                pe.wait_ge(S(f"down_in{u % RING}"), 16 * (u // RING + 1) if i is None else
                           16 * i + 16 * (u // RING + 1))
                wait_from(pe, S("y_by_act"), i, u, 0)
                wait_from(pe, S("y_by_dve"), i, u, 0)
                for n in range(2):
                    for k in range(2):
                        at_ = k * D + n * L
                        ins = mm(bank[2 + n][:, :], hidT[:, u % 2, k * P:(k + 1) * P], d_raw[:, u % RING, at_:at_ + L],
                                 start=k == 0, stop=k == 1)
                ins.then_inc(S("down_done"), 1)

            def expert(i, u):
                gate_up(i, u)
                if exists(i, u - 1):
                    turn_hidden(i, u - 1)
                turn_rows(i, u + 1)
                if exists(i, u - 1):
                    down(i, u - 1)

            def last():
                turn_hidden(*LAST)
                down(*LAST)

            def overflow(i, u):
                gate_up(i, u)
                turn_rows(i, u + 1)
                turn_hidden(i, u)
                down(i, u)

            turn_rows(None, 0)
            for_experts(pe, expert, last, overflow)


def kernel(**inputs):
    import numpy as _np
    import concourse.bacc as _bacc
    from concourse import mybir as _mybir
    from concourse.bass_utils import run_bass_kernel_spmd as _run

    f = _np.float32
    t, u = _np.arange(P)[:, None], _np.arange(P)[None, :]
    inv = (f(1.0) / (f(10000.0) ** (_np.arange(0, HD, 2, dtype=f) / f(HD)))).astype(f)
    angle = (_np.arange(L, dtype=f)[:, None] * inv[None, :]).astype(f)
    cos, sin = _np.cos(angle), _np.sin(angle)
    count = _np.concatenate([1.0 / _np.minimum(_np.arange(16) + 1.0, w) for w in WINDOWS])
    rows = lambda a: _np.broadcast_to(a, (P, a.shape[-1]))
    parts = {
        "ident": t == u, "causal": _np.where(u <= t, 0.0, NEG), "before": _np.where(u > t, 0.0, NEG),
        "earlier": t < u, "pair_causal": (t <= u) & (t // CHUNK == u // CHUNK),
        "cos": _np.tile(cos.T, (4, 1)), "sin": _np.tile(sin.T, (4, 1)),
        "cos_tok": cos.reshape(NT, P, 32).transpose(1, 0, 2).reshape(P, -1),
        "sin_tok": sin.reshape(NT, P, 32).transpose(1, 0, 2).reshape(P, -1),
        "inv_count": rows(count[None]), "iota": rows(_np.arange(P)[None]),
        "down4": rows(_np.arange(NG, 0, -1)[None]), "down8": rows(_np.arange(EPG, 0, -1)[None]),
        "row_id": _np.arange(1, 2 * L + 1).reshape(2 * NT, P).T,
    }
    consts = _np.concatenate([parts[n].astype(f) for n in CONST_COLS], axis=1)

    nc = _bacc.Bacc("TRN2", target_bir_lowering=False, num_devices=1)
    arrays, args = {}, {}
    for name, a in (*inputs.items(), ("consts", consts)):
        a = _np.ascontiguousarray(a)
        arrays[f"in_{name}"] = a
        args[name] = nc.dram_tensor(f"in_{name}", a.shape, _mybir.dt.from_np(a.dtype), kind="ExternalInput").ap()
    out = nc.dram_tensor("out", (L, D), _mybir.dt.float32, kind="ExternalOutput").ap()
    gated_blocks(nc, args, out)
    r = _run(nc, [arrays], core_ids=[0])
    return r.results[0]["out"].reshape(1, L, D)
```
